# Optimizing a Trainium2 kernel written in Bass

```python
import math
import jax, jax.numpy as jnp
from jax import lax
import numpy as np

D_MODEL = 1024
BATCH = 1
SEQ = 256
DEPTH = 1
DEC_BATCH = 1
DEC_SEQ = 1024
PAST_LEN = 128

N_META = 16
RWKV_HEADS = 8
RWKV_HEAD_DIM = 64
RWKV_WIDTH = RWKV_HEADS * RWKV_HEAD_DIM
DIFF_HEADS = 4
DIFF_QK_DIM = 64
DIFF_V_DIM = 2 * DIFF_QK_DIM
DIFF_WIDTH = DIFF_HEADS * DIFF_V_DIM
MIX_WIDTH = RWKV_WIDTH + DIFF_WIDTH
DIFF_QK_WIDTH = DIFF_HEADS * 2 * DIFF_QK_DIM
IN_WIDTH = 3 * RWKV_WIDTH + 2 * DIFF_QK_WIDTH + DIFF_WIDTH
DECAY_LORA = 64
AAA_LORA = 64
GATE_LORA = 160
CONV_WIDTH = 3
ROPE_THETA = 500000.0
ROPE_DIMS = DIFF_QK_DIM // 4
D_FF = -(-8 * D_MODEL // (3 * 256)) * 256
Q_BLOCK = 128
NORM_EPS = 1e-6
GN_EPS = 64e-5
DECAY_SCALE = math.exp(-0.5)

kernel_name = "hymba_rwkv7_diffattn_encoder"

def rms_norm(x, g):
    xf = x.astype(jnp.float32)
    y = xf * lax.rsqrt(jnp.mean(xf * xf, axis=-1, keepdims=True) + NORM_EPS)
    return (y * g.astype(jnp.float32)).astype(x.dtype)

def shift_prev(x):
    return jnp.pad(x, ((0, 0), (1, 0), (0, 0)))[:, :-1]

def shift_next(x):
    return jnp.pad(x, ((0, 0), (0, 1), (0, 0)))[:, 1:]

def centred_conv(x, w):
    return w[0] * shift_prev(x) + w[1] * x + w[2] * shift_next(x)

def wkv7_scan(r, w, k, v, a_, b_, reverse):
    B, T, H, N = r.shape

    def step(S, inp):
        rt, wt, kt, vt, at, bt = inp
        sa = jnp.einsum('bhij,bhj->bhi', S, at)
        S = S * wt[:, :, None, :] + sa[..., None] * bt[:, :, None, :] + vt[..., None] * kt[:, :, None, :]
        return S, jnp.einsum('bhij,bhj->bhi', S, rt)

    xs = tuple(jnp.moveaxis(t, 1, 0) for t in (r, w, k, v, a_, b_))
    S0 = jnp.zeros((B, H, N, N), jnp.float32)
    _, y = lax.scan(step, S0, xs, reverse=reverse)
    return jnp.moveaxis(y, 0, 1)

def rwkv7_mixer(h, r, k, v, p):
    B, T, _ = h.shape
    H, N = RWKV_HEADS, RWKV_HEAD_DIM
    hf = h.astype(jnp.float32)
    r, k, v = (t.astype(jnp.float32) for t in (r, k, v))
    delta = 0.5 * (shift_prev(hf) + shift_next(hf)) - hf
    xg = hf + delta * p['mix_g']
    g = jax.nn.sigmoid(xg @ p['gate_g1']) @ p['gate_g2']
    kk = (k * p['k_k']).reshape(B, T, H, N)
    kk = kk / jnp.maximum(jnp.linalg.norm(kk, axis=-1, keepdims=True), 1e-12)
    rh = r.reshape(B, T, H, N)
    vh = v.reshape(B, T, H, N)
    y_sum = jnp.zeros((B, T, H, N), jnp.float32)
    bonus = jnp.zeros((B, T, H, N), jnp.float32)
    for d in range(2):
        xw = hf + delta * p['mix_w'][d]
        xa = hf + delta * p['mix_a'][d]
        w = jnp.exp(-DECAY_SCALE * jax.nn.sigmoid(p['decay_w0'][d] + jnp.tanh(xw @ p['decay_w1'][d]) @ p['decay_w2'][d]))
        a = jax.nn.sigmoid(p['aaa_a0'][d] + (xa @ p['aaa_a1'][d]) @ p['aaa_a2'][d])
        kd = k * (1.0 + (a - 1.0) * p['k_a'])
        kdh = kd.reshape(B, T, H, N)
        ah = a.reshape(B, T, H, N)
        y_sum = y_sum + wkv7_scan(rh, w.reshape(B, T, H, N), kdh, vh, -kk, kk * ah, reverse=(d == 1))
        bonus = bonus + jnp.sum(rh * kdh * p['r_k'], axis=-1, keepdims=True) * vh
    mu = jnp.mean(y_sum, axis=-1, keepdims=True)
    var = jnp.mean(jnp.square(y_sum - mu), axis=-1, keepdims=True)
    yn = (y_sum - mu) * lax.rsqrt(var + GN_EPS)
    yn = yn * p['lnx_g'].reshape(H, N) + p['lnx_b'].reshape(H, N)
    out = (yn + bonus).reshape(B, T, RWKV_WIDTH) * g
    return out.astype(h.dtype)

def partial_rope(x):
    T = x.shape[1]
    half = ROPE_DIMS // 2
    freqs = ROPE_THETA ** (-jnp.arange(0, ROPE_DIMS, 2, dtype=jnp.float32) / ROPE_DIMS)
    ang = jnp.arange(T, dtype=jnp.float32)[:, None] * freqs[None, :]
    cos = jnp.cos(ang)[None, :, None, None, :]
    sin = jnp.sin(ang)[None, :, None, None, :]
    xf = x.astype(jnp.float32)
    x1, x2, rest = xf[..., :half], xf[..., half:ROPE_DIMS], xf[..., ROPE_DIMS:]
    out = jnp.concatenate([x1 * cos - x2 * sin, x2 * cos + x1 * sin, rest], axis=-1)
    return out.astype(x.dtype)

def diff_attention(q, k, v, p, lambda_init):
    B, T, _ = q.shape
    H, d = DIFF_HEADS, DIFF_QK_DIM
    q = q.reshape(B, T, H, 2, d)
    k = k.reshape(B, T, H, 2, d)
    v = v.reshape(B, T, H, DIFF_V_DIM).astype(jnp.float32)
    q = partial_rope(rms_norm(q, p['q_norm_g'])).astype(jnp.float32) * (d ** -0.5)
    k = partial_rope(rms_norm(k, p['k_norm_g'])).astype(jnp.float32)
    lam_v = p['diff_lambdas'].astype(jnp.float32)
    lam = jnp.exp(jnp.sum(lam_v[0] * lam_v[1])) - jnp.exp(jnp.sum(lam_v[2] * lam_v[3])) + lambda_init

    def attend(qb):
        s = jnp.einsum('bqhcd,bkhcd->bhcqk', qb, k)
        pr = jax.nn.softmax(s, axis=-1)
        amap = pr[:, :, 0] - lam * pr[:, :, 1]
        return jnp.einsum('bhqk,bkhe->bqhe', amap, v)

    meta_out = attend(q[:, :N_META])
    n_blk = (T - N_META) // Q_BLOCK
    qb = q[:, N_META:].reshape(B, n_blk, Q_BLOCK, H, 2, d).transpose(1, 0, 2, 3, 4, 5)
    ob = lax.map(attend, qb)
    real_out = ob.transpose(1, 0, 2, 3, 4).reshape(B, T - N_META, H, DIFF_V_DIM)
    o = jnp.concatenate([meta_out, real_out], axis=1)
    o = rms_norm(o, p['subln_g']) * (1.0 - lambda_init)
    return o.reshape(B, T, DIFF_WIDTH).astype(q.dtype)

def encoder_layer(x, p, lambda_init):
    n = rms_norm(x, p['ln1_g'])
    proj = n @ p['w_in']
    c0 = 3 * RWKV_WIDTH
    rkv = centred_conv(proj[..., :c0], p['conv_rkv'])
    r, k, v = rkv[..., :RWKV_WIDTH], rkv[..., RWKV_WIDTH:2 * RWKV_WIDTH], rkv[..., 2 * RWKV_WIDTH:]
    qd = proj[..., c0:c0 + DIFF_QK_WIDTH]
    kd = proj[..., c0 + DIFF_QK_WIDTH:c0 + 2 * DIFF_QK_WIDTH]
    vd = proj[..., c0 + 2 * DIFF_QK_WIDTH:]
    ya = rwkv7_mixer(n, r, k, v, p)
    yb = diff_attention(qd, kd, vd, p, lambda_init)
    x = x + jnp.concatenate([ya, yb], axis=-1) @ p['w_out']
    n2 = rms_norm(x, p['ln2_g'])
    x = x + (jax.nn.silu(n2 @ p['w_gate']) * (n2 @ p['w_up'])) @ p['w_down']
    return x

def trunk(x, meta_tokens, p):
    B = x.shape[0]
    meta = jnp.broadcast_to(meta_tokens.astype(x.dtype)[None], (B, N_META, D_MODEL))
    h = jnp.concatenate([meta, x], axis=1)
    for l in range(DEPTH):
        pl = {name: arr[l] for name, arr in p.items()}
        lambda_init = 0.8 - 0.6 * math.exp(-0.3 * l)
        h = encoder_layer(h, pl, lambda_init)
    return h[:, N_META:]

def setup_inputs(seed: int = 0) -> dict:
    key = jax.random.key(seed)
    ks = iter(jax.random.split(key, 40))

    def nrm(shape, scale):
        return jax.random.normal(next(ks), shape, jnp.float32) * scale

    L = DEPTH
    conv_c = 1.0 + nrm((L, 1, 3 * RWKV_WIDTH), 0.05)
    conv_s = nrm((L, 2, 3 * RWKV_WIDTH), 0.1)
    conv_rkv = jnp.concatenate([conv_s[:, :1], conv_c, conv_s[:, 1:]], axis=1)
    return {
        'x_prompt': nrm((BATCH, SEQ, D_MODEL), 1.0),
        'x_sample': nrm((DEC_BATCH, DEC_SEQ, D_MODEL), 1.0),
        'meta_tokens': nrm((N_META, D_MODEL), 1.0),
        'ln1_g': 1.0 + nrm((L, D_MODEL), 0.05),
        'w_in': nrm((L, D_MODEL, IN_WIDTH), D_MODEL ** -0.5),
        'conv_rkv': conv_rkv,
        'mix_w': jax.random.uniform(next(ks), (L, 2, D_MODEL), jnp.float32),
        'mix_a': jax.random.uniform(next(ks), (L, 2, D_MODEL), jnp.float32),
        'mix_g': jax.random.uniform(next(ks), (L, D_MODEL), jnp.float32),
        'decay_w0': -1.0 + nrm((L, 2, RWKV_WIDTH), 0.5),
        'decay_w1': nrm((L, 2, D_MODEL, DECAY_LORA), D_MODEL ** -0.5),
        'decay_w2': nrm((L, 2, DECAY_LORA, RWKV_WIDTH), 0.1 * DECAY_LORA ** -0.5),
        'aaa_a0': nrm((L, 2, RWKV_WIDTH), 0.1),
        'aaa_a1': nrm((L, 2, D_MODEL, AAA_LORA), D_MODEL ** -0.5),
        'aaa_a2': nrm((L, 2, AAA_LORA, RWKV_WIDTH), 0.1 * AAA_LORA ** -0.5),
        'gate_g1': nrm((L, D_MODEL, GATE_LORA), D_MODEL ** -0.5),
        'gate_g2': nrm((L, GATE_LORA, RWKV_WIDTH), GATE_LORA ** -0.5),
        'k_k': 0.85 + nrm((L, RWKV_WIDTH), 0.05),
        'k_a': 1.0 + nrm((L, RWKV_WIDTH), 0.05),
        'r_k': nrm((L, RWKV_HEADS, RWKV_HEAD_DIM), 0.1),
        'lnx_g': 1.0 + nrm((L, RWKV_WIDTH), 0.05),
        'lnx_b': nrm((L, RWKV_WIDTH), 0.01),
        'q_norm_g': 1.0 + nrm((L, DIFF_QK_DIM), 0.05),
        'k_norm_g': 1.0 + nrm((L, DIFF_QK_DIM), 0.05),
        'diff_lambdas': nrm((L, 4, DIFF_QK_DIM), 0.1),
        'subln_g': 1.0 + nrm((L, DIFF_V_DIM), 0.05),
        'w_out': nrm((L, MIX_WIDTH, D_MODEL), MIX_WIDTH ** -0.5),
        'ln2_g': 1.0 + nrm((L, D_MODEL), 0.05),
        'w_gate': nrm((L, D_MODEL, D_FF), D_MODEL ** -0.5),
        'w_up': nrm((L, D_MODEL, D_FF), D_MODEL ** -0.5),
        'w_down': nrm((L, D_FF, D_MODEL), D_FF ** -0.5),
    }

def reference(x_prompt, x_sample, meta_tokens, ln1_g, w_in, conv_rkv, mix_w, mix_a, mix_g,
              decay_w0, decay_w1, decay_w2, aaa_a0, aaa_a1, aaa_a2, gate_g1, gate_g2,
              k_k, k_a, r_k, lnx_g, lnx_b, q_norm_g, k_norm_g, diff_lambdas, subln_g,
              w_out, ln2_g, w_gate, w_up, w_down):
    p = {
        'ln1_g': ln1_g, 'w_in': w_in, 'conv_rkv': conv_rkv,
        'mix_w': mix_w, 'mix_a': mix_a, 'mix_g': mix_g,
        'decay_w0': decay_w0, 'decay_w1': decay_w1, 'decay_w2': decay_w2,
        'aaa_a0': aaa_a0, 'aaa_a1': aaa_a1, 'aaa_a2': aaa_a2,
        'gate_g1': gate_g1, 'gate_g2': gate_g2,
        'k_k': k_k, 'k_a': k_a, 'r_k': r_k, 'lnx_g': lnx_g, 'lnx_b': lnx_b,
        'q_norm_g': q_norm_g, 'k_norm_g': k_norm_g, 'diff_lambdas': diff_lambdas,
        'subln_g': subln_g, 'w_out': w_out, 'ln2_g': ln2_g,
        'w_gate': w_gate, 'w_up': w_up, 'w_down': w_down,
    }
    y_prompt = trunk(x_prompt, meta_tokens, p)
    y_sample = trunk(x_sample, meta_tokens, p)
    return (y_prompt, y_sample)


_drawn_inputs = setup_inputs


def setup_inputs(seed=0):
    import zlib

    import numpy as np

    out = dict(_drawn_inputs(seed))
    spreads = {}
    factors = {'mix_w': 8.0,
     'mix_a': 8.0,
     'decay_w1': 8.0,
     'decay_w2': 8.0,
     'aaa_a0': 2.779,
     'aaa_a1': 4.296,
     'aaa_a2': 4.308,
     'k_k': 200.0,
     'k_a': 2.764,
     'lnx_g': 3.447,
     'lnx_b': 26.434,
     'q_norm_g': 3.619,
     'k_norm_g': 3.197,
     'subln_g': 3.744,
     'ln2_g': 3.591}
    for name, (base, spread) in spreads.items():
        noise = np.random.default_rng([zlib.crc32(name.encode()), seed]).standard_normal(out[name].shape)
        drawn = base * np.exp(spread * noise) if base else spread * noise
        out[name] = __import__('jax').numpy.asarray(drawn.astype(out[name].dtype))
    for name, factor in factors.items():
        out[name] = (out[name] * factor).astype(out[name].dtype)
    return out
```

```python
import math
from contextlib import ExitStack

import numpy as np

import concourse.bass as bass
from concourse import mybir
from concourse.alu_op_type import AluOpType as ALU

F32 = mybir.dt.float32
ACT = mybir.ActivationFunctionType
AX_X = mybir.AxisListType.X
ds = bass.ds

P = 128
D = 1024
META = 16
LEN_A, LEN_B = META + 256, META + 1024
TOK = LEN_A + LEN_B
KT = D // P
NCH = 4
CW = TOK // NCH
CH = 64
CH_A, CH_B = -(-LEN_A // CH), -(-LEN_B // CH)
CHUNKS = CH_A + CH_B
PAD_B = CH_A * CH
PTOK = CHUNKS * CH
PW = PTOK // NCH
TT = -(-TOK // P)
RW = 512
FT = RW // P
HEADS = 4
HD = 64
FF = 2816
FFT = FF // P
GL = 160
DECAY = math.exp(-0.5)
LAMBDA_INIT = 0.8 - 0.6 * math.exp(-0.3 * 0)
LEVELS = 5
SEQS = ((0, LEN_A, 0), (LEN_A, LEN_B, PAD_B))

PCOLS = {}
_at = 0
for _name, _n in (("ln1_g", 8), ("ln2_g", 8), ("conv", 36), ("mix_w", 16), ("mix_a", 16), ("mix_g", 8),
                  ("decay_w0", 8), ("aaa_a0", 8), ("k_k", 4), ("k_a", 4), ("r_k", 4), ("lnx_g", 4),
                  ("lnx_b", 4), ("q_norm_g", 1), ("k_norm_g", 1), ("subln_g", 1)):
    PCOLS[_name] = _at
    _at += _n
NPAR = _at


def shape_constants():
    row = np.arange(P)
    h, s = row // CH, row % CH
    t = np.arange(CH)
    eye = np.eye(P, dtype=np.float32)
    block = (row[:, None] // HD == row[None, :] // HD).astype(np.float32)
    out = {"ident": eye, "ident2": (s[:, None] == t[None, :]).astype(np.float32), "heads": block,
           "ones": np.ones((P, P), np.float32)}
    own = (h[:, None, None] == np.arange(2)[None, :, None])
    bd = lambda m: (own & m[:, None, :]).reshape(P, P).astype(np.float32)
    out["own"] = bd(np.ones((P, CH), bool))
    for d in range(2):
        before = s[:, None] < t[None, :] if d == 0 else s[:, None] > t[None, :]
        after = s[:, None] > t[None, :] if d == 0 else s[:, None] < t[None, :]
        same = s[:, None] == t[None, :]
        out[f"incl{d}"] = (before | same).astype(np.float32)
        out[f"strict_bd{d}"] = bd(before)
        out[f"after_bd{d}"] = bd(after)
        lev = lambda z: (s[:, None] // (2 * z) == t[None, :] // (2 * z)) & (s[:, None] // z != t[None, :] // z)
        out[f"pair{d}"] = (lev(1) & before).astype(np.float32)
        out[f"pairT_bd{d}"] = bd((lev(1) & after) | same)
        for n in range(LEVELS):
            out[f"lev{n}_{d}"] = ((lev(2 << n) & before) | same).astype(np.float32)
            out[f"lev{n}_bd{d}"] = bd((lev(2 << n) & before) | same)
    swap = np.zeros((P, P), np.float32)
    for c in range(2):
        for i in range(8):
            swap[c * HD + 8 + i, c * HD + i] = -1.0
            swap[c * HD + i, c * HD + 8 + i] = 1.0
    out["swap"] = swap
    freqs = (np.float32(500000.0) ** (-np.arange(0, 16, 2, dtype=np.float32) / np.float32(16))).astype(np.float32)
    pos = np.concatenate([np.arange(LEN_A), np.arange(LEN_B)]).astype(np.float32)
    ang = (pos[None, :] * freqs[:, None]).astype(np.float32)
    cos, sin = np.ones((P, TOK), np.float32), np.zeros((P, TOK), np.float32)
    for c in range(2):
        for k in range(2):
            r = c * HD + 8 * k
            cos[r:r + 8], sin[r:r + 8] = np.cos(ang), np.sin(ang)
    first = np.ones((P, CHUNKS, CH), np.float32)
    first[:, :, 0] = 0
    keep = np.ones((P, 2, CHUNKS), np.float32)
    keep[:, 0, [CH_A - 1, CHUNKS - 1]] = 0
    keep[:, 1, [0, CH_A]] = 0
    wide = {"cos": cos, "sin": sin, "first": first.reshape(P, PTOK), "keep": keep.reshape(P, 2 * CHUNKS)}
    return out, wide


SMALL, WIDE = shape_constants()
SCOLS, _at = {}, 0
for _name, _a in SMALL.items():
    SCOLS[_name] = (_at, _a.shape[1])
    _at += _a.shape[1]
NSMALL = _at
SMALL_ARRAY = np.concatenate(list(SMALL.values()), axis=1)
SCRATCH_KIND = "Internal"
PRIMED = 1


class Ctx(ExitStack):

    def __init__(self, nc, stage):
        super().__init__()
        self.nc, self.stage, self.sems = nc, stage, []

    def sb(self, name, shape):
        return self.enter_context(self.nc.sbuf_tensor(f"{self.stage}_{name}", list(shape), F32))

    def ps(self, name, shape=(P, 512)):
        return self.enter_context(self.nc.psum_tensor(f"{self.stage}_{name}", list(shape), F32))

    def sem(self, name):
        self.sems.append(self.enter_context(self.nc.semaphore(f"{self.stage}_{name}")))
        return self.sems[-1]

    def prime(self, eng):
        for sem in self.sems:
            eng.sem_inc(sem, PRIMED)


class Chain:

    def __init__(self, eng, sem, base=0):
        self.eng, self.sem, self.base, self.n = eng, sem, base, 0

    def __call__(self, ins):
        self.n += 1
        ins.then_inc(self.sem, 1)
        self.eng.wait_ge(self.sem, PRIMED + self.base + self.n)


def wide(ap, axis, shape):
    return ap.unsqueeze(axis).to_broadcast(list(shape))


def cut(t, lo, n):
    return t[:, lo:lo + n]


def norm_in(nc, g):
    with Ctx(nc, "n1") as c:
        x = c.sb("x", (P, TT, D))
        sq = c.sb("sq", (P, D))
        xn = c.sb("xn", (P, D))
        ss = c.sb("ss", (P, TT))
        rms = c.sb("rms", (P, TT))
        rstd = c.sb("rstd", (P, TT))
        small = c.sb("ident", (P, P))
        tp = [c.ps("tpa"), c.ps("tpb")]
        loaded, squared, rooted, chain = c.sem("loaded"), c.sem("squared"), c.sem("rooted"), c.sem("chain")
        scaled, turned, taken = c.sem("scaled"), c.sem("turned"), c.sem("taken")
        with nc.Block() as block:
            @block.sync
            def _(sp):
                c.prime(sp)
                sp.dma_start(x[:, :, :], g.x.rearrange("(t p) d -> p t d", p=P)).then_inc(loaded, 16)
                sp.dma_start(small[:, :], g.small[:, 0:P]).then_inc(loaded, 16)
                sp.dma_start(g.par_sb[:, :], g.par).then_inc(loaded, 16)

            @block.scalar
            def _(act):
                act.wait_ge(loaded, PRIMED + 48)
                chained = Chain(act, chain)
                for t in range(TT):
                    chained(nc.scalar.activation(sq[:, :], x[:, t, :], ACT.Square, accum_out=ss[:, t:t + 1]))
                nc.scalar.copy(sq[:, 0:1], ss[:, 0:1]).then_inc(squared, 1)
                act.wait_ge(squared, PRIMED + 2)
                nc.scalar.activation(rms[:, :], rstd[:, :], ACT.Sqrt).then_inc(rooted, 1)

            @block.vector
            def _(dve):
                dve.wait_ge(squared, PRIMED + 1)
                nc.vector.tensor_scalar(rstd[:, :], ss[:, :], 1.0 / D, 1e-6, ALU.mult, ALU.add).then_inc(squared, 1)
                dve.wait_ge(rooted, PRIMED + 1)
                nc.vector.reciprocal(rstd[:, :], rms[:, :]).then_inc(rooted, 1)
                dve.wait_ge(rooted, PRIMED + 2)
                gain = cut(g.par_sb, PCOLS["ln1_g"], KT)
                with dve.Fori(0, TT) as i:
                    dve.wait_ge(turned, PRIMED + i)
                    nc.vector.tensor_scalar(xn[:, :], x[:, ds(i, 1), :].rearrange("p a d -> p (a d)"),
                                            rstd[:, ds(i, 1)], None, ALU.mult).then_inc(scaled, 1)
                    dve.wait_ge(turned, PRIMED + i + 1)
                    for b in range(2):
                        last = nc.vector.tensor_tensor(
                            g.nT[:, 4 * b:4 * b + 4, ds(i * P, P)],
                            tp[b][:, :].rearrange("p (k t) -> p k t", k=4),
                            wide(gain[:, 4 * b:4 * b + 4], 2, (P, 4, P)), ALU.mult)
                    last.then_inc(taken, 1)

            @block.tensor
            def _(pe):
                with pe.Fori(0, TT) as i:
                    pe.wait_ge(scaled, PRIMED + i + 1)
                    pe.wait_ge(taken, PRIMED + i)
                    for k in range(KT):
                        last = nc.tensor.transpose(tp[k // 4][:, (k % 4) * P:(k % 4 + 1) * P],
                                                   xn[:, k * P:(k + 1) * P], small[:, :])
                    last.then_inc(turned, 1)


def project(nc, g):
    MT = 3072 // P
    CONV = 3 * FT
    with Ctx(nc, "pj") as c:
        w = [c.sb(f"w{s}", (P, KT, P)) for s in range(2)]
        raw = [c.sb(f"raw{s}", (P, TOK)) for s in range(2)]
        mixed = [c.sb(f"mixed{s}", (P, TOK)) for s in range(2)]
        acc = [[c.ps(f"acc{s}{n}") for n in range(NCH)] for s in range(2)]
        w_in = [c.sem(f"w_in{s}") for s in range(2)]
        done = [c.sem(f"done{s}") for s in range(2)]
        copied = [c.sem(f"copied{s}") for s in range(2)]
        conved = [c.sem(f"conved{s}") for s in range(2)]
        stored = [c.sem(f"stored{s}") for s in range(2)]
        chain = c.sem("chain")
        STEPS = MT // 2
        with nc.Block() as block:
            @block.sync
            def _(sp):
                c.prime(sp)
                def load(i, s):
                    sp.wait_ge(done[s], PRIMED + NCH * i)
                    sp.dma_start(w[s][:, :, :], g.w_in[ds(2 * i + s, 1)].rearrange("a p k n -> (a p) k n")
                                 ).then_inc(w_in[s], 16)

                def store(i, s, conv):
                    if conv:
                        sp.wait_ge(conved[s], PRIMED + i + 1)
                    else:
                        sp.wait_ge(copied[s], PRIMED + NCH * i + NCH)
                    sp.dma_start(g.proj[ds((2 * i + s) * P, P), :], (mixed if conv else raw)[s][:, :]
                                 ).then_inc(stored[s], 16)
                for s in range(2):
                    load(0, s)
                for conv, lo, hi in ((True, 0, CONV // 2), (False, CONV // 2, STEPS - 1)):
                    with sp.Fori(lo, hi) as i:
                        for s in range(2):
                            load(i + 1, s)
                            store(i, s, conv)
                for s in range(2):
                    store(STEPS - 1, s, False)
                for s in range(2):
                    sp.wait_ge(stored[s], PRIMED + 16 * STEPS)

            @block.tensor
            def _(pe):
                with pe.Fori(0, STEPS) as i:
                    for s in range(2):
                        pe.wait_ge(w_in[s], PRIMED + 16 * i + 16)
                        for n in range(NCH):
                            pe.wait_ge(copied[s], PRIMED + NCH * i)
                            for k in range(KT):
                                last = nc.tensor.matmul(acc[s][n][:, 0:CW], w[s][:, k, :],
                                                        g.nT[:, k, n * CW:(n + 1) * CW],
                                                        start=(k == 0), stop=(k == KT - 1))
                            last.then_inc(done[s], 1)

            @block.scalar
            def _(act):
                with act.Fori(0, STEPS) as i:
                    for s in range(2):
                        act.wait_ge(stored[s], PRIMED + 16 * i)
                        for n in range(NCH):
                            act.wait_ge(done[s], PRIMED + NCH * i + n + 1)
                            nc.scalar.copy(raw[s][:, n * CW:(n + 1) * CW], acc[s][n][:, 0:CW]
                                           ).then_inc(copied[s], 1)

            @block.vector
            def _(dve):
                with dve.Fori(0, CONV // 2) as i:
                    chained = Chain(dve, chain, i * 6)
                    for s in range(2):
                        dve.wait_ge(copied[s], PRIMED + NCH * i + NCH)
                        dve.wait_ge(stored[s], PRIMED + 16 * i)
                        tap = lambda n: g.par_sb[:, ds(PCOLS["conv"] + n * CONV + 2 * i + s, 1)]
                        chained(nc.vector.tensor_scalar(mixed[s][:, :], raw[s][:, :], tap(1), None, ALU.mult))
                        for lo, ln, _p in SEQS:
                            last = nc.vector.scalar_tensor_tensor(
                                out=mixed[s][:, lo + 1:lo + ln], in0=raw[s][:, lo:lo + ln - 1], scalar=tap(0),
                                in1=mixed[s][:, lo + 1:lo + ln], op0=ALU.mult, op1=ALU.add)
                            if lo == 0:
                                chained(last)
                        chained(last)
                        for lo, ln, _p in SEQS:
                            last = nc.vector.scalar_tensor_tensor(
                                out=mixed[s][:, lo:lo + ln - 1], in0=raw[s][:, lo + 1:lo + ln], scalar=tap(2),
                                in1=mixed[s][:, lo:lo + ln - 1], op0=ALU.mult, op1=ALU.add)
                        last.then_inc(conved[s], 1)


def lora_in(nc, g):
    CASES = [("mix_w", 0), ("mix_a", 0), ("mix_w", 1), ("mix_a", 1), ("mix_g", 0)]
    with Ctx(nc, "lo") as c:
        delta = c.sb("delta", (P, KT, TOK))
        mixed = [c.sb(f"mixed{s}", (P, TOK)) for s in range(2)]
        w = c.sb("w", (P, KT, 4 * HD + GL))
        acc = [c.ps(f"acc{n}") for n in range(NCH)]
        acc2 = [c.ps(f"acc2{n}") for n in range(NCH)]
        loaded, mixed_s, copied, chain = c.sem("loaded"), c.sem("mixed_s"), c.sem("copied"), c.sem("chain")
        used = [c.sem(f"used{s}") for s in range(2)]
        cols = [(0, HD), (HD, HD), (2 * HD, HD), (3 * HD, HD), (4 * HD, GL)]
        with nc.Block() as block:
            @block.sync
            def _(sp):
                c.prime(sp)
                sp.dma_start(w[:, :, :], g.lora1).then_inc(loaded, 16)

            @block.gpsimd
            def _(pool):
                for t in (g.hid, g.hidg):
                    nc.gpsimd.memset(t[:, :, LEN_A:PAD_B], 0.0)
                    nc.gpsimd.memset(t[:, :, PAD_B + LEN_B:PTOK], 0.0)

            @block.vector
            def _(dve):
                chained = Chain(dve, chain)
                nT = g.nT
                for lo, ln, _p in SEQS:
                    hi = lo + ln
                    nc.vector.tensor_tensor(delta[:, :, lo + 1:hi - 1], nT[:, :, lo:hi - 2], nT[:, :, lo + 2:hi],
                                            ALU.add)
                    nc.vector.tensor_copy(delta[:, :, lo:lo + 1], nT[:, :, lo + 1:lo + 2])
                    chained(nc.vector.tensor_copy(delta[:, :, hi - 1:hi], nT[:, :, hi - 2:hi - 1]))
                for k in range(KT):
                    last = nc.vector.scalar_tensor_tensor(out=delta[:, k, :], in0=delta[:, k, :], scalar=0.5,
                                                          in1=nT[:, k, 0:TOK], op0=ALU.mult, op1=ALU.subtract)
                    if k == 0:
                        chained(last)
                chained(last)
                for m, (mix, d) in enumerate(CASES):
                    with dve.Fori(0, KT // 2) as i:
                        for s in range(2):
                            dve.wait_ge(used[s], PRIMED + m * (KT // 2) + i)
                            nc.vector.scalar_tensor_tensor(
                                out=mixed[s][:, :], in0=delta[:, ds(2 * i + s, 1), :].rearrange("p a t -> p (a t)"),
                                scalar=g.par_sb[:, ds(PCOLS[mix] + d * KT + 2 * i + s, 1)],
                                in1=nT[:, ds(2 * i + s, 1), 0:TOK].rearrange("p a t -> p (a t)"),
                                op0=ALU.mult, op1=ALU.add).then_inc(mixed_s, 1)

            @block.tensor
            def _(pe):
                pe.wait_ge(loaded, PRIMED + 16)
                for m, (_mix, _d) in enumerate(CASES):
                    lo, wd = cols[m]
                    if m:
                        pe.wait_ge(copied, PRIMED + m)
                    for k in range(KT):
                        pe.wait_ge(mixed_s, PRIMED + m * KT + k + 1)
                        for n in range(NCH):
                            for a, (off, rows) in enumerate(((0, min(wd, P)), (P, wd - P))):
                                if rows <= 0:
                                    continue
                                last = nc.tensor.matmul((acc, acc2)[a][n][0:rows, 0:CW],
                                                        w[:, k, lo + off:lo + off + rows],
                                                        mixed[k % 2][:, n * CW:(n + 1) * CW],
                                                        start=(k == 0), stop=(k == KT - 1))
                        last.then_inc(used[k % 2], 1)

            @block.scalar
            def _(act):
                for m, (_mix, _d) in enumerate(CASES):
                    act.wait_ge(used[1], PRIMED + (m + 1) * (KT // 2))
                    wd = cols[m][1]
                    func = (ACT.Tanh, ACT.Copy, ACT.Tanh, ACT.Copy, ACT.Sigmoid)[m]
                    parts = [(g.hid[:, m, :], acc, HD)] if m < 4 else [(g.hidg[:, 0, :], acc, P),
                                                                       (g.hidg[0:GL - P, 1, :], acc2, GL - P)]
                    for dst, ps, rows in parts:
                        for n in range(NCH):
                            lo = n * CW
                            for a, ln, p in SEQS:
                                x0, x1 = max(lo, a), min(lo + CW, a + ln)
                                if x0 < x1:
                                    last = nc.scalar.activation(dst[:, p + x0 - a:p + x1 - a],
                                                                ps[n][0:rows, x0 - lo:x1 - lo], func)
                    last.then_inc(copied, 1)


def prep(nc, g):
    with Ctx(nc, "pr") as c:
        r, k, v = c.sb("r", (P, PTOK)), c.sb("k", (P, PTOK)), c.sb("v", (P, PTOK))
        w2 = c.sb("w2", (HD, 4, P))
        heads = c.sb("heads", (P, P))
        first = c.sb("first", (P, PTOK))
        keep = c.sb("keep", (P, 2, CHUNKS))
        q, kk, kds = c.sb("q", (P, PTOK)), c.sb("kk", (P, PTOK)), c.sb("kds", (P, PTOK))
        sg = [c.sb(f"sg{d}", (P, PTOK)) for d in range(2)]
        av = [c.sb(f"av{d}", (P, PTOK)) for d in range(2)]
        cs = [c.sb(f"cs{d}", (P, PTOK)) for d in range(2)]
        ex = [c.sb(f"ex{d}", (P, PTOK)) for d in range(2)]
        kd = [c.sb(f"kd{d}", (P, PTOK)) for d in range(2)]
        e1 = c.sb("e1", (P, PTOK))
        tot = c.sb("tot", (P, 2, CHUNKS))
        sx = [c.sb(f"sx{d}", (P, CHUNKS, 5, CH)) for d in range(2)]
        psa, psb = c.ps("psa", (P, NCH, 512)), c.ps("psb", (P, NCH, 512))
        consts, loaded, zeroed = c.sem("consts"), c.sem("loaded"), c.sem("zeroed")
        products = c.sem("products")
        squared, floored, rooted = c.sem("squared"), c.sem("floored"), c.sem("rooted")
        sig_w, sig_a, summed, exped = c.sem("sig_w"), c.sem("sig_a"), c.sem("summed"), c.sem("exped")
        scaled_r, vcopied, ready = c.sem("scaled_r"), c.sem("vcopied"), c.sem("ready")
        bonus, stored, chain = c.sem("bonus"), c.sem("stored"), c.sem("chain")
        par = lambda name, off: g.par_sb[:, ds(PCOLS[name] + off, 1)]
        chunked = lambda t: t[:, :].rearrange("p (c t) -> p c t", t=CH)
        with nc.Block() as block:
            @block.sync
            def _(sp):
                c.prime(sp)
                sp.dma_start(heads[:, :], g.small_of("heads")).then_inc(consts, 16)
                sp.dma_start(first[:, :], g.first).then_inc(consts, 16)
                sp.dma_start(keep[:, :, :], g.keep.rearrange("p (d c) -> p d c", d=2)).then_inc(consts, 16)
                sp.wait_ge(zeroed, PRIMED + 3)
                with sp.Fori(0, FT) as f:
                    sp.wait_ge(stored, PRIMED + 48 * f)
                    for n, t in enumerate((r, k, v)):
                        for a, ln, p in SEQS:
                            sp.dma_start(t[:, p:p + ln], g.proj[ds((n * FT + f) * P, P), a:a + ln]
                                         ).then_inc(loaded, 16)
                    sp.dma_start(w2[:, :, :], g.lora2[ds(f, 1)].rearrange("a p m n -> (a p) m n")
                                 ).then_inc(loaded, 16)
                    for d in range(2):
                        sp.wait_ge(ready, PRIMED + 2 * f + d + 1)
                        sp.wait_ge(vcopied, PRIMED + 2 * f + d + 1)
                        sp.dma_start(g.sx[d, ds(f, 1)].rearrange("a p n -> (a p) n"),
                                     sx[d][:, :, :, :].rearrange("p c x t -> p (c x t)")).then_inc(stored, 16)
                    sp.wait_ge(bonus, PRIMED + f + 1)
                    sp.dma_start(g.bonus[ds(f * P, P), :], q[:, :]).then_inc(stored, 16)
                sp.wait_ge(stored, PRIMED + 48 * FT)

            @block.gpsimd
            def _(pool):
                for t in (r, k, v):
                    for a, ln, p in SEQS:
                        last = nc.gpsimd.memset(t[:, p + ln:PAD_B if p == 0 else PTOK], 0.0)
                    last.then_inc(zeroed, 1)

            @block.tensor
            def _(pe):
                pe.wait_ge(consts, PRIMED + 48)
                with pe.Fori(0, FT) as f:
                    def product(ps, lhsT, rhs):
                        for n in range(NCH):
                            last = nc.tensor.matmul(ps[:, n, 0:PW], lhsT, rhs[:, n * PW:(n + 1) * PW],
                                                    start=True, stop=True)
                        last.then_inc(products, 1)
                    pe.wait_ge(squared, PRIMED + f + 1)
                    product(psa, heads[:, :], q)
                    pe.wait_ge(loaded, PRIMED + 112 * f + 112)
                    pe.wait_ge(bonus, PRIMED + f)
                    product(psb, w2[:, 0, :], g.hid[:, 0, :])
                    pe.wait_ge(floored, PRIMED + f + 1)
                    product(psa, w2[:, 1, :], g.hid[:, 1, :])
                    pe.wait_ge(sig_w, PRIMED + 2 * f + 1)
                    product(psb, w2[:, 2, :], g.hid[:, 2, :])
                    pe.wait_ge(sig_a, PRIMED + 2 * f + 1)
                    product(psa, w2[:, 3, :], g.hid[:, 3, :])
                    pe.wait_ge(sig_w, PRIMED + 2 * f + 2)
                    pe.wait_ge(scaled_r, PRIMED + f + 1)
                    product(psb, heads[:, :], kds)

            @block.scalar
            def _(act):
                with act.Fori(0, FT) as f:
                    act.wait_ge(loaded, PRIMED + 112 * f + 112)
                    nc.scalar.activation(q[:, :], k[:, :], ACT.Square, scale=par("k_k", f)).then_inc(squared, 1)
                    for d in range(2):
                        nc.scalar.copy(sx[d][:, :, 4, :], chunked(v)).then_inc(vcopied, 1)
                    act.wait_ge(floored, PRIMED + f + 1)
                    nc.scalar.activation(q[:, :], q[:, :], ACT.Sqrt).then_inc(rooted, 1)
                    split = lambda t: t[:, :].rearrange("p (n t) -> p n t", n=NCH)
                    for d in range(2):
                        act.wait_ge(products, PRIMED + 6 * f + 2 * d + 2)
                        nc.scalar.activation(split(sg[d]), psb[:, :, 0:PW], ACT.Sigmoid,
                                             bias=par("decay_w0", d * FT + f)).then_inc(sig_w, 1)
                        act.wait_ge(products, PRIMED + 6 * f + 2 * d + 3)
                        nc.scalar.activation(split(av[d]), psa[:, :, 0:PW], ACT.Sigmoid,
                                             bias=par("aaa_a0", d * FT + f)).then_inc(sig_a, 1)
                    for d in range(2):
                        act.wait_ge(summed, PRIMED + 2 * f + d + 1)
                        if d:
                            act.wait_ge(ready, PRIMED + 2 * f + 1)
                        nc.scalar.activation(tot[:, d, :], tot[:, d, :], ACT.Exp, scale=-DECAY)
                        nc.scalar.activation(e1[:, :], cs[d][:, :], ACT.Exp, scale=-DECAY).then_inc(exped, 1)
                        nc.scalar.activation(ex[d][:, :], ex[d][:, :], ACT.Exp, scale=-DECAY).then_inc(exped, 1)
                        nc.scalar.activation(cs[d][:, :], cs[d][:, :], ACT.Exp, scale=DECAY).then_inc(exped, 1)

            @block.vector
            def _(dve):
                dve.wait_ge(consts, PRIMED + 48)
                LINKS = 8
                with dve.Fori(0, FT) as f:
                    chained = Chain(dve, chain, f * LINKS)
                    dve.wait_ge(products, PRIMED + 6 * f + 1)
                    nc.vector.tensor_scalar(q[:, :].rearrange("p (n t) -> p n t", n=NCH), psa[:, :, 0:PW], 1e-24, None, ALU.max
                                            ).then_inc(floored, 1)
                    dve.wait_ge(rooted, PRIMED + f + 1)
                    chained(nc.vector.reciprocal(q[:, :], q[:, :]))
                    chained(nc.vector.scalar_tensor_tensor(out=kk[:, :], in0=k[:, :], scalar=par("k_k", f),
                                                           in1=q[:, :], op0=ALU.mult, op1=ALU.mult))
                    for d in range(2):
                        dve.wait_ge(sig_w, PRIMED + 2 * f + d + 1)
                        dve.wait_ge(sig_a, PRIMED + 2 * f + d + 1)
                        c3, s3 = chunked(cs[d]), chunked(sg[d])
                        nc.vector.tensor_scalar(kd[d][:, :], av[d][:, :], -1.0, par("k_a", f), ALU.add, ALU.mult)
                        chained(nc.vector.tensor_tensor_scan(cs[d][:, :], first[:, :], sg[d][:, :], 0.0,
                                                             ALU.mult, ALU.add))
                        nc.vector.tensor_copy(tot[:, d, :].unsqueeze(2), c3[:, :, CH - 1:CH])
                        last = nc.vector.scalar_tensor_tensor(out=kd[d][:, :], in0=kd[d][:, :], scalar=1.0,
                                                              in1=k[:, :], op0=ALU.add, op1=ALU.mult)
                        nc.vector.tensor_tensor(av[d][:, :], kk[:, :], av[d][:, :], ALU.mult)
                        if d == 0:
                            chained(last)
                            nc.vector.tensor_tensor(ex[d][:, :], cs[d][:, :], sg[d][:, :], ALU.subtract
                                                    ).then_inc(summed, 1)
                        else:
                            chained(last)
                            chained(nc.vector.tensor_tensor(chunked(ex[d]), c3[:, :, CH - 1:CH].to_broadcast([P, CHUNKS, CH]),
                                                            c3, ALU.subtract))
                            nc.vector.tensor_tensor(cs[d][:, :], ex[d][:, :], sg[d][:, :], ALU.add
                                                    ).then_inc(summed, 1)
                    chained(nc.vector.tensor_tensor(kds[:, :], kd[0][:, :], kd[1][:, :], ALU.add))
                    nc.vector.scalar_tensor_tensor(out=kds[:, :], in0=r[:, :], scalar=par("r_k", f), in1=kds[:, :],
                                                   op0=ALU.mult, op1=ALU.mult).then_inc(scaled_r, 1)
                    for d in range(2):
                        dve.wait_ge(exped, PRIMED + 6 * f + 3 * d + 3)
                        o = lambda x: sx[d][:, :, x, :]
                        nc.vector.tensor_tensor(g.etot[:, d, ds(f, 1), :], tot[:, d, :].unsqueeze(1), keep[:, d, :].unsqueeze(1), ALU.mult)
                        nc.vector.tensor_tensor(o(0), chunked(r), chunked(e1), ALU.mult)
                        nc.vector.scalar_tensor_tensor(out=o(1), in0=chunked(kk), scalar=-1.0, in1=chunked(ex[d]),
                                                       op0=ALU.mult, op1=ALU.mult)
                        nc.vector.tensor_tensor(o(2), chunked(av[d]), chunked(cs[d]), ALU.mult)
                        nc.vector.tensor_tensor(o(3), chunked(kd[d]), chunked(cs[d]), ALU.mult).then_inc(ready, 1)
                    dve.wait_ge(products, PRIMED + 6 * f + 6)
                    nc.vector.tensor_tensor(q[:, :].rearrange("p (n t) -> p n t", n=NCH), psb[:, :, 0:PW],
                                            v[:, :].rearrange("p (n t) -> p n t", n=NCH), ALU.mult
                                            ).then_inc(bonus, 1)
                    assert chained.n == LINKS


def chunks(nc, g):
    J = 2
    with Ctx(nc, "ch") as c:
        mask = {}
        names = ["ident", "ident2", "own"]
        for d in range(2):
            names += [f"incl{d}", f"strict_bd{d}", f"after_bd{d}", f"pair{d}", f"pairT_bd{d}"]
            names += [f"lev{n}_{d}" for n in range(LEVELS)] + [f"lev{n}_bd{d}" for n in range(LEVELS)]
        masks = c.sb("masks", (P, NSMALL))
        for n in names:
            lo, wd = SCOLS[n]
            mask[n] = masks[:, lo:lo + wd]
        sx = [c.sb(f"sx{d}", (P, J, CHUNKS, 5, CH)) for d in range(2)]
        ys = [c.sb(f"ys{d}", (P, J, PTOK)) for d in range(2)]
        sbd = [c.sb(f"sbd{d}", (P, J, 4, 2, CH)) for d in range(2)]
        bka = [c.sb(f"bka{d}", (P, J, P)) for d in range(2)]
        e_d = [c.sb(f"ed{d}", (P, J * 64 + J * P)) for d in range(2)]
        ebd = [c.sb(f"ebd{d}", (P, J, P)) for d in range(2)]
        akT = [c.sb(f"akT{d}", (P, J, P)) for d in range(2)]
        arT = [c.sb(f"arT{d}", (P, J, 2, CH)) for d in range(2)]
        xst = [c.sb(f"xst{d}", (P, J, CH)) for d in range(2)]
        xbd = [c.sb(f"xbd{d}", (P, J, P)) for d in range(2)]
        bkt = [c.sb(f"bkt{d}", (P, J, 2, P)) for d in range(2)]
        vst = [c.sb(f"vst{d}", (P, J, CH)) for d in range(2)]
        vbd = [c.sb(f"vbd{d}", (P, J, 2, CH)) for d in range(2)]
        bst = [c.sb(f"bst{d}", (P, J, CH)) for d in range(2)]
        ust = [c.sb(f"ust{d}", (P, J, CH)) for d in range(2)]
        ubd = [c.sb(f"ubd{d}", (P, J, 2, CH)) for d in range(2)]
        sst = [c.sb(f"sst{d}", (P, J, CH)) for d in range(2)]
        snw = [c.sb(f"snw{d}", (P, J, CH)) for d in range(2)]
        stb = [c.sb(f"stb{d}", (P, J, 2, CH)) for d in range(2)]
        psa = [c.ps(f"psa{d}") for d in range(2)]
        psm = [c.ps(f"psm{d}") for d in range(2)]
        pse = [c.ps(f"pse{d}") for d in range(2)]
        pss = [c.ps(f"pss{d}") for d in range(2)]
        consts, zeroed, loaded, stored = c.sem("consts"), c.sem("zeroed"), c.sem("loaded"), c.sem("stored")
        two = lambda name: [c.sem(f"{name}{d}") for d in range(2)]
        staged, first_products, a_read, v_copied = two("staged"), two("first"), two("a_read"), two("v_copied")
        turned, prepared = two("turned"), two("prepared")
        z_ready, x_ready, e_ready, e_copied = two("z_ready"), two("x_ready"), two("e_ready"), two("e_copied")
        b_ready, b_copied, u_ready, u_copied = two("b_ready"), two("b_copied"), two("u_ready"), two("u_copied")
        y_ready, s_read, y_copied, s_new, chain = two("y_ready"), two("s_read"), two("y_copied"), two("s_new"), c.sem("chain")
        PASSES = FT // J
        both_ends = lambda n: (n, n * -1 + (CHUNKS - 1))
        with nc.Block() as block:
            @block.sync
            def _(sp):
                c.prime(sp)
                sp.dma_start(masks[:, :], g.small).then_inc(consts, 16)
                with sp.Fori(0, PASSES) as p:
                    for d in range(2):
                        sp.wait_ge(y_ready[d], PRIMED + p * CHUNKS)
                        for j in range(J):
                            sp.dma_start(sx[d][:, j].rearrange("p c x t -> p (c x t)"),
                                         g.sx[d, ds(p * J + j, 1)].rearrange("a p n -> (a p) n")).then_inc(loaded, 16)
                    for d in range(2):
                        sp.wait_ge(y_copied[d], PRIMED + (p + 1) * CHUNKS)
                        for j in range(J):
                            sp.dma_start(g.ydir[d, ds(p * J + j, 1)].rearrange("a p n -> (a p) n"), ys[d][:, j, :]
                                         ).then_inc(stored, 16)
                sp.wait_ge(stored, PRIMED + 32 * J * PASSES)

            @block.gpsimd
            def _(pool):
                for d in range(2):
                    for t in (sbd[d], vbd[d], stb[d], sst[d]):
                        nc.gpsimd.memset(t[:], 0.0).then_inc(zeroed, 1)

            @block.scalar
            def _(act):
                act.wait_ge(zeroed, PRIMED + 8)
                with act.Fori(0, PASSES) as p:
                    act.wait_ge(loaded, PRIMED + 32 * J * (p + 1))
                    act.wait_ge(stored, PRIMED + 32 * J * p)
                    with act.Fori(0, CHUNKS) as n:
                        i = p * CHUNKS + n
                        at = both_ends(n)
                        for d in range(2):
                            act.wait_ge(b_ready[d], PRIMED + i)
                            for h in range(2):
                                rows = slice(h * 64, h * 64 + 64)
                                for j in range(J):
                                    last = nc.scalar.copy(
                                        sbd[d][rows, j, :, h, :],
                                        sx[d][rows, j, ds(at[d], 1), 1:5, :].rearrange("p a x t -> p (a x) t"))
                            last.then_inc(staged[d], 1)
                        for d in range(2):
                            act.wait_ge(first_products[d], PRIMED + i + 1)
                            act.wait_ge(y_ready[d], PRIMED + i)
                            nc.scalar.copy(bkt[d][:, :, :, :].rearrange("p j x t -> p (j x t)"), pse[d][:, :]
                                           ).then_inc(turned[d], 1)
                            act.wait_ge(a_read[d], PRIMED + i + 1)
                            ps_v = psm[d][:, 128:256].rearrange("p (j t) -> p j t", j=J)
                            nc.scalar.copy(vst[d][:, :, :], ps_v)
                            for h in range(2):
                                rows = slice(h * 64, h * 64 + 64)
                                last = nc.scalar.copy(vbd[d][rows, :, h, :], ps_v[rows])
                            last.then_inc(v_copied[d], 1)
                        for n_lev in range(LEVELS):
                            for d in range(2):
                                act.wait_ge(e_ready[d], PRIMED + LEVELS * i + n_lev + 1)
                                if n_lev < LEVELS - 1:
                                    nc.scalar.copy(e_d[d][:, :], pse[d][:, 0:J * 64 + J * P]).then_inc(e_copied[d], 1)
                                else:
                                    nc.scalar.copy(ebd[d][:, :, :].rearrange("p j t -> p (j t)"), pse[d][:, 0:J * P]
                                                   ).then_inc(e_copied[d], 1)
                        for d in range(2):
                            act.wait_ge(b_ready[d], PRIMED + i + 1)
                            nc.scalar.copy(bst[d][:, :, :].rearrange("p j t -> p (j t)"), pss[d][:, 0:128]
                                           ).then_inc(b_copied[d], 1)
                        for d in range(2):
                            act.wait_ge(s_read[d], PRIMED + i + 1)
                            nc.scalar.copy(ys[d][:, :, ds(at[d] * CH, CH)],
                                           pss[d][:, 256:384].rearrange("p (j t) -> p j t", j=J)).then_inc(y_copied[d], 1)

            @block.tensor
            def _(pe):
                pe.wait_ge(consts, PRIMED + 16)
                mm = nc.tensor.matmul
                flat = lambda t: t.rearrange("p a b -> p (a b)")
                with pe.Fori(0, PASSES) as p:
                    with pe.Fori(0, CHUNKS) as n:
                        i = p * CHUNKS + n
                        at = both_ends(n)
                        for d in range(2):
                            def of(j, lo, hi):
                                return sx[d][:, j, ds(at[d], 1), lo:hi, :].rearrange("p a x t -> p (a x t)")
                            pe.wait_ge(staged[d], PRIMED + i + 1)
                            pe.wait_ge(prepared[d], PRIMED + i)
                            pe.wait_ge(x_ready[d], PRIMED + LEVELS * i)
                            pe.wait_ge(e_copied[d], PRIMED + LEVELS * i)
                            for j in range(J):
                                bd = lambda x: flat(sbd[d][:, j, x, :, :])
                                mm(psa[d][:, j * 256:j * 256 + 128], bd(1), of(j, 0, 2), start=True, stop=True)
                                mm(psa[d][:, j * 256 + 128:j * 256 + 256], bd(2), of(j, 0, 2), start=True, stop=True)
                                mm(psm[d][:, j * 64:j * 64 + 64], bd(0), of(j, 2, 3), start=True, stop=True)
                                mm(psm[d][:, 128 + j * 64:192 + j * 64], bd(3), mask["ident2"], start=True, stop=True)
                                for x in (1, 2):
                                    last = nc.tensor.transpose(pse[d][:, (2 * j + x - 1) * P:(2 * j + x) * P], bd(x),
                                                               mask["ident"])
                            last.then_inc(first_products[d], 1)
                        for n_lev in range(LEVELS):
                            for d in range(2):
                                if n_lev == 0:
                                    pe.wait_ge(prepared[d], PRIMED + i + 1)
                                    pe.wait_ge(v_copied[d], PRIMED + i + 1)
                                    pe.wait_ge(turned[d], PRIMED + i + 1)
                                else:
                                    pe.wait_ge(e_copied[d], PRIMED + LEVELS * i + n_lev)
                                for j in range(J):
                                    last = mm(psm[d][:, 256 + j * 64:320 + j * 64], bka[d][:, j, :],
                                              e_d[d][:, j * 64:j * 64 + 64], start=True, stop=True)
                                last.then_inc(z_ready[d], 1)
                            for d in range(2):
                                pe.wait_ge(x_ready[d], PRIMED + LEVELS * i + n_lev + 1)
                                for j in range(J):
                                    eT = e_d[d][:, J * 64 + j * P:J * 64 + (j + 1) * P]
                                    if n_lev < LEVELS - 1:
                                        mm(pse[d][:, j * 64:j * 64 + 64], eT, xst[d][:, j, :], start=True, stop=True)
                                        last = mm(pse[d][:, J * 64 + j * P:J * 64 + (j + 1) * P], xbd[d][:, j, :], eT,
                                                  start=True, stop=True)
                                    else:
                                        last = mm(pse[d][:, j * P:(j + 1) * P], eT, xbd[d][:, j, :],
                                                  start=True, stop=True)
                                last.then_inc(e_ready[d], 1)
                        for d in range(2):
                            pe.wait_ge(s_new[d], PRIMED + i)
                            pe.wait_ge(y_copied[d], PRIMED + i)
                            for j in range(J):
                                o = pss[d][:, j * 64:j * 64 + 64]
                                mm(o, flat(sbd[d][:, j, 0, :, :]), sst[d][:, j, :], start=True, stop=False)
                                last = mm(o, akT[d][:, j, :], vst[d][:, j, :], start=False, stop=True)
                            last.then_inc(b_ready[d], 1)
                        for d in range(2):
                            pe.wait_ge(b_copied[d], PRIMED + i + 1)
                            pe.wait_ge(e_copied[d], PRIMED + LEVELS * (i + 1))
                            for j in range(J):
                                last = mm(pss[d][:, 128 + j * 64:192 + j * 64], ebd[d][:, j, :], bst[d][:, j, :],
                                          start=True, stop=True)
                            last.then_inc(u_ready[d], 1)
                        for d in range(2):
                            def of(j, lo, hi):
                                return sx[d][:, j, ds(at[d], 1), lo:hi, :].rearrange("p a x t -> p (a x t)")
                            pe.wait_ge(u_copied[d], PRIMED + i + 1)
                            for j in range(J):
                                o = pss[d][:, 256 + j * 64:320 + j * 64]
                                mm(o, flat(stb[d][:, j]), of(j, 0, 1), start=True, stop=False)
                                mm(o, flat(vbd[d][:, j]), arT[d][:, j, 1, :], start=False, stop=False)
                                mm(o, flat(ubd[d][:, j]), arT[d][:, j, 0, :], start=False, stop=True)
                                o = pss[d][:, 384 + j * 64:448 + j * 64]
                                mm(o, bkt[d][:, j, 0, :], ust[d][:, j, :], start=True, stop=False)
                                last = mm(o, bkt[d][:, j, 1, :], vst[d][:, j, :], start=False, stop=True)
                            last.then_inc(y_ready[d], 1)

            @block.vector
            def _(dve):
                dve.wait_ge(consts, PRIMED + 16)
                dve.wait_ge(zeroed, PRIMED + 8)
                tt = nc.vector.tensor_tensor
                LINKS = 6
                own4 = mask["own"].rearrange("p (h t) -> p h t", h=2)

                def blocks(out, src, m):
                    return tt(out, wide(src, 2, (P, J, 2, CH)), wide(m, 1, (P, J, 2, CH)), ALU.mult)

                with dve.Fori(0, PASSES) as p:
                    with dve.Fori(0, CHUNKS) as n:
                        i = p * CHUNKS + n
                        at = both_ends(n)
                        chained = Chain(dve, chain, i * LINKS)
                        m3 = lambda name: mask[name].rearrange("p (h t) -> p h t", h=2)
                        for d in range(2):
                            dve.wait_ge(first_products[d], PRIMED + i + 1)
                            dve.wait_ge(y_ready[d], PRIMED + i)
                            ps_a = psa[d][:, :].rearrange("p (j x y t) -> p j x y t", j=J, x=2, y=2)
                            bka4 = bka[d][:, :, :].rearrange("p j (h t) -> p j h t", h=2)
                            est = e_d[d][:, 0:J * 64].rearrange("p (j t) -> p j t", j=J)
                            eT = e_d[d][:, J * 64:].rearrange("p (j t) -> p j t", j=J)
                            blocks(bka4, psm[d][:, 0:128].rearrange("p (j t) -> p j t", j=J), m3(f"after_bd{d}")
                                   ).then_inc(a_read[d], 1)
                            tt(est, ps_a[:, :, 0, 1, :], wide(mask[f"pair{d}"], 1, (P, J, CH)), ALU.mult)
                            blocks(akT[d][:, :, :].rearrange("p j (h t) -> p j h t", h=2), ps_a[:, :, 1, 1, :],
                                   m3(f"strict_bd{d}"))
                            chained(tt(arT[d][:, :, :, :], ps_a[:, :, :, 0, :],
                                       mask[f"incl{d}"].unsqueeze(1).unsqueeze(1).to_broadcast([P, J, 2, CH]), ALU.mult))
                            tt(est, est, wide(mask["ident2"], 1, (P, J, CH)), ALU.add)
                            chained(tt(bka[d][:, :, :], bka[d][:, :, :], wide(mask["ident"], 1, (P, J, P)), ALU.add))
                            tt(eT, bka[d][:, :, :], wide(mask[f"pairT_bd{d}"], 1, (P, J, P)), ALU.mult
                               ).then_inc(prepared[d], 1)
                        for n_lev in range(LEVELS):
                            for d in range(2):
                                z = psm[d][:, 256:384].rearrange("p (j t) -> p j t", j=J)
                                dve.wait_ge(z_ready[d], PRIMED + LEVELS * i + n_lev + 1)
                                if n_lev < LEVELS - 1:
                                    tt(xst[d][:, :, :], z, wide(mask[f"lev{n_lev}_{d}"], 1, (P, J, CH)), ALU.mult)
                                blocks(xbd[d][:, :, :].rearrange("p j (h t) -> p j h t", h=2), z,
                                       m3(f"lev{n_lev}_bd{d}")).then_inc(x_ready[d], 1)
                        for d in range(2):
                            dve.wait_ge(u_ready[d], PRIMED + i + 1)
                            u = pss[d][:, 128:256].rearrange("p (j t) -> p j t", j=J)
                            nc.vector.tensor_copy(ust[d][:, :, :], u)
                            blocks(ubd[d][:, :, :, :], u, own4).then_inc(u_copied[d], 1)
                        for d in range(2):
                            dve.wait_ge(y_ready[d], PRIMED + i + 1)
                            tt(snw[d][:, :, :], pss[d][:, 384:512].rearrange("p (j t) -> p j t", j=J), sst[d][:, :, :],
                               ALU.add).then_inc(s_read[d], 1)
                            dve.wait_ge(s_read[d], PRIMED + i + 1)
                            chained(tt(sst[d][:, :, :], snw[d][:, :, :],
                                       g.etot[:, d, ds(p * J, J), ds(at[d], 1)].to_broadcast([P, J, CH]), ALU.mult))
                            blocks(stb[d][:, :, :, :], sst[d][:, :, :], own4).then_inc(s_new[d], 1)
                        assert chained.n == LINKS


def mix_out(nc, g):
    with Ctx(nc, "mo") as c:
        y0, y1, bon = c.sb("y0", (P, PTOK)), c.sb("y1", (P, PTOK)), c.sb("bon", (P, PTOK))
        sq, ya = c.sb("sq", (P, PTOK)), c.sb("ya", (P, PTOK))
        heads = c.sb("heads", (P, P))
        zero = c.sb("zero", (P, KT, TT * P - TOK))
        psa, psb = c.ps("psa", (P, NCH, 512)), c.ps("psb", (P, NCH, 512))
        consts, loaded, stored, chain = c.sem("consts"), c.sem("loaded"), c.sem("stored"), c.sem("chain")
        added, products, squared, gates = c.sem("added"), c.sem("products"), c.sem("squared"), c.sem("gates")
        spread, rooted, done, pads, zeroed = c.sem("spread"), c.sem("rooted"), c.sem("done"), c.sem("pads"), c.sem("zeroed")
        w2f = c.sb("w2f", (P, 2, P))
        split = lambda t: t[:, :].rearrange("p (n t) -> p n t", n=NCH)
        par = lambda name, off: g.par_sb[:, ds(PCOLS[name] + off, 1)]
        with nc.Block() as block:
            @block.sync
            def _(sp):
                c.prime(sp)
                sp.dma_start(heads[:, :], g.small_of("heads")).then_inc(consts, 16)
                sp.wait_ge(zeroed, PRIMED + 1)
                sp.dma_start(g.mix[:, TOK:TT * P].rearrange("(k p) t -> p k t", p=P), zero[:, :, :]).then_inc(pads, 16)
                with sp.Fori(0, FT) as f:
                    sp.wait_ge(stored, PRIMED + 32 * f)
                    for n, t in enumerate((y0, y1)):
                        sp.dma_start(t[:, :], g.ydir[n, ds(f, 1)].rearrange("a p n -> (a p) n")).then_inc(loaded, 16)
                    sp.dma_start(bon[:, :], g.bonus[ds(f * P, P), :]).then_inc(loaded, 16)
                    sp.dma_start(w2f[:, 0, :], g.gate2[0:P, ds(f * P, P)]).then_inc(loaded, 16)
                    sp.dma_start(w2f[0:GL - P, 1, :], g.gate2[P:GL, ds(f * P, P)]).then_inc(loaded, 16)
                    sp.wait_ge(done, PRIMED + f + 1)
                    for a, ln, p in SEQS:
                        sp.dma_start(g.mix[ds(f * P, P), a:a + ln], ya[:, p:p + ln]).then_inc(stored, 16)
                sp.wait_ge(stored, PRIMED + 32 * FT)
                sp.wait_ge(pads, PRIMED + 16)

            @block.gpsimd
            def _(pool):
                nc.gpsimd.memset(zero[:], 0.0).then_inc(zeroed, 1)

            @block.tensor
            def _(pe):
                pe.wait_ge(consts, PRIMED + 16)
                with pe.Fori(0, FT) as f:
                    def sums(src, sem, count):
                        pe.wait_ge(sem, PRIMED + count)
                        for n in range(NCH):
                            last = nc.tensor.matmul(psa[:, n, 0:PW], heads[:, :], src[:, n * PW:(n + 1) * PW],
                                                    start=True, stop=True)
                        last.then_inc(products, 1)
                    sums(y0, added, f + 1)
                    pe.wait_ge(loaded, PRIMED + 80 * f + 80)
                    pe.wait_ge(done, PRIMED + f)
                    for n in range(NCH):
                        nc.tensor.matmul(psb[:, n, 0:PW], w2f[:, 0, :], g.hidg[:, 0, n * PW:(n + 1) * PW],
                                         start=True, stop=False)
                        last = nc.tensor.matmul(psb[:, n, 0:PW], w2f[0:GL - P, 1, :],
                                                g.hidg[0:GL - P, 1, n * PW:(n + 1) * PW], start=False, stop=True)
                    last.then_inc(gates, 1)
                    sums(sq, squared, f + 1)

            @block.scalar
            def _(act):
                with act.Fori(0, FT) as f:
                    act.wait_ge(chain, PRIMED + 5 * f + 1)
                    nc.scalar.activation(sq[:, :], y1[:, :], ACT.Square).then_inc(squared, 1)
                    act.wait_ge(spread, PRIMED + f + 1)
                    nc.scalar.activation(sq[:, :], sq[:, :], ACT.Sqrt).then_inc(rooted, 1)

            @block.vector
            def _(dve):
                with dve.Fori(0, FT) as f:
                    chained = Chain(dve, chain, f * 5)
                    dve.wait_ge(loaded, PRIMED + 80 * f + 80)
                    nc.vector.tensor_tensor(y0[:, :], y0[:, :], y1[:, :], ALU.add).then_inc(added, 1)
                    dve.wait_ge(products, PRIMED + 2 * f + 1)
                    chained(nc.vector.scalar_tensor_tensor(out=split(y1), in0=psa[:, :, 0:PW], scalar=-1.0 / HD,
                                                           in1=split(y0), op0=ALU.mult, op1=ALU.add))
                    dve.wait_ge(products, PRIMED + 2 * f + 2)
                    nc.vector.tensor_scalar(split(sq), psa[:, :, 0:PW], 1.0 / HD, 64e-5, ALU.mult, ALU.add
                                            ).then_inc(spread, 1)
                    dve.wait_ge(rooted, PRIMED + f + 1)
                    chained(nc.vector.reciprocal(sq[:, :], sq[:, :]))
                    chained(nc.vector.tensor_tensor(y1[:, :], y1[:, :], sq[:, :], ALU.mult))
                    chained(nc.vector.tensor_scalar(y1[:, :], y1[:, :], par("lnx_g", f), par("lnx_b", f),
                                                    ALU.mult, ALU.add))
                    chained(nc.vector.tensor_tensor(y1[:, :], y1[:, :], bon[:, :], ALU.add))
                    dve.wait_ge(gates, PRIMED + f + 1)
                    dve.wait_ge(stored, PRIMED + 32 * f)
                    nc.vector.tensor_tensor(split(ya), psb[:, :, 0:PW], split(y1), ALU.mult).then_inc(done, 1)


def attention(nc, g):
    units = []
    vtiles = []
    for a, ln, _p in SEQS:
        v0 = len(vtiles)
        pieces = [(a + t, min(P, ln - t)) for t in range(0, ln, P)]
        vtiles += pieces
        even = -(-ln // len(pieces))
        units += [(a + t, min(even, ln - t), a, ln, v0) for t in range(0, ln, even)]
    NU, NV = len(units), len(vtiles)
    with Ctx(nc, "at") as c:
        q, k, v = c.sb("q", (P, TOK)), c.sb("k", (P, TOK)), c.sb("v", (P, TOK))
        sq, rot = c.sb("sq", (P, TOK)), c.sb("rot", (P, TOK))
        cos, sin = c.sb("cos", (P, TOK)), c.sb("sin", (P, TOK))
        consts_sb = c.sb("consts", (P, NSMALL))
        small = lambda name: consts_sb[:, SCOLS[name][0]:SCOLS[name][0] + SCOLS[name][1]]
        vt = c.sb("vt", (P, NV, P))
        pr = [[c.sb(f"pr{s}{x}", (P, LEN_B)) for x in range(2)] for s in range(2)]
        amT = c.sb("amT", (P, 9, P))
        oT = c.sb("oT", (P, TOK))
        st = c.sb("st", (P, 2, 8))
        lam = c.sb("lam", (P, 4 * HD))
        lams = c.sb("lams", (P, 4))
        sg = c.sb("sg", (P, 1))
        pS = [c.ps("pS0", (P, 3, 512)), c.ps("pS1", (P, 3, 512))]
        pT, pO = c.ps("pT"), c.ps("pO")
        consts, loaded, stored, chain = c.sem("consts"), c.sem("loaded"), c.sem("stored"), c.sem("chain")
        squared, sums, meaned, rooted = c.sem("squared"), c.sem("sums"), c.sem("meaned"), c.sem("rooted")
        normed, rotated, roped, vturned, vcopied = c.sem("normed"), c.sem("rotated"), c.sem("roped"), c.sem("vturned"), c.sem("vcopied")
        scores = [c.sem("scores0"), c.sem("scores1")]
        maxed = [c.sem("maxed0"), c.sem("maxed1")]
        exped = [c.sem("exped0"), c.sem("exped1")]
        lamb, diffed, turned, tcopied, outs, ocopied, odone = (c.sem("lamb"), c.sem("diffed"), c.sem("turned"), c.sem("tcopied"),
                                                               c.sem("outs"), c.sem("ocopied"), c.sem("odone"))
        c_max = [c.sem("rowmax0"), c.sem("rowmax1")]
        batches = {u: -(-(-(-units[u][3] // P)) // 4) for u in range(NU)}
        NB = sum(batches.values())
        bat0 = [sum(batches[w] for w in range(u)) for u in range(NU)]
        scale = HD ** -0.5
        four = lambda t: t[:, :].rearrange("p (n t) -> p n t", n=NCH)
        bank = lambda n: (pS[0][:, n, 0:CW] if n < 3 else pS[1][:, 0, 0:CW])
        with nc.Block() as block:
            @block.sync
            def _(sp):
                c.prime(sp)
                sp.dma_start(consts_sb[:, :], g.small).then_inc(consts, 16)
                sp.dma_start(cos[:, :], g.cos).then_inc(consts, 16)
                sp.dma_start(sin[:, :], g.sin).then_inc(consts, 16)
                sp.dma_start(lam[:, :], g.lambdas.partition_broadcast(P)).then_inc(consts, 16)
                with sp.Fori(0, HEADS) as h:
                    sp.wait_ge(stored, PRIMED + 16 * h)
                    for n, t in enumerate((q, k, v)):
                        sp.dma_start(t[:, :], g.proj[ds((12 + n * FT + h) * P, P), :]).then_inc(loaded, 16)
                    sp.wait_ge(odone, PRIMED + h + 1)
                    sp.dma_start(g.mix[ds(RW + h * P, P), 0:TOK], oT[:, :]).then_inc(stored, 16)
                sp.wait_ge(stored, PRIMED + 16 * HEADS)

            @block.tensor
            def _(pe):
                pe.wait_ge(consts, PRIMED + 64)
                mm = nc.tensor.matmul
                with pe.Fori(0, HEADS) as h:
                    def over(lhsT, src, sem):
                        for n in range(NCH):
                            last = mm(bank(n), lhsT, src[:, n * CW:(n + 1) * CW], start=True, stop=True)
                        last.then_inc(sem, 1)

                    pe.wait_ge(loaded, PRIMED + 48 * h + 48)
                    for b in range(NV // 4):
                        pe.wait_ge(vcopied, PRIMED + 3 * h + b)
                        for w in range(4):
                            t0, tn = vtiles[4 * b + w]
                            last = nc.tensor.transpose(pT[0:tn, w * P:(w + 1) * P], v[:, t0:t0 + tn], small("ident"))
                        last.then_inc(vturned, 1)
                    for x in range(2):
                        pe.wait_ge(squared, PRIMED + 3 * h + x + 1)
                        pe.wait_ge(roped, PRIMED + 2 * h + x)
                        pe.wait_ge(meaned, PRIMED + 3 * h)
                        over(small("heads"), sq, sums)
                        pe.wait_ge(normed, PRIMED + 2 * h + x + 1)
                        over(small("swap"), q if x == 0 else k, rotated)
                    pe.wait_ge(roped, PRIMED + 2 * h + 2)

                    def out_of(u):
                        q0, qn, a, ln, v0 = units[u]
                        pe.wait_ge(diffed, PRIMED + NU * h + u + 1)
                        nk = -(-ln // P)
                        if u == 0:
                            pe.wait_ge(vcopied, PRIMED + 3 * h + 3)
                        pe.wait_ge(ocopied, PRIMED + NU * h + u)
                        for b in range(batches[u]):
                            g0 = NB * h + bat0[u] + b
                            pe.wait_ge(tcopied, PRIMED + g0)
                            for w in range(4 * b, min(4 * b + 4, nk)):
                                kn = min(P, ln - w * P)
                                last = nc.tensor.transpose(pT[0:kn, (w % 4) * P:(w % 4) * P + qn],
                                                           pr[u % 2][0][0:qn, w * P:w * P + kn],
                                                           small("ident")[0:qn, 0:qn])
                            last.then_inc(turned, 1)
                        for w in range(nk):
                            kn = min(P, ln - w * P)
                            if w % 4 == 0:
                                pe.wait_ge(tcopied, PRIMED + NB * h + bat0[u] + w // 4 + 1)
                            last = mm(pO[:, 0:qn], vt[0:kn, v0 + w, :], amT[0:kn, w, 0:qn],
                                      start=(w == 0), stop=(w == nk - 1))
                        last.then_inc(outs, 1)

                    for u, (q0, qn, a, ln, v0) in enumerate(units):
                        for x in range(2):
                            pe.wait_ge(exped[x], PRIMED + NU * h + u)
                            rows = slice(x * HD, x * HD + HD)
                            for lo in range(0, ln, 512):
                                wd = min(512, ln - lo)
                                last = mm(pS[x][0:qn, lo // 512, 0:wd], q[rows, q0:q0 + qn],
                                          k[rows, a + lo:a + lo + wd], start=True, stop=True)
                            last.then_inc(scores[x], 1)
                        if u:
                            out_of(u - 1)
                    out_of(NU - 1)
                    pe.wait_ge(squared, PRIMED + 3 * h + 3)
                    pe.wait_ge(exped[0], PRIMED + NU * (h + 1))
                    pe.wait_ge(exped[1], PRIMED + NU * (h + 1))
                    over(small("ones"), sq, sums)

            @block.scalar
            def _(act):
                act.wait_ge(lamb, PRIMED + 1)
                nc.scalar.activation(lams[:, 0:2], lams[:, 0:2], ACT.Exp).then_inc(lamb, 1)
                with act.Fori(0, HEADS) as h:
                    act.wait_ge(loaded, PRIMED + 48 * h + 48)
                    for x, t in enumerate((q, k)):
                        act.wait_ge(normed, PRIMED + 2 * h + x)
                        nc.scalar.activation(sq[:, :], t[:, :], ACT.Square).then_inc(squared, 1)
                        act.wait_ge(meaned, PRIMED + 3 * h + x + 1)
                        nc.scalar.activation(sq[:, :], sq[:, :], ACT.Sqrt).then_inc(rooted, 1)

                    def out_of(u):
                        q0, qn, a, ln, v0 = units[u]
                        act.wait_ge(outs, PRIMED + NU * h + u + 1)
                        nc.scalar.copy(oT[:, q0:q0 + qn], pO[:, 0:qn]).then_inc(ocopied, 1)

                    for u, (q0, qn, a, ln, v0) in enumerate(units):
                        for x in range(2):
                            act.wait_ge(maxed[x], PRIMED + NU * h + u + 1)
                            if u >= 2:
                                act.wait_ge(turned, PRIMED + NB * h + bat0[u - 2] + batches[u - 2])
                            nc.scalar.activation(pr[u % 2][x][0:qn, 0:ln],
                                                 pS[x][:, :, :].rearrange("p a b -> p (a b)")[0:qn, 0:ln], ACT.Exp,
                                                 bias=st[0:qn, x, 1:2], scale=scale, accum_out=st[0:qn, x, 2:3]
                                                 ).then_inc(exped[x], 1)
                        if u:
                            out_of(u - 1)
                    out_of(NU - 1)
                    act.wait_ge(ocopied, PRIMED + NU * (h + 1))
                    nc.scalar.activation(sq[:, :], oT[:, :], ACT.Square).then_inc(squared, 1)
                    act.wait_ge(meaned, PRIMED + 3 * h + 3)
                    nc.scalar.activation(sq[:, :], sq[:, :], ACT.Sqrt).then_inc(rooted, 1)

            @block.vector
            def _(dve):
                LINKS = 3 + 4 + 3 * NU
                dve.wait_ge(consts, PRIMED + 64)
                pre = Chain(dve, chain)
                for x in range(2):
                    pre(nc.vector.tensor_tensor(lam[:, 2 * x * HD:(2 * x + 1) * HD], lam[:, 2 * x * HD:(2 * x + 1) * HD],
                                                lam[:, (2 * x + 1) * HD:(2 * x + 2) * HD], ALU.mult))
                    last = nc.vector.reduce_sum(lams[:, x:x + 1], lam[:, 2 * x * HD:(2 * x + 1) * HD], AX_X)
                    pre(last)
                pre(nc.vector.tensor_copy(lams[:, 3:4], lams[:, 0:1]))
                nc.vector.tensor_copy(lams[:, 2:3], lams[:, 1:2]).then_inc(lamb, 1)
                dve.wait_ge(lamb, PRIMED + 2)
                pre(nc.vector.tensor_tensor(lams[:, 2:3], lams[:, 1:2], lams[:, 0:1], ALU.subtract))
                pre(nc.vector.tensor_scalar(lams[:, 3:4], lams[:, 2:3], -LAMBDA_INIT, None, ALU.add))
                pre(nc.vector.tensor_scalar(sg[:, :], g.par_sb[:, PCOLS["subln_g"]:PCOLS["subln_g"] + 1],
                                            1.0 - LAMBDA_INIT, None, ALU.mult))
                PRE = pre.n
                with dve.Fori(0, HEADS) as h:
                    chained = Chain(dve, chain, h * LINKS + PRE)

                    def to_root(m, width, count):
                        dve.wait_ge(sums, PRIMED + 3 * h + count)
                        for n in range(NCH):
                            last = nc.vector.tensor_scalar(sq[:, n * CW:(n + 1) * CW], bank(n), 1.0 / width, 1e-6,
                                                           ALU.mult, ALU.add)
                        last.then_inc(meaned, 1)
                        dve.wait_ge(rooted, PRIMED + 3 * h + count)
                        chained(nc.vector.reciprocal(sq[:, :], sq[:, :]))

                    for b in range(NV // 4):
                        dve.wait_ge(vturned, PRIMED + 3 * h + b + 1)
                        dve.wait_ge(outs, PRIMED + NU * h)
                        for w in range(4):
                            tn = vtiles[4 * b + w][1]
                            last = nc.vector.tensor_copy(vt[0:tn, 4 * b + w, :], pT[0:tn, w * P:(w + 1) * P])
                        last.then_inc(vcopied, 1)
                    for x, (t, gain) in enumerate(((q, "q_norm_g"), (k, "k_norm_g"))):
                        to_root(t, HD, x + 1)
                        nc.vector.scalar_tensor_tensor(out=t[:, :], in0=t[:, :],
                                                       scalar=g.par_sb[:, PCOLS[gain]:PCOLS[gain] + 1], in1=sq[:, :],
                                                       op0=ALU.mult, op1=ALU.mult).then_inc(normed, 1)
                        dve.wait_ge(rotated, PRIMED + 2 * h + x + 1)
                        for n in range(NCH):
                            last = nc.vector.tensor_tensor(rot[:, n * CW:(n + 1) * CW], bank(n),
                                                           sin[:, n * CW:(n + 1) * CW], ALU.mult)
                        chained(last)
                        chained(nc.vector.tensor_tensor(t[:, :], t[:, :], cos[:, :], ALU.mult))
                        nc.vector.tensor_tensor(t[:, :], t[:, :], rot[:, :], ALU.add).then_inc(roped, 1)

                    def difference(u):
                        q0, qn, a, ln, v0 = units[u]
                        for x in range(2):
                            dve.wait_ge(exped[x], PRIMED + NU * h + u + 1)
                        chained(nc.vector.reciprocal(st[0:qn, :, 3:4], st[0:qn, :, 2:3]))
                        chained(nc.vector.tensor_tensor(st[0:qn, 1, 4:5], st[0:qn, 1, 3:4], lams[0:qn, 3:4], ALU.mult))
                        p0, p1 = pr[u % 2][0][0:qn, 0:ln], pr[u % 2][1][0:qn, 0:ln]
                        chained(nc.vector.tensor_scalar(p1, p1, st[0:qn, 1, 4:5], None, ALU.mult))
                        nc.vector.scalar_tensor_tensor(out=p0, in0=p0, scalar=st[0:qn, 0, 3:4], in1=p1,
                                                       op0=ALU.mult, op1=ALU.add).then_inc(diffed, 1)

                    def turn(u):
                        nk = -(-units[u][3] // P)
                        for b in range(batches[u]):
                            dve.wait_ge(turned, PRIMED + NB * h + bat0[u] + b + 1)
                            dve.wait_ge(outs, PRIMED + NU * h + u)
                            qn = units[u][1]
                            w0, w1 = 4 * b, min(4 * b + 4, nk)
                            full = [w for w in range(w0, w1) if units[u][3] - w * P >= P]
                            if full:
                                last = nc.vector.tensor_copy(amT[:, w0:w0 + len(full), 0:qn],
                                                             pT[:, :].rearrange("p (w t) -> p w t", w=4)[:, 0:len(full), 0:qn])
                            if len(full) < w1 - w0:
                                kn = units[u][3] - (w1 - 1) * P
                                last = nc.vector.tensor_copy(amT[0:kn, w1 - 1, 0:qn],
                                                             pT[0:kn, ((w1 - 1) % 4) * P:((w1 - 1) % 4) * P + qn])
                            last.then_inc(tcopied, 1)

                    for u, (q0, qn, a, ln, v0) in enumerate(units):
                        for x in range(2):
                            dve.wait_ge(scores[x], PRIMED + NU * h + u + 1)
                            last = nc.vector.reduce_max(st[0:qn, x, 0:1],
                                                        pS[x][:, :, :].rearrange("p a b -> p (a b)")[0:qn, 0:ln], AX_X)
                            last.then_inc(c_max[x], 1)
                            dve.wait_ge(c_max[x], PRIMED + NU * h + u + 1)
                            nc.vector.tensor_scalar(st[0:qn, x, 1:2], st[0:qn, x, 0:1], -scale, None, ALU.mult
                                                    ).then_inc(maxed[x], 1)
                        if u:
                            turn(u - 1)
                        difference(u)
                    turn(NU - 1)
                    to_root(oT, P, 3)
                    chained_o = nc.vector.scalar_tensor_tensor(out=oT[:, :], in0=oT[:, :], scalar=sg[:, 0:1],
                                                               in1=sq[:, :], op0=ALU.mult, op1=ALU.mult)
                    chained_o.then_inc(odone, 1)


def out_project(nc, g):
    with Ctx(nc, "op") as c:
        w = c.sb("w", (P, KT, D))
        ident = c.sb("ident", (P, P))
        m = [c.sb(f"m{s}", (P, KT, P)) for s in range(2)]
        x = [c.sb(f"x{s}", (P, D)) for s in range(2)]
        x1, sq, xn = c.sb("sum", (P, D)), c.sb("sq", (P, D)), c.sb("xn", (P, D))
        st = c.sb("st", (P, 4))
        acc = [c.ps(f"acc{s}", (P, 2, 512)) for s in range(2)]
        tp = c.ps("tp", (P, 2, 512))
        weights, stored = c.sem("weights"), c.sem("stored")
        loaded = [c.sem(f"loaded{s}") for s in range(2)]
        products = [c.sem(f"products{s}") for s in range(2)]
        added, squared, rooted, scaled = c.sem("added"), c.sem("squared"), c.sem("rooted"), c.sem("scaled")
        chain = [c.sem(f"chain{s}") for s in range(2)]
        turned, taken = c.sem("turned"), c.sem("taken")
        gain = cut(g.par_sb, PCOLS["ln2_g"], KT)
        PAIRS = TT // 2

        with nc.Block() as block:
            @block.sync
            def _(sp):
                c.prime(sp)
                sp.dma_start(w[:, :, :], g.w_out.rearrange("(k p) n -> p k n", p=P)).then_inc(weights, 16)
                sp.dma_start(ident[:, :], g.small_of("ident")).then_inc(weights, 16)

                def load(i, s, t):
                    sp.wait_ge(products[s], PRIMED + i)
                    sp.wait_ge(chain[s], PRIMED + 2 * i)
                    sp.dma_start(m[s][:, :, :], g.mix[:, ds(t * P, P)].rearrange("(k p) t -> p k t", p=P)
                                 ).then_inc(loaded[s], 16)
                    sp.dma_start(x[s][:, :], g.x[ds(t * P, P), :]).then_inc(loaded[s], 16)

                def store(t):
                    sp.wait_ge(added, PRIMED + t + 1)
                    sp.dma_start(g.x1[ds(t * P, P), :], x1[:, :]).then_inc(stored, 16)
                load(0, 0, 0)
                load(0, 1, 1)
                with sp.Fori(0, PAIRS - 1) as i:
                    for s in range(2):
                        store(2 * i + s)
                        load(i + 1, s, 2 * i + 2 + s)
                store(2 * PAIRS - 2)
                load(PAIRS, 0, 2 * PAIRS)
                store(2 * PAIRS - 1)
                store(2 * PAIRS)
                sp.wait_ge(stored, PRIMED + 16 * TT)

            @block.tensor
            def _(pe):
                pe.wait_ge(weights, PRIMED + 32)

                def product(i, s, t):
                    pe.wait_ge(loaded[s], PRIMED + 32 * i + 32)
                    pe.wait_ge(chain[s], PRIMED + 2 * i)
                    for b in range(2):
                        for k in range(KT):
                            last = nc.tensor.matmul(acc[s][:, b, :], m[s][:, k, :], w[:, k, b * 512:(b + 1) * 512],
                                                    start=(k == 0), stop=(k == KT - 1))
                    last.then_inc(products[s], 1)

                def turn(t):
                    pe.wait_ge(scaled, PRIMED + t + 1)
                    pe.wait_ge(taken, PRIMED + t)
                    for k in range(KT):
                        last = nc.tensor.transpose(tp[:, k // 4, (k % 4) * P:(k % 4 + 1) * P],
                                                   xn[:, k * P:(k + 1) * P], ident[:, :])
                    last.then_inc(turned, 1)
                product(0, 0, 0)
                with pe.Fori(0, PAIRS) as i:
                    product(i, 1, 2 * i + 1)
                    turn(2 * i)
                    product(i + 1, 0, 2 * i + 2)
                    turn(2 * i + 1)
                turn(2 * PAIRS)

            @block.scalar
            def _(act):
                def tile(i, s, t):
                    act.wait_ge(added, PRIMED + t + 1)
                    nc.scalar.activation(sq[:, :], x1[:, :], ACT.Square, accum_out=st[:, 0:1]).then_inc(squared, 1)
                    act.wait_ge(chain[s], PRIMED + 2 * i + 1)
                    nc.scalar.activation(st[:, 2:3], st[:, 1:2], ACT.Sqrt).then_inc(rooted, 1)
                with act.Fori(0, PAIRS) as i:
                    tile(i, 0, 2 * i)
                    tile(i, 1, 2 * i + 1)
                tile(PAIRS, 0, 2 * PAIRS)

            @block.vector
            def _(dve):
                def tile(i, s, t):
                    chained = Chain(dve, chain[s], 2 * i)
                    dve.wait_ge(products[s], PRIMED + i + 1)
                    dve.wait_ge(stored, PRIMED + 16 * t)
                    nc.vector.tensor_tensor(x1[:, :].rearrange("p (b n) -> p b n", b=2), acc[s][:, :, :],
                                            x[s][:, :].rearrange("p (b n) -> p b n", b=2), ALU.add
                                            ).then_inc(added, 1)
                    dve.wait_ge(squared, PRIMED + t + 1)
                    nc.vector.tensor_scalar(st[:, 1:2], st[:, 0:1], 1.0 / D, 1e-6, ALU.mult, ALU.add
                                            ).then_inc(chain[s], 1)
                    chained.n += 1
                    dve.wait_ge(rooted, PRIMED + t + 1)
                    chained(nc.vector.reciprocal(st[:, 3:4], st[:, 2:3]))
                    dve.wait_ge(turned, PRIMED + t)
                    nc.vector.tensor_scalar(xn[:, :], x1[:, :], st[:, 3:4], None, ALU.mult).then_inc(scaled, 1)
                    dve.wait_ge(turned, PRIMED + t + 1)
                    nc.vector.tensor_tensor(g.nT[:, :, ds(t * P, P)].rearrange("p (b k) t -> p b k t", b=2),
                                            tp[:, :, :].rearrange("p b (k t) -> p b k t", k=4),
                                            gain.rearrange("p (b k) -> p b k", b=2).unsqueeze(3).to_broadcast([P, 2, 4, P]),
                                            ALU.mult).then_inc(taken, 1)
                with dve.Fori(0, PAIRS) as i:
                    tile(i, 0, 2 * i)
                    tile(i, 1, 2 * i + 1)
                tile(PAIRS, 0, 2 * PAIRS)


def ffn_up(nc, g):
    with Ctx(nc, "fu") as c:
        wg = [c.sb(f"wg{s}", (P, KT, P)) for s in range(2)]
        wu = [c.sb(f"wu{s}", (P, KT, P)) for s in range(2)]
        gate = c.sb("gate", (P, TOK))
        pg = [c.ps(f"pg{n}") for n in range(NCH)]
        pu = [c.ps(f"pu{n}") for n in range(NCH)]
        loaded = [c.sem(f"loaded{s}") for s in range(2)]
        gated, silued, done = c.sem("gated"), c.sem("silued"), c.sem("done")
        upped = [c.sem(f"upped{s}") for s in range(2)]
        STEPS = FFT // 2
        with nc.Block() as block:
            @block.sync
            def _(sp):
                c.prime(sp)
                with sp.Fori(0, STEPS) as i:
                    for s in range(2):
                        sp.wait_ge(upped[s], PRIMED + NCH * i)
                        for t, src in ((wg[s], g.w_gate), (wu[s], g.w_up)):
                            sp.dma_start(t[:, :, :], src[ds(2 * i + s, 1)].rearrange("a p k n -> (a p) k n")
                                         ).then_inc(loaded[s], 16)

            @block.tensor
            def _(pe):
                with pe.Fori(0, STEPS) as i:
                    for s in range(2):
                        pe.wait_ge(loaded[s], PRIMED + 32 * i + 32)
                        m = 2 * i + s
                        for n in range(NCH):
                            pe.wait_ge(done, PRIMED + NCH * m)
                            for ps, w, sem in ((pg, wg, gated), (pu, wu, upped[s])):
                                for k in range(KT):
                                    last = nc.tensor.matmul(ps[n][:, 0:CW], w[s][:, k, :],
                                                            g.nT[:, k, n * CW:(n + 1) * CW],
                                                            start=(k == 0), stop=(k == KT - 1))
                                last.then_inc(sem, 1)

            @block.scalar
            def _(act):
                with act.Fori(0, FFT) as m:
                    act.wait_ge(done, PRIMED + NCH * m)
                    for n in range(NCH):
                        act.wait_ge(gated, PRIMED + NCH * m + n + 1)
                        nc.scalar.activation(gate[:, n * CW:(n + 1) * CW], pg[n][:, 0:CW], ACT.Silu
                                             ).then_inc(silued, 1)

            @block.vector
            def _(dve):
                with dve.Fori(0, STEPS) as i:
                    for s, n in [(s, n) for s in range(2) for n in range(NCH)]:
                        m = 2 * i + s
                        dve.wait_ge(silued, PRIMED + NCH * m + n + 1)
                        dve.wait_ge(upped[s], PRIMED + NCH * i + n + 1)
                        nc.vector.tensor_tensor(g.hT[:, ds(m, 1), n * CW:(n + 1) * CW].rearrange("p a t -> p (a t)"),
                                                pu[n][:, 0:CW], gate[:, n * CW:(n + 1) * CW], ALU.mult).then_inc(done, 1)


def ffn_down(nc, g):
    with Ctx(nc, "fd") as c:
        w = [c.sb(f"w{s}", (P, FFT, P)) for s in range(2)]
        x1, out = c.sb("x1", (P, TT, P)), c.sb("out", (P, TT, P))
        yT = c.sb("yT", (P, TT * P))
        ident = c.sb("ident", (P, P))
        acc = [c.ps(f"acc{n}") for n in range(NCH)]
        tp = c.ps("tp", (P, 3, 512))
        loaded = [c.sem(f"loaded{s}") for s in range(2)]
        consts, rows, copied = c.sem("consts"), c.sem("rows"), c.sem("copied")
        turned, added, stored, zeroed = c.sem("turned"), c.sem("added"), c.sem("stored"), c.sem("zeroed")
        products = [c.sem(f"products{s}") for s in range(2)]
        STEPS = KT // 2
        PIECES = [(META, P - META, 0, 1, 0, 0), (0, P, 1, 1, 0, P - META), (0, META, 2, 1, 0, 2 * P - META),
                  (32, P - 32, 2, 1, 1, 0), (0, P, 3, 7, 1, 96), (0, 32, 10, 1, 1, 992)]
        with nc.Block() as block:
            @block.sync
            def _(sp):
                c.prime(sp)
                sp.dma_start(ident[:, :], g.small_of("ident")).then_inc(consts, 16)

                def weights(i, s):
                    sp.wait_ge(products[s], PRIMED + NCH * i)
                    sp.dma_start(w[s][:, :, :], g.w_down[ds(2 * i + s, 1)].rearrange("a p k n -> (a p) k n")
                                 ).then_inc(loaded[s], 16)

                def residual(m):
                    sp.wait_ge(added, PRIMED + m)
                    sp.dma_start(x1[:, :, :], g.x1[:, ds(m * P, P)].rearrange("(t p) n -> p t n", p=P)
                                 ).then_inc(rows, 16)

                def store(m):
                    sp.wait_ge(added, PRIMED + m + 1)
                    for p0, pn, t0, tn, o, r0 in PIECES:
                        dst = g.out[o][0, r0:r0 + pn * tn, ds(m * P, P)]
                        sp.dma_start(dst.rearrange("(t p) n -> p t n", t=tn), out[p0:p0 + pn, t0:t0 + tn, :]
                                     ).then_inc(stored, 16)
                weights(0, 0)
                weights(0, 1)
                residual(0)
                with sp.Fori(0, STEPS - 1) as i:
                    for s in range(2):
                        residual(2 * i + s + 1)
                        weights(i + 1, s)
                        store(2 * i + s)
                residual(KT - 1)
                store(KT - 2)
                store(KT - 1)
                sp.wait_ge(stored, PRIMED + 16 * len(PIECES) * KT)

            @block.tensor
            def _(pe):
                pe.wait_ge(consts, PRIMED + 16)
                pe.wait_ge(zeroed, PRIMED + 1)
                with pe.Fori(0, STEPS) as i:
                    for s in range(2):
                        m = 2 * i + s
                        pe.wait_ge(loaded[s], PRIMED + 16 * i + 16)
                        pe.wait_ge(copied, PRIMED + NCH * m)
                        for n in range(NCH):
                            for k in range(FFT):
                                last = nc.tensor.matmul(acc[n][:, 0:CW], w[s][:, k, :], g.hT[:, k, n * CW:(n + 1) * CW],
                                                        start=(k == 0), stop=(k == FFT - 1))
                            last.then_inc(products[s], 1)
                        pe.wait_ge(copied, PRIMED + NCH * m + NCH)
                        pe.wait_ge(added, PRIMED + m)
                        for t in range(TT):
                            last = nc.tensor.transpose(tp[:, t // 4, (t % 4) * P:(t % 4 + 1) * P],
                                                       yT[:, t * P:(t + 1) * P], ident[:, :])
                        last.then_inc(turned, 1)

            @block.scalar
            def _(act):
                with act.Fori(0, STEPS) as i:
                    for s, n in [(s, n) for s in range(2) for n in range(NCH)]:
                        act.wait_ge(turned, PRIMED + 2 * i + s)
                        act.wait_ge(products[s], PRIMED + NCH * i + n + 1)
                        nc.scalar.copy(yT[:, n * CW:(n + 1) * CW], acc[n][:, 0:CW]).then_inc(copied, 1)

            @block.vector
            def _(dve):
                nc.vector.memset(yT[:, TOK:TT * P], 0.0).then_inc(zeroed, 1)
                with dve.Fori(0, KT) as m:
                    dve.wait_ge(turned, PRIMED + m + 1)
                    dve.wait_ge(rows, PRIMED + 16 * m + 16)
                    dve.wait_ge(stored, PRIMED + 16 * len(PIECES) * m)
                    nc.vector.tensor_tensor(out[:, :, :].rearrange("p t n -> p (t n)"),
                                            tp[:, :, :].rearrange("p b n -> p (b n)")[:, 0:TT * P],
                                            x1[:, :, :].rearrange("p t n -> p (t n)"), ALU.add).then_inc(added, 1)


class Tensors:

    def __init__(self, dram, out):
        self.out = out
        self.x = dram["x"]
        self.par = dram["par"]
        self.w_in = dram["w_in"]
        self.lora1 = dram["lora1"]
        self.lora2 = dram["lora2"]
        self.gate2 = dram["gate2"]
        self.lambdas = dram["lambdas"]
        self.w_out = dram["w_out"]
        self.w_gate = dram["w_gate"]
        self.w_up = dram["w_up"]
        self.w_down = dram["w_down"]
        self.small = dram["small"]
        self.cos = dram["cos"]
        self.sin = dram["sin"]
        self.first = dram["first"]
        self.keep = dram["keep"]

    def small_of(self, name):
        lo, wd = SCOLS[name]
        return self.small[:, lo:lo + wd]


def encoder(nc, g):
    scratch = lambda name, shape: nc.dram_tensor(f"dram_{name}", list(shape), F32, kind=SCRATCH_KIND).ap()
    g.proj = scratch("proj", (3072, TOK))
    g.sx = scratch("sx", (2, FT, P, CHUNKS * 5 * CH))
    g.bonus = scratch("bonus", (RW, PTOK))
    g.ydir = scratch("ydir", (2, FT, P, PTOK))
    g.mix = scratch("mix", (D, TT * P))
    g.x1 = scratch("x1", (TT * P, D))

    with Ctx(nc, "all") as whole:
        g.par_sb = whole.sb("par", (P, NPAR))
        with Ctx(nc, "mixer") as mixer:
            g.etot = mixer.sb("etot", (P, 2, FT, CHUNKS))
            g.hidg = mixer.sb("hidg", (P, 2, PTOK))
            with Ctx(nc, "lora") as lora:
                g.hid = lora.sb("hid", (HD, 4, PTOK))
                with Ctx(nc, "n") as norm:
                    g.nT = norm.sb("nT", (P, KT, TT * P))
                    norm_in(nc, g)
                    project(nc, g)
                    lora_in(nc, g)
                prep(nc, g)
            chunks(nc, g)
            mix_out(nc, g)
        attention(nc, g)
        g.nT = whole.sb("n2T", (P, KT, TT * P))
        out_project(nc, g)
        g.hT = whole.sb("hT", (P, FFT, TOK))
        ffn_up(nc, g)
        ffn_down(nc, g)


def laid_out(inputs):
    a = {n: np.asarray(v) for n, v in inputs.items()}
    cat = np.concatenate
    meta = a["meta_tokens"]
    x = cat([meta, a["x_prompt"][0], meta, a["x_sample"][0], np.zeros((TT * P - TOK, D), np.float32)])
    column = lambda v: v.reshape(-1, P).T
    rows = [column(a["ln1_g"][0]), column(a["ln2_g"][0])]
    rows += [column(a["conv_rkv"][0, n]) for n in range(3)]
    for name in ("mix_w", "mix_a"):
        rows += [column(a[name][0, d]) for d in range(2)]
    rows.append(column(a["mix_g"][0]))
    for name in ("decay_w0", "aaa_a0"):
        rows += [column(a[name][0, d]) for d in range(2)]
    rows += [column(a[name][0].reshape(-1)) for name in ("k_k", "k_a", "r_k", "lnx_g", "lnx_b")]
    rows += [cat([a[name][0]] * 2)[:, None] for name in ("q_norm_g", "k_norm_g")]
    rows.append(a["subln_g"][0][:, None])
    tiles = lambda w: np.ascontiguousarray(w.reshape(w.shape[0] // P, P, w.shape[1] // P, P).transpose(2, 1, 0, 3))
    by_row = lambda w: w.reshape(KT, P, w.shape[1]).transpose(1, 0, 2)
    lora1 = cat([by_row(a["decay_w1"][0, 0]), by_row(a["aaa_a1"][0, 0]), by_row(a["decay_w1"][0, 1]),
                 by_row(a["aaa_a1"][0, 1]), by_row(a["gate_g1"][0])], axis=2)
    second = np.stack([a["decay_w2"][0, 0], a["aaa_a2"][0, 0], a["decay_w2"][0, 1], a["aaa_a2"][0, 1]])
    lora2 = second.reshape(4, HD, FT, P).transpose(2, 1, 0, 3)
    arrays = {
        "x": x, "par": cat(rows, axis=1), "w_in": tiles(a["w_in"][0]), "lora1": lora1, "lora2": lora2,
        "gate2": a["gate_g2"][0], "lambdas": a["diff_lambdas"][0].reshape(-1), "w_out": a["w_out"][0],
        "w_gate": tiles(a["w_gate"][0]), "w_up": tiles(a["w_up"][0]), "w_down": tiles(a["w_down"][0]),
        "small": SMALL_ARRAY, **WIDE,
    }
    return {n: np.ascontiguousarray(v) for n, v in arrays.items()}


def kernel(**inputs):
    import concourse.bacc as _bacc
    from concourse.bass_utils import run_bass_kernel_spmd as _run

    nc = _bacc.Bacc("TRN2", target_bir_lowering=False, num_devices=1)
    arrays = laid_out(inputs)
    dram = {n: nc.dram_tensor(f"in_{n}", a.shape, F32, kind="ExternalInput").ap() for n, a in arrays.items()}
    out = [nc.dram_tensor(f"out_{n}", (1, rows, D), F32, kind="ExternalOutput").ap()
           for n, rows in enumerate((LEN_A - META, LEN_B - META))]
    encoder(nc, Tensors(dram, out))
    r = _run(nc, [{f"in_{n}": a for n, a in arrays.items()}], core_ids=[0])
    return tuple(r.results[0][f"out_{n}"] for n in range(2))
```

```python
import math
from contextlib import ExitStack

import numpy as np

import concourse.bass as bass
from concourse import mybir
from concourse.alu_op_type import AluOpType as ALU

F32 = mybir.dt.float32
ACT = mybir.ActivationFunctionType
AX_X = mybir.AxisListType.X
ds = bass.ds

P = 128
D = 1024
META = 16
LEN_A, LEN_B = META + 256, META + 1024
TOK = LEN_A + LEN_B
KT = D // P
NCH = 4
CW = TOK // NCH
CH = 64
CH_A, CH_B = -(-LEN_A // CH), -(-LEN_B // CH)
CHUNKS = CH_A + CH_B
PAD_B = CH_A * CH
PTOK = CHUNKS * CH
PW = PTOK // NCH
TT = -(-TOK // P)
RW = 512
FT = RW // P
HEADS = 4
HD = 64
FF = 2816
FFT = FF // P
GL = 160
DECAY = math.exp(-0.5)
LAMBDA_INIT = 0.8 - 0.6 * math.exp(-0.3 * 0)
LEVELS = 5
SEQS = ((0, LEN_A, 0), (LEN_A, LEN_B, PAD_B))

VTILES = [(a + t, min(P, ln - t)) for a, ln, _p in SEQS for t in range(0, ln, P)]
assert [n for _t, n in VTILES] == [P] * 2 + [LEN_A % P] + [P] * 8 + [LEN_B % P]
VRUNS = [(0, 2, P), (2, 3, LEN_A % P), (3, 11, P), (11, 12, LEN_B % P)]

PCOLS = {}
_at = 0
for _name, _n in (("ln1_g", 8), ("ln2_g", 8), ("conv", 36), ("mix_w", 16), ("mix_a", 16), ("mix_g", 8),
                  ("decay_w0", 8), ("aaa_a0", 8), ("k_k", 4), ("k_a", 4), ("r_k", 4), ("lnx_g", 4),
                  ("lnx_b", 4), ("q_norm_g", 1), ("k_norm_g", 1), ("subln_g", 1)):
    PCOLS[_name] = _at
    _at += _n
NPAR = _at


def shape_constants():
    row = np.arange(P)
    h, s = row // CH, row % CH
    t = np.arange(CH)
    eye = np.eye(P, dtype=np.float32)
    block = (row[:, None] // HD == row[None, :] // HD).astype(np.float32)
    out = {"ident": eye, "heads": block,
           "ones": np.ones((P, P), np.float32)}
    own = (h[:, None, None] == np.arange(2)[None, :, None])
    bd = lambda m: (own & m[:, None, :]).reshape(P, P).astype(np.float32)
    for d in range(2):
        before = s[:, None] < t[None, :] if d == 0 else s[:, None] > t[None, :]
        after = s[:, None] > t[None, :] if d == 0 else s[:, None] < t[None, :]
        same = s[:, None] == t[None, :]
        out[f"incl{d}"] = (before | same).astype(np.float32)
        out[f"strict_bd{d}"] = bd(before)
        out[f"after_bd{d}"] = bd(after)
        lev = lambda z: (s[:, None] // (2 * z) == t[None, :] // (2 * z)) & (s[:, None] // z != t[None, :] // z)
        out[f"pair_bd{d}"] = bd(lev(1) & before)
        out[f"pairT_bd{d}"] = bd((lev(1) & after) | same)
        for n in range(LEVELS):
            out[f"lev{n}_bd{d}"] = bd((lev(2 << n) & before) | same)
    swap = np.zeros((P, P), np.float32)
    for c in range(2):
        for i in range(8):
            swap[c * HD + 8 + i, c * HD + i] = -1.0
            swap[c * HD + i, c * HD + 8 + i] = 1.0
    out["swap"] = swap
    freqs = (np.float32(500000.0) ** (-np.arange(0, 16, 2, dtype=np.float32) / np.float32(16))).astype(np.float32)
    pos = np.concatenate([np.arange(LEN_A), np.arange(LEN_B)]).astype(np.float32)
    ang = (pos[None, :] * freqs[:, None]).astype(np.float32)
    cos, sin = np.ones((P, TOK), np.float32), np.zeros((P, TOK), np.float32)
    for c in range(2):
        for k in range(2):
            r = c * HD + 8 * k
            cos[r:r + 8], sin[r:r + 8] = np.cos(ang), np.sin(ang)
    first = np.ones((P, CHUNKS, CH), np.float32)
    first[:, :, 0] = 0
    keep = np.ones((P, 2, CHUNKS), np.float32)
    keep[:, 0, [CH_A - 1, CHUNKS - 1]] = 0
    keep[:, 1, [0, CH_A]] = 0
    wide = {"cos": cos, "sin": sin, "first": first.reshape(P, PTOK), "keep": keep.reshape(P, 2 * CHUNKS)}
    return out, wide


SMALL, WIDE = shape_constants()
SCOLS, _at = {}, 0
for _name, _a in SMALL.items():
    SCOLS[_name] = (_at, _a.shape[1])
    _at += _a.shape[1]
NSMALL = _at
SMALL_ARRAY = np.concatenate(list(SMALL.values()), axis=1)
SCRATCH_KIND = "Internal"
PRIMED = 2


class Ctx(ExitStack):

    def __init__(self, nc, stage):
        super().__init__()
        self.nc, self.stage, self.sems = nc, stage, []

    def sb(self, name, shape):
        return self.enter_context(self.nc.sbuf_tensor(f"{self.stage}_{name}", list(shape), F32))

    def ps(self, name, shape=(P, 512)):
        return self.enter_context(self.nc.psum_tensor(f"{self.stage}_{name}", list(shape), F32))

    def sem(self, name):
        self.sems.append(self.nc.alloc_semaphore(name=f"{self.stage}_{name}"))
        return self.sems[-1]

    def reset(self):
        self.nc.clear_and_free_semaphores(self.sems)
        self.nc.all_engine_barrier()
        self.sems = []

    def prime(self, eng):
        for sem in self.sems:
            eng.sem_inc(sem, PRIMED)


class Chain:

    def __init__(self, eng, sem, base=0):
        self.eng, self.sem, self.base, self.n = eng, sem, base, 0

    def __call__(self, ins):
        self.n += 1
        ins.then_inc(self.sem, 1)
        self.eng.wait_ge(self.sem, PRIMED + self.base + self.n)


def wide(ap, axis, shape):
    return ap.unsqueeze(axis).to_broadcast(list(shape))


def cut(t, lo, n):
    return t[:, lo:lo + n]


def norm_in(nc, g):
    with Ctx(nc, "n1") as c:
        x = c.sb("x", (P, TT, D))
        sq = c.sb("sq", (P, D))
        xn = c.sb("xn", (P, D))
        ss = c.sb("ss", (P, TT))
        rms = c.sb("rms", (P, TT))
        rstd = c.sb("rstd", (P, TT))
        small = c.sb("ident", (P, P))
        tp = [c.ps("tpa"), c.ps("tpb")]
        loaded, squared, rooted, chain = c.sem("loaded"), c.sem("squared"), c.sem("rooted"), c.sem("chain")
        scaled, turned, taken = c.sem("scaled"), c.sem("turned"), c.sem("taken")
        c.callback(c.reset)
        with nc.Block() as block:
            @block.sync
            def _(sp):
                c.prime(sp)
                sp.dma_start(x[:, :, :], g.x.rearrange("(t p) d -> p t d", p=P)).then_inc(loaded, 16)
                sp.dma_start(small[:, :], g.small[:, 0:P]).then_inc(loaded, 16)
                sp.dma_start(g.par_sb[:, :], g.par).then_inc(loaded, 16)

            @block.scalar
            def _(act):
                act.wait_ge(loaded, PRIMED + 48)
                chained = Chain(act, chain)
                for t in range(TT):
                    chained(nc.scalar.activation(sq[:, :], x[:, t, :], ACT.Square, accum_out=ss[:, t:t + 1]))
                nc.scalar.copy(sq[:, 0:1], ss[:, 0:1]).then_inc(squared, 1)
                act.wait_ge(squared, PRIMED + 2)
                nc.scalar.activation(rms[:, :], rstd[:, :], ACT.Sqrt).then_inc(rooted, 1)

            @block.vector
            def _(dve):
                dve.wait_ge(squared, PRIMED + 1)
                nc.vector.tensor_scalar(rstd[:, :], ss[:, :], 1.0 / D, 1e-6, ALU.mult, ALU.add).then_inc(squared, 1)
                dve.wait_ge(rooted, PRIMED + 1)
                nc.vector.reciprocal(rstd[:, :], rms[:, :]).then_inc(rooted, 1)
                dve.wait_ge(rooted, PRIMED + 2)
                gain = cut(g.par_sb, PCOLS["ln1_g"], KT)
                with dve.Fori(0, TT) as i:
                    dve.wait_ge(turned, PRIMED + i)
                    nc.vector.tensor_scalar(xn[:, :], x[:, ds(i, 1), :].rearrange("p a d -> p (a d)"),
                                            rstd[:, ds(i, 1)], None, ALU.mult).then_inc(scaled, 1)
                    dve.wait_ge(turned, PRIMED + i + 1)
                    for b in range(2):
                        last = nc.vector.tensor_tensor(
                            g.nT[:, 4 * b:4 * b + 4, ds(i * P, P)],
                            tp[b][:, :].rearrange("p (k t) -> p k t", k=4),
                            wide(gain[:, 4 * b:4 * b + 4], 2, (P, 4, P)), ALU.mult)
                    last.then_inc(taken, 1)

            @block.tensor
            def _(pe):
                with pe.Fori(0, TT) as i:
                    pe.wait_ge(scaled, PRIMED + i + 1)
                    pe.wait_ge(taken, PRIMED + i)
                    for k in range(KT):
                        last = nc.tensor.transpose(tp[k // 4][:, (k % 4) * P:(k % 4 + 1) * P],
                                                   xn[:, k * P:(k + 1) * P], small[:, :])
                    last.then_inc(turned, 1)


def project(nc, g):
    MT = 3072 // P
    CONV = 3 * FT
    with Ctx(nc, "pj") as c:
        w = [c.sb(f"w{s}", (P, KT, P)) for s in range(2)]
        raw = [c.sb(f"raw{s}", (P, TOK)) for s in range(2)]
        mixed = [c.sb(f"mixed{s}", (P, TOK)) for s in range(2)]
        acc = [[c.ps(f"acc{s}{n}") for n in range(NCH)] for s in range(2)]
        w_in = [c.sem(f"w_in{s}") for s in range(2)]
        done = [c.sem(f"done{s}") for s in range(2)]
        copied = [c.sem(f"copied{s}") for s in range(2)]
        conved = [c.sem(f"conved{s}") for s in range(2)]
        stored = [c.sem(f"stored{s}") for s in range(2)]
        chain = c.sem("chain")
        STEPS = MT // 2
        c.callback(c.reset)
        with nc.Block() as block:
            @block.sync
            def _(sp):
                c.prime(sp)
                def load(i, s):
                    sp.wait_ge(done[s], PRIMED + NCH * i)
                    sp.dma_start(w[s][:, :, :], g.w_in[ds(2 * i + s, 1)].rearrange("a p k n -> (a p) k n")
                                 ).then_inc(w_in[s], 16)

                def store(i, s, conv):
                    if conv:
                        sp.wait_ge(conved[s], PRIMED + i + 1)
                    else:
                        sp.wait_ge(copied[s], PRIMED + NCH * i + NCH)
                    sp.dma_start(g.proj[ds((2 * i + s) * P, P), :], (mixed if conv else raw)[s][:, :]
                                 ).then_inc(stored[s], 16)
                for s in range(2):
                    load(0, s)
                for conv, lo, hi in ((True, 0, CONV // 2), (False, CONV // 2, STEPS - 1)):
                    with sp.Fori(lo, hi) as i:
                        for s in range(2):
                            load(i + 1, s)
                            store(i, s, conv)
                for s in range(2):
                    store(STEPS - 1, s, False)
                for s in range(2):
                    sp.wait_ge(stored[s], PRIMED + 16 * STEPS)

            @block.tensor
            def _(pe):
                with pe.Fori(0, STEPS) as i:
                    for s in range(2):
                        pe.wait_ge(w_in[s], PRIMED + 16 * i + 16)
                        for n in range(NCH):
                            pe.wait_ge(copied[s], PRIMED + NCH * i)
                            for k in range(KT):
                                last = nc.tensor.matmul(acc[s][n][:, 0:CW], w[s][:, k, :],
                                                        g.nT[:, k, n * CW:(n + 1) * CW],
                                                        start=(k == 0), stop=(k == KT - 1))
                            last.then_inc(done[s], 1)

            @block.scalar
            def _(act):
                with act.Fori(0, STEPS) as i:
                    for s in range(2):
                        act.wait_ge(stored[s], PRIMED + 16 * i)
                        for n in range(NCH):
                            act.wait_ge(done[s], PRIMED + NCH * i + n + 1)
                            nc.scalar.copy(raw[s][:, n * CW:(n + 1) * CW], acc[s][n][:, 0:CW]
                                           ).then_inc(copied[s], 1)

            @block.vector
            def _(dve):
                with dve.Fori(0, CONV // 2) as i:
                    chained = Chain(dve, chain, i * 6)
                    for s in range(2):
                        dve.wait_ge(copied[s], PRIMED + NCH * i + NCH)
                        dve.wait_ge(stored[s], PRIMED + 16 * i)
                        tap = lambda n: g.par_sb[:, ds(PCOLS["conv"] + n * CONV + 2 * i + s, 1)]
                        chained(nc.vector.tensor_scalar(mixed[s][:, :], raw[s][:, :], tap(1), None, ALU.mult))
                        for lo, ln, _p in SEQS:
                            last = nc.vector.scalar_tensor_tensor(
                                out=mixed[s][:, lo + 1:lo + ln], in0=raw[s][:, lo:lo + ln - 1], scalar=tap(0),
                                in1=mixed[s][:, lo + 1:lo + ln], op0=ALU.mult, op1=ALU.add)
                            if lo == 0:
                                chained(last)
                        chained(last)
                        for lo, ln, _p in SEQS:
                            last = nc.vector.scalar_tensor_tensor(
                                out=mixed[s][:, lo:lo + ln - 1], in0=raw[s][:, lo + 1:lo + ln], scalar=tap(2),
                                in1=mixed[s][:, lo:lo + ln - 1], op0=ALU.mult, op1=ALU.add)
                        last.then_inc(conved[s], 1)


def lora_in(nc, g):
    CASES = [("mix_w", 0), ("mix_a", 0), ("mix_w", 1), ("mix_a", 1), ("mix_g", 0)]
    with Ctx(nc, "lo") as c:
        delta = c.sb("delta", (P, KT, TOK))
        mixed = [c.sb(f"mixed{s}", (P, TOK)) for s in range(2)]
        w = c.sb("w", (P, KT, 4 * HD + GL))
        acc = [c.ps(f"acc{n}") for n in range(NCH)]
        acc2 = [c.ps(f"acc2{n}") for n in range(NCH)]
        loaded, mixed_s, copied, chain = c.sem("loaded"), c.sem("mixed_s"), c.sem("copied"), c.sem("chain")
        zeroed, stored = c.sem("zeroed"), c.sem("stored")
        hidg = c.sb("hidg", (P, 2, PTOK))
        used = [c.sem(f"used{s}") for s in range(2)]
        cols = [(0, HD), (HD, HD), (2 * HD, HD), (3 * HD, HD), (4 * HD, GL)]
        c.callback(c.reset)
        with nc.Block() as block:
            @block.sync
            def _(sp):
                c.prime(sp)
                sp.dma_start(w[:, :, :], g.lora1).then_inc(loaded, 16)
                sp.wait_ge(copied, PRIMED + 5)
                sp.wait_ge(zeroed, PRIMED + 2)
                sp.dma_start(g.hidg_dram[:, 0, :], hidg[:, 0, :]).then_inc(stored, 16)
                sp.dma_start(g.hidg_dram[0:GL - P, 1, :], hidg[0:GL - P, 1, :]).then_inc(stored, 16)
                sp.wait_ge(stored, PRIMED + 32)

            @block.gpsimd
            def _(pool):
                for t in (g.hid, hidg):
                    nc.gpsimd.memset(t[:, :, LEN_A:PAD_B], 0.0)
                    nc.gpsimd.memset(t[:, :, PAD_B + LEN_B:PTOK], 0.0).then_inc(zeroed, 1)

            @block.vector
            def _(dve):
                chained = Chain(dve, chain)
                nT = g.nT
                for lo, ln, _p in SEQS:
                    hi = lo + ln
                    nc.vector.tensor_tensor(delta[:, :, lo + 1:hi - 1], nT[:, :, lo:hi - 2], nT[:, :, lo + 2:hi],
                                            ALU.add)
                    nc.vector.tensor_copy(delta[:, :, lo:lo + 1], nT[:, :, lo + 1:lo + 2])
                    chained(nc.vector.tensor_copy(delta[:, :, hi - 1:hi], nT[:, :, hi - 2:hi - 1]))
                for k in range(KT):
                    last = nc.vector.scalar_tensor_tensor(out=delta[:, k, :], in0=delta[:, k, :], scalar=0.5,
                                                          in1=nT[:, k, 0:TOK], op0=ALU.mult, op1=ALU.subtract)
                    if k == 0:
                        chained(last)
                chained(last)
                for m, (mix, d) in enumerate(CASES):
                    with dve.Fori(0, KT // 2) as i:
                        for s in range(2):
                            dve.wait_ge(used[s], PRIMED + m * (KT // 2) + i)
                            nc.vector.scalar_tensor_tensor(
                                out=mixed[s][:, :], in0=delta[:, ds(2 * i + s, 1), :].rearrange("p a t -> p (a t)"),
                                scalar=g.par_sb[:, ds(PCOLS[mix] + d * KT + 2 * i + s, 1)],
                                in1=nT[:, ds(2 * i + s, 1), 0:TOK].rearrange("p a t -> p (a t)"),
                                op0=ALU.mult, op1=ALU.add).then_inc(mixed_s, 1)

            @block.tensor
            def _(pe):
                pe.wait_ge(loaded, PRIMED + 16)
                for m, (_mix, _d) in enumerate(CASES):
                    lo, wd = cols[m]
                    if m:
                        pe.wait_ge(copied, PRIMED + m)
                    for k in range(KT):
                        pe.wait_ge(mixed_s, PRIMED + m * KT + k + 1)
                        for n in range(NCH):
                            for a, (off, rows) in enumerate(((0, min(wd, P)), (P, wd - P))):
                                if rows <= 0:
                                    continue
                                last = nc.tensor.matmul((acc, acc2)[a][n][0:rows, 0:CW],
                                                        w[:, k, lo + off:lo + off + rows],
                                                        mixed[k % 2][:, n * CW:(n + 1) * CW],
                                                        start=(k == 0), stop=(k == KT - 1))
                        last.then_inc(used[k % 2], 1)

            @block.scalar
            def _(act):
                for m, (_mix, _d) in enumerate(CASES):
                    act.wait_ge(used[1], PRIMED + (m + 1) * (KT // 2))
                    wd = cols[m][1]
                    func = (ACT.Tanh, ACT.Copy, ACT.Tanh, ACT.Copy, ACT.Sigmoid)[m]
                    parts = [(g.hid[:, m, :], acc, HD)] if m < 4 else [(hidg[:, 0, :], acc, P),
                                                                       (hidg[0:GL - P, 1, :], acc2, GL - P)]
                    for dst, ps, rows in parts:
                        for n in range(NCH):
                            lo = n * CW
                            for a, ln, p in SEQS:
                                x0, x1 = max(lo, a), min(lo + CW, a + ln)
                                if x0 < x1:
                                    last = nc.scalar.activation(dst[:, p + x0 - a:p + x1 - a],
                                                                ps[n][0:rows, x0 - lo:x1 - lo], func)
                    last.then_inc(copied, 1)


def prep(nc, g):
    with Ctx(nc, "pr") as c:
        r, k, v = c.sb("r", (P, PTOK)), c.sb("k", (P, PTOK)), c.sb("v", (P, PTOK))
        w2 = c.sb("w2", (HD, 4, P))
        heads = c.sb("heads", (P, P))
        first = c.sb("first", (P, PTOK))
        keep = c.sb("keep", (P, 2, CHUNKS))
        q, kk, kds = c.sb("q", (P, PTOK)), c.sb("kk", (P, PTOK)), c.sb("kds", (P, PTOK))
        sg = [c.sb(f"sg{d}", (P, PTOK)) for d in range(2)]
        av = [c.sb(f"av{d}", (P, PTOK)) for d in range(2)]
        cs = [c.sb(f"cs{d}", (P, PTOK)) for d in range(2)]
        ex = [c.sb(f"ex{d}", (P, PTOK)) for d in range(2)]
        kd = [c.sb(f"kd{d}", (P, PTOK)) for d in range(2)]
        e1 = c.sb("e1", (P, PTOK))
        tot = c.sb("tot", (P, 2, CHUNKS))
        sx = [c.sb(f"sx{d}", (P, CHUNKS, 5, CH)) for d in range(2)]
        psa, psb = c.ps("psa", (P, NCH, 512)), c.ps("psb", (P, NCH, 512))
        consts, loaded, zeroed = c.sem("consts"), c.sem("loaded"), c.sem("zeroed")
        products = c.sem("products")
        squared, floored, rooted = c.sem("squared"), c.sem("floored"), c.sem("rooted")
        sig_w, sig_a, summed, exped = c.sem("sig_w"), c.sem("sig_a"), c.sem("summed"), c.sem("exped")
        scaled_r, vcopied, ready = c.sem("scaled_r"), c.sem("vcopied"), c.sem("ready")
        bonus, stored, chain = c.sem("bonus"), c.sem("stored"), c.sem("chain")
        par = lambda name, off: g.par_sb[:, ds(PCOLS[name] + off, 1)]
        chunked = lambda t: t[:, :].rearrange("p (c t) -> p c t", t=CH)
        c.callback(c.reset)
        with nc.Block() as block:
            @block.sync
            def _(sp):
                c.prime(sp)
                sp.dma_start(heads[:, :], g.small_of("heads")).then_inc(consts, 16)
                sp.dma_start(first[:, :], g.first).then_inc(consts, 16)
                sp.dma_start(keep[:, :, :], g.keep.rearrange("p (d c) -> p d c", d=2)).then_inc(consts, 16)
                sp.wait_ge(zeroed, PRIMED + 3)
                with sp.Fori(0, FT) as f:
                    sp.wait_ge(stored, PRIMED + 48 * f)
                    for n, t in enumerate((r, k, v)):
                        for a, ln, p in SEQS:
                            sp.dma_start(t[:, p:p + ln], g.proj[ds((n * FT + f) * P, P), a:a + ln]
                                         ).then_inc(loaded, 16)
                    sp.dma_start(w2[:, :, :], g.lora2[ds(f, 1)].rearrange("a p m n -> (a p) m n")
                                 ).then_inc(loaded, 16)
                    for d in range(2):
                        sp.wait_ge(ready, PRIMED + 2 * f + d + 1)
                        sp.wait_ge(vcopied, PRIMED + 2 * f + d + 1)
                        sp.dma_start(g.sx[d, ds(f, 1)].rearrange("a p n -> (a p) n"),
                                     sx[d][:, :, :, :].rearrange("p c x t -> p (c x t)")).then_inc(stored, 16)
                    sp.wait_ge(bonus, PRIMED + f + 1)
                    sp.dma_start(g.bonus[ds(f * P, P), :], q[:, :]).then_inc(stored, 16)
                sp.wait_ge(stored, PRIMED + 48 * FT)

            @block.gpsimd
            def _(pool):
                for t in (r, k, v):
                    for a, ln, p in SEQS:
                        last = nc.gpsimd.memset(t[:, p + ln:PAD_B if p == 0 else PTOK], 0.0)
                    last.then_inc(zeroed, 1)

            @block.tensor
            def _(pe):
                pe.wait_ge(consts, PRIMED + 48)
                with pe.Fori(0, FT) as f:
                    def product(ps, lhsT, rhs):
                        for n in range(NCH):
                            last = nc.tensor.matmul(ps[:, n, 0:PW], lhsT, rhs[:, n * PW:(n + 1) * PW],
                                                    start=True, stop=True)
                        last.then_inc(products, 1)
                    pe.wait_ge(squared, PRIMED + f + 1)
                    product(psa, heads[:, :], q)
                    pe.wait_ge(loaded, PRIMED + 112 * f + 112)
                    pe.wait_ge(bonus, PRIMED + f)
                    product(psb, w2[:, 0, :], g.hid[:, 0, :])
                    pe.wait_ge(floored, PRIMED + f + 1)
                    product(psa, w2[:, 1, :], g.hid[:, 1, :])
                    pe.wait_ge(sig_w, PRIMED + 2 * f + 1)
                    product(psb, w2[:, 2, :], g.hid[:, 2, :])
                    pe.wait_ge(sig_a, PRIMED + 2 * f + 1)
                    product(psa, w2[:, 3, :], g.hid[:, 3, :])
                    pe.wait_ge(sig_w, PRIMED + 2 * f + 2)
                    pe.wait_ge(scaled_r, PRIMED + f + 1)
                    product(psb, heads[:, :], kds)

            @block.scalar
            def _(act):
                with act.Fori(0, FT) as f:
                    act.wait_ge(loaded, PRIMED + 112 * f + 112)
                    nc.scalar.activation(q[:, :], k[:, :], ACT.Square, scale=par("k_k", f)).then_inc(squared, 1)
                    for d in range(2):
                        nc.scalar.copy(sx[d][:, :, 4, :], chunked(v)).then_inc(vcopied, 1)
                    act.wait_ge(floored, PRIMED + f + 1)
                    nc.scalar.activation(q[:, :], q[:, :], ACT.Sqrt).then_inc(rooted, 1)
                    split = lambda t: t[:, :].rearrange("p (n t) -> p n t", n=NCH)
                    for d in range(2):
                        act.wait_ge(products, PRIMED + 6 * f + 2 * d + 2)
                        nc.scalar.activation(split(sg[d]), psb[:, :, 0:PW], ACT.Sigmoid,
                                             bias=par("decay_w0", d * FT + f)).then_inc(sig_w, 1)
                        act.wait_ge(products, PRIMED + 6 * f + 2 * d + 3)
                        nc.scalar.activation(split(av[d]), psa[:, :, 0:PW], ACT.Sigmoid,
                                             bias=par("aaa_a0", d * FT + f)).then_inc(sig_a, 1)
                    for d in range(2):
                        act.wait_ge(summed, PRIMED + 2 * f + d + 1)
                        if d:
                            act.wait_ge(ready, PRIMED + 2 * f + 1)
                        nc.scalar.activation(tot[:, d, :], tot[:, d, :], ACT.Exp, scale=-DECAY)
                        nc.scalar.activation(e1[:, :], cs[d][:, :], ACT.Exp, scale=-DECAY).then_inc(exped, 1)
                        nc.scalar.activation(ex[d][:, :], ex[d][:, :], ACT.Exp, scale=-DECAY).then_inc(exped, 1)
                        nc.scalar.activation(cs[d][:, :], cs[d][:, :], ACT.Exp, scale=DECAY).then_inc(exped, 1)

            @block.vector
            def _(dve):
                dve.wait_ge(consts, PRIMED + 48)
                LINKS = 8
                with dve.Fori(0, FT) as f:
                    chained = Chain(dve, chain, f * LINKS)
                    dve.wait_ge(products, PRIMED + 6 * f + 1)
                    nc.vector.tensor_scalar(q[:, :].rearrange("p (n t) -> p n t", n=NCH), psa[:, :, 0:PW], 1e-24, None, ALU.max
                                            ).then_inc(floored, 1)
                    dve.wait_ge(rooted, PRIMED + f + 1)
                    chained(nc.vector.reciprocal(q[:, :], q[:, :]))
                    chained(nc.vector.scalar_tensor_tensor(out=kk[:, :], in0=k[:, :], scalar=par("k_k", f),
                                                           in1=q[:, :], op0=ALU.mult, op1=ALU.mult))
                    for d in range(2):
                        dve.wait_ge(sig_w, PRIMED + 2 * f + d + 1)
                        dve.wait_ge(sig_a, PRIMED + 2 * f + d + 1)
                        c3, s3 = chunked(cs[d]), chunked(sg[d])
                        nc.vector.tensor_scalar(kd[d][:, :], av[d][:, :], -1.0, par("k_a", f), ALU.add, ALU.mult)
                        chained(nc.vector.tensor_tensor_scan(cs[d][:, :], first[:, :], sg[d][:, :], 0.0,
                                                             ALU.mult, ALU.add))
                        nc.vector.tensor_copy(tot[:, d, :].unsqueeze(2), c3[:, :, CH - 1:CH])
                        last = nc.vector.scalar_tensor_tensor(out=kd[d][:, :], in0=kd[d][:, :], scalar=1.0,
                                                              in1=k[:, :], op0=ALU.add, op1=ALU.mult)
                        nc.vector.tensor_tensor(av[d][:, :], kk[:, :], av[d][:, :], ALU.mult)
                        if d == 0:
                            chained(last)
                            nc.vector.tensor_tensor(ex[d][:, :], cs[d][:, :], sg[d][:, :], ALU.subtract
                                                    ).then_inc(summed, 1)
                        else:
                            chained(last)
                            chained(nc.vector.tensor_tensor(chunked(ex[d]), c3[:, :, CH - 1:CH].to_broadcast([P, CHUNKS, CH]),
                                                            c3, ALU.subtract))
                            nc.vector.tensor_tensor(cs[d][:, :], ex[d][:, :], sg[d][:, :], ALU.add
                                                    ).then_inc(summed, 1)
                    chained(nc.vector.tensor_tensor(kds[:, :], kd[0][:, :], kd[1][:, :], ALU.add))
                    nc.vector.scalar_tensor_tensor(out=kds[:, :], in0=r[:, :], scalar=par("r_k", f), in1=kds[:, :],
                                                   op0=ALU.mult, op1=ALU.mult).then_inc(scaled_r, 1)
                    for d in range(2):
                        dve.wait_ge(exped, PRIMED + 6 * f + 3 * d + 3)
                        o = lambda x: sx[d][:, :, x, :]
                        nc.vector.tensor_tensor(g.etot[:, d, ds(f, 1), :], tot[:, d, :].unsqueeze(1), keep[:, d, :].unsqueeze(1), ALU.mult)
                        nc.vector.tensor_tensor(o(0), chunked(r), chunked(e1), ALU.mult)
                        nc.vector.scalar_tensor_tensor(out=o(1), in0=chunked(kk), scalar=-1.0, in1=chunked(ex[d]),
                                                       op0=ALU.mult, op1=ALU.mult)
                        nc.vector.tensor_tensor(o(2), chunked(av[d]), chunked(cs[d]), ALU.mult)
                        nc.vector.tensor_tensor(o(3), chunked(kd[d]), chunked(cs[d]), ALU.mult).then_inc(ready, 1)
                    dve.wait_ge(products, PRIMED + 6 * f + 6)
                    nc.vector.tensor_tensor(q[:, :].rearrange("p (n t) -> p n t", n=NCH), psb[:, :, 0:PW],
                                            v[:, :].rearrange("p (n t) -> p n t", n=NCH), ALU.mult
                                            ).then_inc(bonus, 1)
                    assert chained.n == LINKS


def chunks(nc, g):
    J = 2
    PASSES = FT // J
    LOADS = (0, 3, CHUNKS // 2 + 2, CHUNKS)
    PAIRS = (CHUNKS - 2) // 2
    with Ctx(nc, "ch") as c:
        masks = c.sb("masks", (P, NSMALL))
        mask = {n: masks[:, lo:lo + wd] for n, (lo, wd) in SCOLS.items()}
        per_d = lambda name, shape: [c.sb(f"{name}{d}", shape) for d in range(2)]
        slots = lambda name, shape: [[c.sb(f"{name}{d}{s}", shape) for s in range(2)] for d in range(2)]
        sx = per_d("sx", (P, J, CHUNKS, 5, CH))
        ys = per_d("ys", (P, J, PTOK))
        bka = per_d("bka", (P, J, P))
        e_d = per_d("ed", (P, 2, J, P))
        xbd = per_d("xbd", (P, J, P))
        bbd, ubd = per_d("bbd", (P, J, P)), per_d("ubd", (P, J, P))
        sst, snw = per_d("sst", (P, J, P)), per_d("snw", (P, J, P))
        ops = slots("ops", (P, J, 4, 2, CH))
        ebd, akT = slots("ebd", (P, J, P)), slots("akT", (P, J, P))
        arT = slots("arT", (P, J, 2, CH))
        bkt = slots("bkt", (P, J, 2, P))
        vbd = slots("vbd", (P, J, P))
        bank = lambda name: [c.ps(f"{name}{d}") for d in range(2)]
        psa = bank("psa")
        psm = bank("psm")
        pse = bank("pse")
        pss = bank("pss")
        consts, zeroed, stored = c.sem("consts"), c.sem("zeroed"), c.sem("stored")
        loaded = [c.sem(f"loaded{h}") for h in range(3)]
        two = lambda name: [c.sem(f"{name}{d}") for d in range(2)]
        staged, first_products, a_read, v_copied = two("staged"), two("first"), two("a_read"), two("v_copied")
        turned, prepared = two("turned"), two("prepared")
        b_ready, b_copied, u_ready, u_copied = two("b_ready"), two("b_copied"), two("u_ready"), two("u_copied")
        y_ready, s_read, y_copied, s_new = two("y_ready"), two("s_read"), two("y_copied"), two("s_new")
        chain = two("chain")
        z_ready, x_ready, e_ready, e_copied = two("z_ready"), two("x_ready"), two("e_ready"), two("e_copied")
        pair = lambda ap: ap.rearrange("p (j t) -> p j t", j=J)
        halves = lambda ap: ap.rearrange("p j (h t) -> p j h t", h=2)
        flat = lambda ap: ap.rearrange("p a b -> p (a b)")

        def at(d, n):
            return n if d == 0 else n * -1 + (CHUNKS - 1)

        nothing = lambda d, k, n, slot: None

        def weave(eng, p, stages, between=None, ahead=nothing):
            pre, level, b_step, u_step, y_step = stages

            def half(d, n, slot, second, first=False, last=False):
                k = p * CHUNKS + n
                lev = lambda w: lambda: level(d, k, n, slot, w)
                old = lambda step: lambda: None if first else step(d, k - 1, n - 1, 1 - slot)
                next_one = lambda: None if last else ahead(d, k + 1, n + 1, 1 - slot)
                if not second:
                    return {0: [lambda: pre(d, k, n, slot)], 3: [lev(0), old(b_step)], 4: [lev(1)], 5: [lev(2)],
                            6: [lev(3)], 7: [old(u_step)], 8: [lev(4)]}
                return {1: [lev(5)], 2: [next_one, old(y_step)], 4: [lev(6)], 5: [lev(7)], 6: [lev(8)], 7: [lev(9)]}

            def together(*halves):
                for place in range(9):
                    for steps in halves:
                        for do in steps.get(place, ()):
                            do()

            def step(n, slot, last=False):
                together(half(0, n, slot, False), half(1, n - 1, 1 - slot, True))
                together(half(0, n, slot, True, last=last), half(1, n, slot, False))
            together(half(0, 0, 0, False, first=True))
            together(half(0, 0, 0, True, first=True), half(1, 0, 0, False, first=True))
            if between:
                between(p, 0)
            together(half(0, 1, 1, False), half(1, 0, 0, True, first=True))
            together(half(0, 1, 1, True), half(1, 1, 1, False))
            for h, (lo, hi) in enumerate(((1, 1 + PAIRS // 2), (1 + PAIRS // 2, PAIRS))):
                if between:
                    between(p, h + 1)
                with eng.Fori(lo, hi) as m:
                    step(2 * m, 0)
                    step(2 * m + 1, 1)
            step(CHUNKS - 2, 0)
            step(CHUNKS - 1, 1, last=True)
            together(half(1, CHUNKS - 1, 1, True, last=True))
            for q in (b_step, u_step, y_step):
                for d in range(2):
                    q(d, p * CHUNKS + CHUNKS - 1, CHUNKS - 1, 1)

        with nc.Block() as block:
            @block.sync
            def _(sp):
                c.prime(sp)
                sp.dma_start(masks[:, :], g.small).then_inc(consts, 16)
                for p in range(PASSES):
                    for h, (lo, hi) in enumerate(zip(LOADS, LOADS[1:])):
                        for d in range(2):
                            if p:
                                sp.wait_ge(y_ready[d], PRIMED + (p - 1) * CHUNKS + LOADS[h + 1])
                            lo, hi = LOADS[h:h + 2]
                            if d:
                                lo, hi = CHUNKS - hi, CHUNKS - lo
                            for j in range(J):
                                sp.dma_start(sx[d][:, j, lo:hi].rearrange("p c x t -> p (c x t)"),
                                             g.sx[d, p * J + j][:, lo * 5 * CH:hi * 5 * CH]).then_inc(loaded[h], 16)
                    for d in range(2):
                        sp.wait_ge(y_copied[d], PRIMED + (p + 1) * CHUNKS)
                        for j in range(J):
                            sp.dma_start(g.ydir[d, p * J + j], ys[d][:, j, :]).then_inc(stored, 16)
                sp.wait_ge(stored, PRIMED + 32 * J * PASSES)

            @block.gpsimd
            def _(pool):
                for d in range(2):
                    for t in (ops[d][0], ops[d][1], sst[d]):
                        nc.gpsimd.memset(t[:], 0.0).then_inc(zeroed, 1)

            @block.scalar
            def _(act):
                copy = nc.scalar.copy

                def stage(d, k, n, slot):
                    act.wait_ge(b_ready[d], PRIMED + k - 1)
                    for h in range(2):
                        rows = slice(h * CH, h * CH + CH)
                        for j in range(J):
                            src = sx[d][rows, j, ds(at(d, n), 1), :, :].rearrange("p a x t -> p (a x) t")
                            last = copy(ops[d][slot][rows, j, :, h, :], src[:, 1:5, :])
                    last.then_inc(staged[d], 1)

                def pre(d, k, n, slot):
                    act.wait_ge(first_products[d], PRIMED + k + 1)
                    act.wait_ge(y_ready[d], PRIMED + k - 1)
                    copy(bkt[d][slot][:, :, :, :].rearrange("p j x t -> p (j x t)"), pse[d][:, :]
                         ).then_inc(turned[d], 1)
                    act.wait_ge(a_read[d], PRIMED + k + 1)
                    copy(flat(vbd[d][slot][:, :, :]), psm[d][:, J * P:2 * J * P]).then_inc(v_copied[d], 1)

                def level(d, k, n, slot, w):
                    if w % 2:
                        act.wait_ge(e_ready[d], PRIMED + LEVELS * k + w // 2 + 1)
                        if w // 2 < LEVELS - 1:
                            copy(e_d[d][:, :, :, :].rearrange("p e j t -> p (e j t)"), pse[d][:, :]
                                 ).then_inc(e_copied[d], 1)
                        else:
                            copy(flat(ebd[d][slot][:, :, :]), pse[d][:, 0:J * P]).then_inc(e_copied[d], 1)

                def b_copy(d, k, n, slot):
                    act.wait_ge(b_ready[d], PRIMED + k + 1)
                    copy(flat(bbd[d][:, :, :]), pss[d][:, 0:J * P]).then_inc(b_copied[d], 1)

                def y_copy(d, k, n, slot):
                    act.wait_ge(s_read[d], PRIMED + k + 1)
                    copy(ys[d][:, :, ds(at(d, n) * CH, CH)], pair(pss[d][:, J * P:J * P + J * CH])
                         ).then_inc(y_copied[d], 1)

                def between(p, h):
                    if h == 0:
                        act.wait_ge(stored, PRIMED + 32 * J * p)
                    else:
                        act.wait_ge(loaded[h], PRIMED + 32 * J * (p + 1))
                act.wait_ge(zeroed, PRIMED + 6)
                with act.Fori(0, PASSES) as p:
                    act.wait_ge(loaded[0], PRIMED + 32 * J * (p + 1))
                    for d in range(2):
                        stage(d, p * CHUNKS, 0, 0)
                    weave(act, p, (pre, level, b_copy, nothing, y_copy), between, ahead=stage)

            @block.tensor
            def _(pe):
                pe.wait_ge(consts, PRIMED + 16)
                mm = nc.tensor.matmul

                def of(d, n, j, lo, hi):
                    return sx[d][:, j, ds(at(d, n), 1), lo:hi, :].rearrange("p a x t -> p (a x t)")

                def pre(d, k, n, slot):
                    pe.wait_ge(prepared[d], PRIMED + k)
                    pe.wait_ge(x_ready[d], PRIMED + LEVELS * k)
                    pe.wait_ge(e_copied[d], PRIMED + LEVELS * k)
                    pe.wait_ge(staged[d], PRIMED + k + 1)
                    for j in range(J):
                        a, b, kx, v = (flat(ops[d][slot][:, j, x]) for x in range(4))
                        mm(psm[d][:, j * P:(j + 1) * P], a, b, start=True, stop=True)
                        nc.tensor.transpose(psm[d][:, (J + j) * P:(J + j + 1) * P], v, mask["ident"])
                        for x, lhsT in enumerate((b, kx)):
                            mm(psa[d][:, (2 * j + x) * P:(2 * j + x + 1) * P], lhsT, of(d, n, j, 0, 2),
                               start=True, stop=True)
                            last = nc.tensor.transpose(pse[d][:, (2 * j + x) * P:(2 * j + x + 1) * P], lhsT,
                                                       mask["ident"])
                    last.then_inc(first_products[d], 1)

                def level(d, k, n, slot, w):
                    lev = w // 2
                    if w % 2 == 0:
                        if lev == 0:
                            pe.wait_ge(v_copied[d], PRIMED + k + 1)
                            pe.wait_ge(turned[d], PRIMED + k + 1)
                            pe.wait_ge(prepared[d], PRIMED + k + 1)
                        else:
                            pe.wait_ge(e_copied[d], PRIMED + LEVELS * k + lev)
                        for j in range(J):
                            last = mm(psm[d][:, j * P:(j + 1) * P], bka[d][:, j, :], e_d[d][:, 0, j, :],
                                      start=True, stop=True)
                        last.then_inc(z_ready[d], 1)
                    else:
                        pe.wait_ge(x_ready[d], PRIMED + LEVELS * k + lev + 1)
                        for j in range(J):
                            eT = e_d[d][:, 1, j, :]
                            last = mm(pse[d][:, j * P:(j + 1) * P], eT, xbd[d][:, j, :], start=True, stop=True)
                            if lev < LEVELS - 1:
                                last = mm(pse[d][:, (J + j) * P:(J + j + 1) * P], xbd[d][:, j, :], eT,
                                          start=True, stop=True)
                        last.then_inc(e_ready[d], 1)

                def b_step(d, k, n, slot):
                    pe.wait_ge(s_new[d], PRIMED + k)
                    pe.wait_ge(y_copied[d], PRIMED + k)
                    for j in range(J):
                        o = pss[d][:, j * P:(j + 1) * P]
                        mm(o, akT[d][slot][:, j, :], vbd[d][slot][:, j, :], start=True, stop=False)
                        last = mm(o, flat(ops[d][slot][:, j, 0]), sst[d][:, j, :], start=False, stop=True)
                    last.then_inc(b_ready[d], 1)

                def u_step(d, k, n, slot):
                    pe.wait_ge(b_copied[d], PRIMED + k + 1)
                    for j in range(J):
                        last = mm(pss[d][:, j * P:(j + 1) * P], ebd[d][slot][:, j, :], bbd[d][:, j, :],
                                  start=True, stop=True)
                    last.then_inc(u_ready[d], 1)

                def y_step(d, k, n, slot):
                    pe.wait_ge(u_copied[d], PRIMED + k + 1)
                    for j in range(J):
                        o = pss[d][:, J * P + j * CH:J * P + (j + 1) * CH]
                        v, u = vbd[d][slot][:, j, :], ubd[d][:, j, :]
                        mm(o, v, arT[d][slot][:, j, 1, :], start=True, stop=False)
                        mm(o, u, arT[d][slot][:, j, 0, :], start=False, stop=False)
                        mm(o, sst[d][:, j, :], of(d, n, j, 0, 1), start=False, stop=True)
                        o = pss[d][:, j * P:(j + 1) * P]
                        mm(o, bkt[d][slot][:, j, 0, :], u, start=True, stop=False)
                        last = mm(o, bkt[d][slot][:, j, 1, :], v, start=False, stop=True)
                    last.then_inc(y_ready[d], 1)
                with pe.Fori(0, PASSES) as p:
                    weave(pe, p, (pre, level, b_step, u_step, y_step))

            @block.vector
            def _(dve):
                tt = nc.vector.tensor_tensor
                both = lambda name: wide(mask[name], 1, (P, J, P))

                def blocks(out, src, name):
                    return tt(halves(out), wide(src, 2, (P, J, 2, CH)),
                              wide(mask[name].rearrange("p (h t) -> p h t", h=2), 1, (P, J, 2, CH)), ALU.mult)

                def pre(d, k, n, slot):
                    chained = Chain(dve, chain[d], k * 2)
                    dve.wait_ge(first_products[d], PRIMED + k + 1)
                    dve.wait_ge(y_ready[d], PRIMED + k - 1)
                    ps_a = psa[d][:, :].rearrange("p (j x y t) -> p j x y t", j=J, x=2, y=2)
                    e, eT = e_d[d][:, 0, :, :], e_d[d][:, 1, :, :]
                    tt(bka[d][:, :, :], pair(psm[d][:, 0:J * P]), both(f"after_bd{d}"), ALU.mult
                       ).then_inc(a_read[d], 1)
                    chained(blocks(e, ps_a[:, :, 0, 1, :], f"pair_bd{d}"))
                    chained(tt(bka[d][:, :, :], bka[d][:, :, :], both("ident"), ALU.add))
                    tt(e, e, both("ident"), ALU.add)
                    tt(eT, bka[d][:, :, :], both(f"pairT_bd{d}"), ALU.mult)
                    blocks(akT[d][slot][:, :, :], ps_a[:, :, 1, 1, :], f"strict_bd{d}")
                    tt(arT[d][slot][:, :, :, :], ps_a[:, :, :, 0, :],
                       mask[f"incl{d}"].unsqueeze(1).unsqueeze(1).to_broadcast([P, J, 2, CH]), ALU.mult
                       ).then_inc(prepared[d], 1)

                def level(d, k, n, slot, w):
                    if w % 2 == 0:
                        dve.wait_ge(z_ready[d], PRIMED + LEVELS * k + w // 2 + 1)
                        tt(xbd[d][:, :, :], pair(psm[d][:, 0:J * P]), both(f"lev{w // 2}_bd{d}"), ALU.mult
                           ).then_inc(x_ready[d], 1)

                def u_copy(d, k, n, slot):
                    dve.wait_ge(u_ready[d], PRIMED + k + 1)
                    nc.vector.tensor_copy(ubd[d][:, :, :], pair(pss[d][:, 0:J * P])).then_inc(u_copied[d], 1)

                def state(d, k, n, slot):
                    dve.wait_ge(y_ready[d], PRIMED + k + 1)
                    tt(snw[d][:, :, :], pair(pss[d][:, 0:J * P]), sst[d][:, :, :], ALU.add
                       ).then_inc(s_read[d], 1)
                    dve.wait_ge(s_read[d], PRIMED + k + 1)
                    tt(sst[d][:, :, :], snw[d][:, :, :],
                       g.etot[:, d, ds(p * J, J), ds(at(d, n), 1)].to_broadcast([P, J, P]), ALU.mult
                       ).then_inc(s_new[d], 1)
                dve.wait_ge(consts, PRIMED + 16)
                dve.wait_ge(zeroed, PRIMED + 6)
                with dve.Fori(0, PASSES) as p:
                    weave(dve, p, (pre, level, nothing, u_copy, state))


def mix_out(nc, g):
    with Ctx(nc, "mo") as c:
        y0, y1, bon = c.sb("y0", (P, PTOK)), c.sb("y1", (P, PTOK)), c.sb("bon", (P, PTOK))
        sq, ya = c.sb("sq", (P, PTOK)), c.sb("ya", (P, PTOK))
        heads = c.sb("heads", (P, P))
        zero = c.sb("zero", (P, KT, TT * P - TOK))
        psa, psb = c.ps("psa", (P, NCH, 512)), c.ps("psb", (P, NCH, 512))
        consts, loaded, stored, chain = c.sem("consts"), c.sem("loaded"), c.sem("stored"), c.sem("chain")
        added, products, squared, gates = c.sem("added"), c.sem("products"), c.sem("squared"), c.sem("gates")
        spread, rooted, done, pads, zeroed = c.sem("spread"), c.sem("rooted"), c.sem("done"), c.sem("pads"), c.sem("zeroed")
        w2f = c.sb("w2f", (P, 2, P))
        hidg = c.sb("hidg", (P, 2, PTOK))
        split = lambda t: t[:, :].rearrange("p (n t) -> p n t", n=NCH)
        par = lambda name, off: g.par_sb[:, ds(PCOLS[name] + off, 1)]
        c.callback(c.reset)
        with nc.Block() as block:
            @block.sync
            def _(sp):
                c.prime(sp)
                sp.dma_start(heads[:, :], g.small_of("heads")).then_inc(consts, 16)
                sp.dma_start(hidg[:, 0, :], g.hidg_dram[:, 0, :]).then_inc(consts, 16)
                sp.dma_start(hidg[0:GL - P, 1, :], g.hidg_dram[0:GL - P, 1, :]).then_inc(consts, 16)
                sp.wait_ge(zeroed, PRIMED + 1)
                sp.dma_start(g.mix[:, TOK:TT * P].rearrange("(k p) t -> p k t", p=P), zero[:, :, :]).then_inc(pads, 16)
                with sp.Fori(0, FT) as f:
                    sp.wait_ge(stored, PRIMED + 32 * f)
                    for n, t in enumerate((y0, y1)):
                        sp.dma_start(t[:, :], g.ydir[n, ds(f, 1)].rearrange("a p n -> (a p) n")).then_inc(loaded, 16)
                    sp.dma_start(bon[:, :], g.bonus[ds(f * P, P), :]).then_inc(loaded, 16)
                    sp.dma_start(w2f[:, 0, :], g.gate2[0:P, ds(f * P, P)]).then_inc(loaded, 16)
                    sp.dma_start(w2f[0:GL - P, 1, :], g.gate2[P:GL, ds(f * P, P)]).then_inc(loaded, 16)
                    sp.wait_ge(done, PRIMED + f + 1)
                    for a, ln, p in SEQS:
                        sp.dma_start(g.mix[ds(f * P, P), a:a + ln], ya[:, p:p + ln]).then_inc(stored, 16)
                sp.wait_ge(stored, PRIMED + 32 * FT)
                sp.wait_ge(pads, PRIMED + 16)

            @block.gpsimd
            def _(pool):
                nc.gpsimd.memset(zero[:], 0.0).then_inc(zeroed, 1)

            @block.tensor
            def _(pe):
                pe.wait_ge(consts, PRIMED + 48)
                with pe.Fori(0, FT) as f:
                    def sums(src, sem, count):
                        pe.wait_ge(sem, PRIMED + count)
                        for n in range(NCH):
                            last = nc.tensor.matmul(psa[:, n, 0:PW], heads[:, :], src[:, n * PW:(n + 1) * PW],
                                                    start=True, stop=True)
                        last.then_inc(products, 1)
                    sums(y0, added, f + 1)
                    pe.wait_ge(loaded, PRIMED + 80 * f + 80)
                    pe.wait_ge(done, PRIMED + f)
                    for n in range(NCH):
                        nc.tensor.matmul(psb[:, n, 0:PW], w2f[:, 0, :], hidg[:, 0, n * PW:(n + 1) * PW],
                                         start=True, stop=False)
                        last = nc.tensor.matmul(psb[:, n, 0:PW], w2f[0:GL - P, 1, :],
                                                hidg[0:GL - P, 1, n * PW:(n + 1) * PW], start=False, stop=True)
                    last.then_inc(gates, 1)
                    sums(sq, squared, f + 1)

            @block.scalar
            def _(act):
                with act.Fori(0, FT) as f:
                    act.wait_ge(chain, PRIMED + 5 * f + 1)
                    nc.scalar.activation(sq[:, :], y1[:, :], ACT.Square).then_inc(squared, 1)
                    act.wait_ge(spread, PRIMED + f + 1)
                    nc.scalar.activation(sq[:, :], sq[:, :], ACT.Sqrt).then_inc(rooted, 1)

            @block.vector
            def _(dve):
                with dve.Fori(0, FT) as f:
                    chained = Chain(dve, chain, f * 5)
                    dve.wait_ge(loaded, PRIMED + 80 * f + 80)
                    nc.vector.tensor_tensor(y0[:, :], y0[:, :], y1[:, :], ALU.add).then_inc(added, 1)
                    dve.wait_ge(products, PRIMED + 2 * f + 1)
                    chained(nc.vector.scalar_tensor_tensor(out=split(y1), in0=psa[:, :, 0:PW], scalar=-1.0 / HD,
                                                           in1=split(y0), op0=ALU.mult, op1=ALU.add))
                    dve.wait_ge(products, PRIMED + 2 * f + 2)
                    nc.vector.tensor_scalar(split(sq), psa[:, :, 0:PW], 1.0 / HD, 64e-5, ALU.mult, ALU.add
                                            ).then_inc(spread, 1)
                    dve.wait_ge(rooted, PRIMED + f + 1)
                    chained(nc.vector.reciprocal(sq[:, :], sq[:, :]))
                    chained(nc.vector.tensor_tensor(y1[:, :], y1[:, :], sq[:, :], ALU.mult))
                    chained(nc.vector.tensor_scalar(y1[:, :], y1[:, :], par("lnx_g", f), par("lnx_b", f),
                                                    ALU.mult, ALU.add))
                    chained(nc.vector.tensor_tensor(y1[:, :], y1[:, :], bon[:, :], ALU.add))
                    dve.wait_ge(gates, PRIMED + f + 1)
                    dve.wait_ge(stored, PRIMED + 32 * f)
                    nc.vector.tensor_tensor(split(ya), psb[:, :, 0:PW], split(y1), ALU.mult).then_inc(done, 1)


def attention_in(nc, g):
    with Ctx(nc, "ai") as c:
        two = lambda name: [c.sb(f"{name}{s}", (P, TOK)) for s in range(2)]
        raw, sq, nrm, rot = two("raw"), two("sq"), two("nrm"), two("rot")
        cos, sin = c.sb("cos", (P, TOK)), c.sb("sin", (P, TOK))
        heads, swap, ident = c.sb("heads", (P, P)), c.sb("swap", (P, P)), c.sb("ident", (P, P))
        psn, psr = c.ps("psn", (P, NCH, 512)), c.ps("psr", (P, NCH, 512))
        split = lambda t: t[:, :].rearrange("p (n t) -> p n t", n=NCH)
        squared, sums, meaned, rooted, inverted, normed, rotated, roped, placed = (
            c.sem(n) for n in ("squared", "sums", "meaned", "rooted", "inverted", "normed", "rotated",
                               "roped", "placed"))
        consts, zeroed, cosed, sined = c.sem("consts"), c.sem("zeroed"), c.sem("cosed"), c.sem("sined")
        v_turned, v_copied = c.sem("v_turned"), c.sem("v_copied")
        loaded, v_loaded = [[c.sem(f"{n}{s}") for s in range(2)] for n in ("loaded", "v_loaded")]
        TILES = 2 * HEADS
        with nc.Block() as block:
            @block.sync
            def _(sp):
                c.prime(sp)
                for t, name in ((heads, "heads"), (swap, "swap"), (ident, "ident")):
                    sp.dma_start(t[:, :], g.small_of(name)).then_inc(consts, 16)
                sp.dma_start(cos[:, :], g.cos).then_inc(consts, 16)
                sp.dma_start(sin[:, :], g.sin).then_inc(consts, 16)
                with sp.Fori(0, TILES // 2) as i:
                    for s in range(2):
                        sp.wait_ge(normed, PRIMED + 2 * i + s - 1 if s else PRIMED + 2 * i - 1)
                        sp.dma_start(raw[s][:, :], g.proj[ds((3 * FT + 2 * i + s) * P, P), :]).then_inc(loaded[s], 16)
                with sp.Fori(0, HEADS // 2) as i:
                    for s in range(2):
                        if s == 0:
                            sp.wait_ge(normed, PRIMED + TILES)
                        sp.wait_ge(v_turned, PRIMED + 2 * i)
                        sp.dma_start(raw[s][:, :], g.proj[ds((5 * FT + 2 * i + s) * P, P), :]).then_inc(v_loaded[s], 16)

            @block.gpsimd
            def _(pool):
                for x in range(2):
                    nc.gpsimd.memset(g.qx[(1 - x) * HD:(2 - x) * HD, :, x, :], 0.0).then_inc(zeroed, 1)

            @block.scalar
            def _(act):
                def square(i, s):
                    t = 2 * i + s
                    act.wait_ge(loaded[s], PRIMED + 16 * i + 16)
                    act.wait_ge(inverted, PRIMED + t - 1)
                    act.wait_ge(normed, PRIMED + t - 1)
                    nc.scalar.activation(sq[s][:, :], raw[s][:, :], ACT.Square).then_inc(squared, 1)

                def root(i, s):
                    t = 2 * i + s
                    act.wait_ge(meaned, PRIMED + t + 1)
                    nc.scalar.activation(sq[s][:, :], sq[s][:, :], ACT.Sqrt).then_inc(rooted, 1)

                def place(i, s, which):
                    t = 2 * i + s
                    act.wait_ge(roped, PRIMED + t + 1)
                    if which == 0:
                        for x in range(2):
                            rows = slice(x * HD, (x + 1) * HD)
                            last = nc.scalar.copy(g.qx[rows, ds(t, 1), x, :].rearrange("p a t -> p (a t)"),
                                                  rot[s][rows, :])
                        last.then_inc(placed, 1)
                square(0, 0)
                for which in range(2):
                    with act.Fori(which * 2, which * 2 + 2 - which) as i:
                        for s in range(2):
                            root(i, s)
                            square(i + s, 1 - s)
                            place(i, s, which)
                root(3, 0)
                square(3, 1)
                root(3, 1)

            @block.tensor
            def _(pe):
                pe.wait_ge(consts, PRIMED + 80)

                def over(ps, lhsT, src, sem):
                    for n in range(NCH):
                        last = nc.tensor.matmul(ps[:, n, 0:CW], lhsT, src[:, n * CW:(n + 1) * CW], start=True, stop=True)
                    last.then_inc(sem, 1)
                with pe.Fori(0, TILES // 2) as i:
                    for s in range(2):
                        t = 2 * i + s
                        pe.wait_ge(squared, PRIMED + t + 1)
                        pe.wait_ge(meaned, PRIMED + t)
                        over(psn, heads[:, :], sq[s], sums)
                        pe.wait_ge(normed, PRIMED + t + 1)
                        pe.wait_ge(sined, PRIMED + t)
                        over(psr, swap[:, :], nrm[s], rotated)
                pe.wait_ge(sined, PRIMED + TILES)
                pe.wait_ge(meaned, PRIMED + TILES)
                with pe.Fori(0, HEADS // 2) as i:
                    for s, ps in enumerate((psn, psr)):
                        pe.wait_ge(v_loaded[s], PRIMED + 16 * i + 16)
                        pe.wait_ge(v_copied, PRIMED + 2 * i + s - 1 if s else PRIMED + 2 * i)
                        for w, (t0, tn) in enumerate(VTILES):
                            last = nc.tensor.transpose(ps[0:tn, w // 4, (w % 4) * P:(w % 4 + 1) * P],
                                                       raw[s][:, t0:t0 + tn], ident[:, :])
                        last.then_inc(v_turned, 1)

            @block.vector
            def _(dve):
                dve.wait_ge(consts, PRIMED + 80)
                dve.wait_ge(zeroed, PRIMED + 2)

                def mean(t, s):
                    dve.wait_ge(sums, PRIMED + t + 1)
                    nc.vector.tensor_scalar(split(sq[s]), psn[:, :, 0:CW], 1.0 / HD, 1e-6, ALU.mult, ALU.add
                                            ).then_inc(meaned, 1)
                for which, gain in enumerate(("q_norm_g", "k_norm_g")):
                    with dve.Fori(which * 2, which * 2 + 2) as i:
                        for s in range(2):
                            t = 2 * i + s
                            mean(t, s)
                            dve.wait_ge(rooted, PRIMED + t + 1)
                            nc.vector.reciprocal(sq[s][:, :], sq[s][:, :]).then_inc(inverted, 1)
                            dve.wait_ge(inverted, PRIMED + t + 1)
                            nc.vector.scalar_tensor_tensor(out=nrm[s][:, :], in0=raw[s][:, :],
                                                           scalar=cut(g.par_sb, PCOLS[gain], 1), in1=sq[s][:, :],
                                                           op0=ALU.mult, op1=ALU.mult).then_inc(normed, 1)
                            if which == 0:
                                dve.wait_ge(placed, PRIMED + t - 1)
                            dve.wait_ge(rotated, PRIMED + t + 1)
                            nc.vector.tensor_tensor(split(rot[s]), psr[:, :, 0:CW], split(sin), ALU.mult
                                                    ).then_inc(sined, 1)
                            nc.vector.tensor_tensor(nrm[s][:, :], nrm[s][:, :], cos[:, :], ALU.mult
                                                    ).then_inc(cosed, 1)
                            dve.wait_ge(sined, PRIMED + t + 1)
                            dve.wait_ge(cosed, PRIMED + t + 1)
                            out = (rot[s][:, :] if which == 0 else
                                   g.kr[:, ds(t - HEADS, 1), :].rearrange("p a t -> p (a t)"))
                            nc.vector.tensor_tensor(out, nrm[s][:, :], rot[s][:, :], ALU.add).then_inc(roped, 1)
                with dve.Fori(0, HEADS // 2) as i:
                    for s, ps in enumerate((psn, psr)):
                        h = 2 * i + s
                        dve.wait_ge(v_turned, PRIMED + h + 1)
                        for w0, w1, rows in VRUNS:
                            last = nc.vector.tensor_copy(g.vt[0:rows, ds(h, 1), w0:w1, :].rearrange("p a w t -> p (a w t)"),
                                                         ps[:, :, :].rearrange("p b t -> p (b t)")[0:rows, w0 * P:w1 * P])
                        last.then_inc(v_copied, 1)


def attention(nc, g):
    units = []
    v0 = 0
    for a, ln, _p in SEQS:
        pieces = -(-ln // P)
        even = -(-ln // pieces)
        units += [(a + t, min(even, ln - t), a, ln, v0) for t in range(0, ln, even)]
        v0 += pieces
    NU = len(units)
    with Ctx(nc, "at") as c:
        ident = c.sb("ident", (P, P))
        pr = [[c.sb(f"pr{s}{x}", (P, LEN_B)) for x in range(2)] for s in range(2)]
        amT = [c.sb(f"amT{s}", (P, 9, P)) for s in range(2)]
        st = [c.sb(f"st{s}", (P, 2, 8)) for s in range(2)]
        lam = c.sb("lam", (P, 4 * HD))
        lams = c.sb("lams", (P, 4))
        pS = [c.ps("pS0", (P, 3, 512)), c.ps("pS1", (P, 3, 512))]
        pT, pO = c.ps("pT"), c.ps("pO")
        consts, chain, lamb = c.sem("consts"), c.sem("chain"), c.sem("lamb")
        two = lambda name: [c.sem(f"{name}0"), c.sem(f"{name}1")]
        scores, row_max, maxed, exped = two("scores"), two("row_max"), two("maxed"), two("exped")
        diffed, outs, ocopied = c.sem("diffed"), c.sem("outs"), c.sem("ocopied")
        turned, tcopied = c.sem("turned"), c.sem("tcopied")
        batches = [-(-(-(-u[3] // P)) // 4) for u in units]
        NB = sum(batches)
        bat0 = [sum(batches[:u]) for u in range(NU)]
        scale = HD ** -0.5
        line = lambda t: t[:, :, :].rearrange("p a b -> p (a b)")

        def weave(eng, h, ahead, batch, finish):
            for u in range(NU + 1):
                if u < NU:
                    ahead(h, u, 0)
                if u:
                    batch(h, u - 1, 0)
                if u < NU:
                    ahead(h, u, 1)
                if u:
                    for b in range(1, batches[u - 1]):
                        batch(h, u - 1, b)
                    finish(h, u - 1)

        with nc.Block() as block:
            @block.sync
            def _(sp):
                c.prime(sp)
                sp.dma_start(ident[:, :], g.small_of("ident")).then_inc(consts, 16)
                sp.dma_start(lam[:, :], g.lambdas.partition_broadcast(P)).then_inc(consts, 16)

            @block.tensor
            def _(pe):
                pe.wait_ge(consts, PRIMED + 32)
                mm = nc.tensor.matmul

                def score(h, u, x):
                    q0, qn, a, ln, v0 = units[u]
                    pe.wait_ge(exped[x], PRIMED + NU * h + u)
                    for lo in range(0, ln, 512):
                        wd = min(512, ln - lo)
                        last = mm(pS[x][0:qn, lo // 512, 0:wd], q_now[:, x, q0:q0 + qn], k_of(h)[:, a + lo:a + lo + wd],
                                  start=True, stop=True)
                    last.then_inc(scores[x], 1)

                def turn(h, u, b):
                    q0, qn, a, ln, v0 = units[u]
                    if b == 0:
                        pe.wait_ge(diffed, PRIMED + NU * h + u + 1)
                    pe.wait_ge(tcopied, PRIMED + NB * h + bat0[u] + b)
                    for w in range(4 * b, min(4 * b + 4, -(-ln // P))):
                        kn = min(P, ln - w * P)
                        last = nc.tensor.transpose(pT[0:kn, (w % 4) * P:(w % 4) * P + qn],
                                                   pr[u % 2][0][0:qn, w * P:w * P + kn], ident[0:qn, 0:qn])
                    last.then_inc(turned, 1)
                    if b:
                        times_v(h, u, b - 1)

                def times_v(h, u, b):
                    q0, qn, a, ln, v0 = units[u]
                    nk = -(-ln // P)
                    if b == 0:
                        pe.wait_ge(ocopied, PRIMED + NU * h + u)
                    pe.wait_ge(tcopied, PRIMED + NB * h + bat0[u] + b + 1)
                    for w in range(4 * b, min(4 * b + 4, nk)):
                        kn = min(P, ln - w * P)
                        last = mm(pO[:, 0:qn], v_now[0:kn, v0 + w, :], amT[u % 2][0:kn, w, 0:qn],
                                  start=(w == 0), stop=(w == nk - 1))
                    if b == batches[u] - 1:
                        last.then_inc(outs, 1)
                k_of = lambda h: g.kr[:, ds(h, 1), :].rearrange("p a t -> p (a t)")
                for h in range(HEADS):
                    q_now, v_now = g.qx[:, h], g.vt[:, h]
                    k_of = lambda h: g.kr[:, h]
                    weave(pe, h, score, turn, lambda h, u: times_v(h, u, batches[u] - 1))

            @block.scalar
            def _(act):
                act.wait_ge(lamb, PRIMED + 1)
                nc.scalar.activation(lams[:, 0:2], lams[:, 0:2], ACT.Exp).then_inc(lamb, 1)

                def exp(h, u, x):
                    q0, qn, a, ln, v0 = units[u]
                    act.wait_ge(maxed[x], PRIMED + NU * h + u + 1)
                    nc.scalar.activation(pr[u % 2][x][0:qn, 0:ln], line(pS[x])[0:qn, 0:ln], ACT.Exp,
                                         bias=st[u % 2][0:qn, x, 1:2], scale=scale,
                                         accum_out=st[u % 2][0:qn, x, 2:3]).then_inc(exped[x], 1)

                def out_of(h, u):
                    q0, qn, a, ln, v0 = units[u]
                    act.wait_ge(outs, PRIMED + NU * h + u + 1)
                    nc.scalar.copy(g.oT[:, ds(h, 1), q0:q0 + qn].rearrange("p a t -> p (a t)"), pO[:, 0:qn]
                                   ).then_inc(ocopied, 1)
                with act.Fori(0, HEADS) as h:
                    weave(act, h, exp, lambda h, u, b: None, out_of)

            @block.vector
            def _(dve):
                LINKS = 3 * NU
                dve.wait_ge(consts, PRIMED + 32)
                pre = Chain(dve, chain)
                for x in range(2):
                    pre(nc.vector.tensor_tensor(lam[:, 2 * x * HD:(2 * x + 1) * HD], lam[:, 2 * x * HD:(2 * x + 1) * HD],
                                                lam[:, (2 * x + 1) * HD:(2 * x + 2) * HD], ALU.mult))
                    pre(nc.vector.reduce_sum(lams[:, x:x + 1], lam[:, 2 * x * HD:(2 * x + 1) * HD], AX_X))
                pre(nc.vector.tensor_copy(lams[:, 3:4], lams[:, 0:1]))
                nc.vector.tensor_copy(lams[:, 2:3], lams[:, 1:2]).then_inc(lamb, 1)
                dve.wait_ge(lamb, PRIMED + 2)
                pre(nc.vector.tensor_tensor(lams[:, 2:3], lams[:, 1:2], lams[:, 0:1], ALU.subtract))
                pre(nc.vector.tensor_scalar(lams[:, 3:4], lams[:, 2:3], -LAMBDA_INIT, None, ALU.add))
                PRE = pre.n

                def largest(h, u, x):
                    q0, qn, a, ln, v0 = units[u]
                    s = st[u % 2]
                    dve.wait_ge(scores[x], PRIMED + NU * h + u + 1)
                    nc.vector.reduce_max(s[0:qn, x, 0:1], line(pS[x])[0:qn, 0:ln], AX_X).then_inc(row_max[x], 1)
                    dve.wait_ge(row_max[x], PRIMED + NU * h + u + 1)
                    nc.vector.tensor_scalar(s[0:qn, x, 1:2], s[0:qn, x, 0:1], -scale, None, ALU.mult
                                            ).then_inc(maxed[x], 1)

                def turn_copy(h, u, b):
                    q0, qn, a, ln, v0 = units[u]
                    dve.wait_ge(turned, PRIMED + NB * h + bat0[u] + b + 1)
                    dve.wait_ge(outs, PRIMED + NU * h + u - 1)
                    w0, w1 = 4 * b, min(4 * b + 4, -(-ln // P))
                    full = min(w1, ln // P)
                    if full > w0:
                        last = nc.vector.tensor_copy(amT[u % 2][:, w0:full, 0:qn],
                                                     pT[:, :].rearrange("p (w t) -> p w t", w=4)[:, 0:full - w0, 0:qn])
                    if full < w1:
                        kn = ln - full * P
                        last = nc.vector.tensor_copy(amT[u % 2][0:kn, full, 0:qn],
                                                     pT[0:kn, (full % 4) * P:(full % 4) * P + qn])
                    last.then_inc(tcopied, 1)

                with dve.Fori(0, HEADS) as h:
                    chained = Chain(dve, chain, h * LINKS + PRE)

                    def difference(u):
                        q0, qn, a, ln, v0 = units[u]
                        s = st[u % 2]
                        for x in range(2):
                            dve.wait_ge(exped[x], PRIMED + NU * h + u + 1)
                        chained(nc.vector.reciprocal(s[0:qn, :, 3:4], s[0:qn, :, 2:3]))
                        chained(nc.vector.tensor_tensor(s[0:qn, 1, 4:5], s[0:qn, 1, 3:4], lams[0:qn, 3:4], ALU.mult))
                        p0, p1 = pr[u % 2][0][0:qn, 0:ln], pr[u % 2][1][0:qn, 0:ln]
                        chained(nc.vector.tensor_scalar(p1, p1, s[0:qn, 1, 4:5], None, ALU.mult))
                        nc.vector.scalar_tensor_tensor(out=p0, in0=p0, scalar=s[0:qn, 0, 3:4], in1=p1,
                                                       op0=ALU.mult, op1=ALU.add).then_inc(diffed, 1)

                    def one(h, u, x):
                        if x == 0 and u:
                            difference(u - 1)
                        largest(h, u, x)

                    def batch(h, u, b):
                        if b == 0 and u == NU - 1:
                            difference(u)
                        turn_copy(h, u, b)
                    weave(dve, h, one, batch, lambda h, u: None)


def attention_out(nc, g):
    with Ctx(nc, "ao") as c:
        sq = [c.sb(f"sq{s}", (P, TOK)) for s in range(2)]
        ones, sg = c.sb("ones", (P, P)), c.sb("sg", (P, 1))
        acc = [c.ps(f"acc{s}", (P, NCH, 512)) for s in range(2)]
        consts, stored, gained = c.sem("consts"), c.sem("stored"), c.sem("gained")
        squared, sums, meaned, rooted, inverted, done = (
            c.sem(n) for n in ("squared", "sums", "meaned", "rooted", "inverted", "done"))
        split = lambda t: t[:, :].rearrange("p (n t) -> p n t", n=NCH)
        with nc.Block() as block:
            @block.sync
            def _(sp):
                c.prime(sp)
                sp.dma_start(ones[:, :], g.small_of("ones")).then_inc(consts, 16)
                for h in range(HEADS):
                    sp.wait_ge(done, PRIMED + h + 1)
                    sp.dma_start(g.mix[RW + h * P:RW + (h + 1) * P, 0:TOK], g.oT[:, h]).then_inc(stored, 16)
                sp.wait_ge(stored, PRIMED + 16 * HEADS)

            @block.scalar
            def _(act):
                for h in range(HEADS):
                    if h >= 2:
                        act.wait_ge(done, PRIMED + h - 1)
                    nc.scalar.activation(sq[h % 2][:, :], g.oT[:, h], ACT.Square).then_inc(squared, 1)
                    if h:
                        act.wait_ge(meaned, PRIMED + h)
                        nc.scalar.activation(sq[(h - 1) % 2][:, :], sq[(h - 1) % 2][:, :], ACT.Sqrt).then_inc(rooted, 1)
                act.wait_ge(meaned, PRIMED + HEADS)
                nc.scalar.activation(sq[(HEADS - 1) % 2][:, :], sq[(HEADS - 1) % 2][:, :], ACT.Sqrt).then_inc(rooted, 1)

            @block.tensor
            def _(pe):
                pe.wait_ge(consts, PRIMED + 16)
                for h in range(HEADS):
                    pe.wait_ge(squared, PRIMED + h + 1)
                    if h >= 2:
                        pe.wait_ge(meaned, PRIMED + h - 1)
                    for n in range(NCH):
                        last = nc.tensor.matmul(acc[h % 2][:, n, 0:CW], ones[:, :], sq[h % 2][:, n * CW:(n + 1) * CW],
                                                start=True, stop=True)
                    last.then_inc(sums, 1)

            @block.vector
            def _(dve):
                nc.vector.tensor_scalar(sg[:, :], cut(g.par_sb, PCOLS["subln_g"], 1), 1.0 - LAMBDA_INIT, None, ALU.mult
                                        ).then_inc(gained, 1)
                dve.wait_ge(gained, PRIMED + 1)
                for h in range(HEADS):
                    dve.wait_ge(sums, PRIMED + h + 1)
                    nc.vector.tensor_scalar(split(sq[h % 2]), acc[h % 2][:, :, 0:CW], 1.0 / P, 1e-6, ALU.mult, ALU.add
                                            ).then_inc(meaned, 1)
                    dve.wait_ge(rooted, PRIMED + h + 1)
                    nc.vector.reciprocal(sq[h % 2][:, :], sq[h % 2][:, :]).then_inc(inverted, 1)
                    dve.wait_ge(inverted, PRIMED + h + 1)
                    nc.vector.scalar_tensor_tensor(out=g.oT[:, h], in0=g.oT[:, h], scalar=sg[:, 0:1], in1=sq[h % 2][:, :],
                                                   op0=ALU.mult, op1=ALU.mult).then_inc(done, 1)


def out_project(nc, g):
    with Ctx(nc, "op") as c:
        w = c.sb("w", (P, KT, D))
        ident = c.sb("ident", (P, P))
        m = [c.sb(f"m{s}", (P, KT, P)) for s in range(2)]
        x = [c.sb(f"x{s}", (P, D)) for s in range(2)]
        x1, sq, xn = c.sb("sum", (P, D)), c.sb("sq", (P, D)), c.sb("xn", (P, D))
        st = c.sb("st", (P, 4))
        acc = [c.ps(f"acc{s}", (P, 2, 512)) for s in range(2)]
        tp = c.ps("tp", (P, 2, 512))
        weights, stored = c.sem("weights"), c.sem("stored")
        loaded = [c.sem(f"loaded{s}") for s in range(2)]
        products = [c.sem(f"products{s}") for s in range(2)]
        added, squared, rooted, scaled = c.sem("added"), c.sem("squared"), c.sem("rooted"), c.sem("scaled")
        chain = [c.sem(f"chain{s}") for s in range(2)]
        turned, taken = c.sem("turned"), c.sem("taken")
        gain = cut(g.par_sb, PCOLS["ln2_g"], KT)
        PAIRS = TT // 2

        c.callback(c.reset)
        with nc.Block() as block:
            @block.sync
            def _(sp):
                c.prime(sp)
                sp.dma_start(w[:, :, :], g.w_out.rearrange("(k p) n -> p k n", p=P)).then_inc(weights, 16)
                sp.dma_start(ident[:, :], g.small_of("ident")).then_inc(weights, 16)

                def load(i, s, t):
                    sp.wait_ge(products[s], PRIMED + i)
                    sp.wait_ge(chain[s], PRIMED + 2 * i)
                    sp.dma_start(m[s][:, :, :], g.mix[:, ds(t * P, P)].rearrange("(k p) t -> p k t", p=P)
                                 ).then_inc(loaded[s], 16)
                    sp.dma_start(x[s][:, :], g.x[ds(t * P, P), :]).then_inc(loaded[s], 16)

                def store(t):
                    sp.wait_ge(added, PRIMED + t + 1)
                    sp.dma_start(g.x1[ds(t * P, P), :], x1[:, :]).then_inc(stored, 16)
                load(0, 0, 0)
                load(0, 1, 1)
                with sp.Fori(0, PAIRS - 1) as i:
                    for s in range(2):
                        store(2 * i + s)
                        load(i + 1, s, 2 * i + 2 + s)
                store(2 * PAIRS - 2)
                load(PAIRS, 0, 2 * PAIRS)
                store(2 * PAIRS - 1)
                store(2 * PAIRS)
                sp.wait_ge(stored, PRIMED + 16 * TT)

            @block.tensor
            def _(pe):
                pe.wait_ge(weights, PRIMED + 32)

                def product(i, s, t):
                    pe.wait_ge(loaded[s], PRIMED + 32 * i + 32)
                    pe.wait_ge(chain[s], PRIMED + 2 * i)
                    for b in range(2):
                        for k in range(KT):
                            last = nc.tensor.matmul(acc[s][:, b, :], m[s][:, k, :], w[:, k, b * 512:(b + 1) * 512],
                                                    start=(k == 0), stop=(k == KT - 1))
                    last.then_inc(products[s], 1)

                def turn(t):
                    pe.wait_ge(scaled, PRIMED + t + 1)
                    pe.wait_ge(taken, PRIMED + t)
                    for k in range(KT):
                        last = nc.tensor.transpose(tp[:, k // 4, (k % 4) * P:(k % 4 + 1) * P],
                                                   xn[:, k * P:(k + 1) * P], ident[:, :])
                    last.then_inc(turned, 1)
                product(0, 0, 0)
                with pe.Fori(0, PAIRS) as i:
                    product(i, 1, 2 * i + 1)
                    turn(2 * i)
                    product(i + 1, 0, 2 * i + 2)
                    turn(2 * i + 1)
                turn(2 * PAIRS)

            @block.scalar
            def _(act):
                def tile(i, s, t):
                    act.wait_ge(added, PRIMED + t + 1)
                    nc.scalar.activation(sq[:, :], x1[:, :], ACT.Square, accum_out=st[:, 0:1]).then_inc(squared, 1)
                    act.wait_ge(chain[s], PRIMED + 2 * i + 1)
                    nc.scalar.activation(st[:, 2:3], st[:, 1:2], ACT.Sqrt).then_inc(rooted, 1)
                with act.Fori(0, PAIRS) as i:
                    tile(i, 0, 2 * i)
                    tile(i, 1, 2 * i + 1)
                tile(PAIRS, 0, 2 * PAIRS)

            @block.vector
            def _(dve):
                def tile(i, s, t):
                    chained = Chain(dve, chain[s], 2 * i)
                    dve.wait_ge(products[s], PRIMED + i + 1)
                    dve.wait_ge(stored, PRIMED + 16 * t)
                    nc.vector.tensor_tensor(x1[:, :].rearrange("p (b n) -> p b n", b=2), acc[s][:, :, :],
                                            x[s][:, :].rearrange("p (b n) -> p b n", b=2), ALU.add
                                            ).then_inc(added, 1)
                    dve.wait_ge(squared, PRIMED + t + 1)
                    nc.vector.tensor_scalar(st[:, 1:2], st[:, 0:1], 1.0 / D, 1e-6, ALU.mult, ALU.add
                                            ).then_inc(chain[s], 1)
                    chained.n += 1
                    dve.wait_ge(rooted, PRIMED + t + 1)
                    chained(nc.vector.reciprocal(st[:, 3:4], st[:, 2:3]))
                    dve.wait_ge(turned, PRIMED + t)
                    nc.vector.tensor_scalar(xn[:, :], x1[:, :], st[:, 3:4], None, ALU.mult).then_inc(scaled, 1)
                    dve.wait_ge(turned, PRIMED + t + 1)
                    nc.vector.tensor_tensor(g.nT[:, :, ds(t * P, P)].rearrange("p (b k) t -> p b k t", b=2),
                                            tp[:, :, :].rearrange("p b (k t) -> p b k t", k=4),
                                            gain.rearrange("p (b k) -> p b k", b=2).unsqueeze(3).to_broadcast([P, 2, 4, P]),
                                            ALU.mult).then_inc(taken, 1)
                with dve.Fori(0, PAIRS) as i:
                    tile(i, 0, 2 * i)
                    tile(i, 1, 2 * i + 1)
                tile(PAIRS, 0, 2 * PAIRS)


def ffn_up(nc, g):
    with Ctx(nc, "fu") as c:
        wg = [c.sb(f"wg{s}", (P, KT, P)) for s in range(2)]
        wu = [c.sb(f"wu{s}", (P, KT, P)) for s in range(2)]
        gate = c.sb("gate", (P, TOK))
        pg = [c.ps(f"pg{n}") for n in range(NCH)]
        pu = [c.ps(f"pu{n}") for n in range(NCH)]
        loaded = [c.sem(f"loaded{s}") for s in range(2)]
        gated, silued, done = c.sem("gated"), c.sem("silued"), c.sem("done")
        upped = [c.sem(f"upped{s}") for s in range(2)]
        STEPS = FFT // 2
        c.callback(c.reset)
        with nc.Block() as block:
            @block.sync
            def _(sp):
                c.prime(sp)
                with sp.Fori(0, STEPS) as i:
                    for s in range(2):
                        sp.wait_ge(upped[s], PRIMED + NCH * i)
                        for t, src in ((wg[s], g.w_gate), (wu[s], g.w_up)):
                            sp.dma_start(t[:, :, :], src[ds(2 * i + s, 1)].rearrange("a p k n -> (a p) k n")
                                         ).then_inc(loaded[s], 16)

            @block.tensor
            def _(pe):
                with pe.Fori(0, STEPS) as i:
                    for s in range(2):
                        pe.wait_ge(loaded[s], PRIMED + 32 * i + 32)
                        m = 2 * i + s
                        for n in range(NCH):
                            pe.wait_ge(done, PRIMED + NCH * m)
                            for ps, w, sem in ((pg, wg, gated), (pu, wu, upped[s])):
                                for k in range(KT):
                                    last = nc.tensor.matmul(ps[n][:, 0:CW], w[s][:, k, :],
                                                            g.nT[:, k, n * CW:(n + 1) * CW],
                                                            start=(k == 0), stop=(k == KT - 1))
                                last.then_inc(sem, 1)

            @block.scalar
            def _(act):
                with act.Fori(0, FFT) as m:
                    act.wait_ge(done, PRIMED + NCH * m)
                    for n in range(NCH):
                        act.wait_ge(gated, PRIMED + NCH * m + n + 1)
                        nc.scalar.activation(gate[:, n * CW:(n + 1) * CW], pg[n][:, 0:CW], ACT.Silu
                                             ).then_inc(silued, 1)

            @block.vector
            def _(dve):
                with dve.Fori(0, STEPS) as i:
                    for s, n in [(s, n) for s in range(2) for n in range(NCH)]:
                        m = 2 * i + s
                        dve.wait_ge(silued, PRIMED + NCH * m + n + 1)
                        dve.wait_ge(upped[s], PRIMED + NCH * i + n + 1)
                        nc.vector.tensor_tensor(g.hT[:, ds(m, 1), n * CW:(n + 1) * CW].rearrange("p a t -> p (a t)"),
                                                pu[n][:, 0:CW], gate[:, n * CW:(n + 1) * CW], ALU.mult).then_inc(done, 1)


def ffn_down(nc, g):
    with Ctx(nc, "fd") as c:
        w = [c.sb(f"w{s}", (P, FFT, P)) for s in range(2)]
        x1, out = c.sb("x1", (P, TT, P)), c.sb("out", (P, TT, P))
        yT = c.sb("yT", (P, TT * P))
        ident = c.sb("ident", (P, P))
        acc = [c.ps(f"acc{n}") for n in range(NCH)]
        tp = c.ps("tp", (P, 3, 512))
        loaded = [c.sem(f"loaded{s}") for s in range(2)]
        consts, rows, copied = c.sem("consts"), c.sem("rows"), c.sem("copied")
        turned, added, stored, zeroed = c.sem("turned"), c.sem("added"), c.sem("stored"), c.sem("zeroed")
        products = [c.sem(f"products{s}") for s in range(2)]
        STEPS = KT // 2
        PIECES = [(META, P - META, 0, 1, 0, 0), (0, P, 1, 1, 0, P - META), (0, META, 2, 1, 0, 2 * P - META),
                  (32, P - 32, 2, 1, 1, 0), (0, P, 3, 7, 1, 96), (0, 32, 10, 1, 1, 992)]
        c.callback(c.reset)
        with nc.Block() as block:
            @block.sync
            def _(sp):
                c.prime(sp)
                sp.dma_start(ident[:, :], g.small_of("ident")).then_inc(consts, 16)

                def weights(i, s):
                    sp.wait_ge(products[s], PRIMED + NCH * i)
                    sp.dma_start(w[s][:, :, :], g.w_down[ds(2 * i + s, 1)].rearrange("a p k n -> (a p) k n")
                                 ).then_inc(loaded[s], 16)

                def residual(m):
                    sp.wait_ge(added, PRIMED + m)
                    sp.dma_start(x1[:, :, :], g.x1[:, ds(m * P, P)].rearrange("(t p) n -> p t n", p=P)
                                 ).then_inc(rows, 16)

                def store(m):
                    sp.wait_ge(added, PRIMED + m + 1)
                    for p0, pn, t0, tn, o, r0 in PIECES:
                        dst = g.out[o][0, r0:r0 + pn * tn, ds(m * P, P)]
                        sp.dma_start(dst.rearrange("(t p) n -> p t n", t=tn), out[p0:p0 + pn, t0:t0 + tn, :]
                                     ).then_inc(stored, 16)
                weights(0, 0)
                weights(0, 1)
                residual(0)
                with sp.Fori(0, STEPS - 1) as i:
                    for s in range(2):
                        residual(2 * i + s + 1)
                        weights(i + 1, s)
                        store(2 * i + s)
                residual(KT - 1)
                store(KT - 2)
                store(KT - 1)
                sp.wait_ge(stored, PRIMED + 16 * len(PIECES) * KT)

            @block.tensor
            def _(pe):
                pe.wait_ge(consts, PRIMED + 16)
                pe.wait_ge(zeroed, PRIMED + 1)
                with pe.Fori(0, STEPS) as i:
                    for s in range(2):
                        m = 2 * i + s
                        pe.wait_ge(loaded[s], PRIMED + 16 * i + 16)
                        pe.wait_ge(copied, PRIMED + NCH * m)
                        for n in range(NCH):
                            for k in range(FFT):
                                last = nc.tensor.matmul(acc[n][:, 0:CW], w[s][:, k, :], g.hT[:, k, n * CW:(n + 1) * CW],
                                                        start=(k == 0), stop=(k == FFT - 1))
                            last.then_inc(products[s], 1)
                        pe.wait_ge(copied, PRIMED + NCH * m + NCH)
                        pe.wait_ge(added, PRIMED + m)
                        for t in range(TT):
                            last = nc.tensor.transpose(tp[:, t // 4, (t % 4) * P:(t % 4 + 1) * P],
                                                       yT[:, t * P:(t + 1) * P], ident[:, :])
                        last.then_inc(turned, 1)

            @block.scalar
            def _(act):
                with act.Fori(0, STEPS) as i:
                    for s, n in [(s, n) for s in range(2) for n in range(NCH)]:
                        act.wait_ge(turned, PRIMED + 2 * i + s)
                        act.wait_ge(products[s], PRIMED + NCH * i + n + 1)
                        nc.scalar.copy(yT[:, n * CW:(n + 1) * CW], acc[n][:, 0:CW]).then_inc(copied, 1)

            @block.vector
            def _(dve):
                nc.vector.memset(yT[:, TOK:TT * P], 0.0).then_inc(zeroed, 1)
                with dve.Fori(0, KT) as m:
                    dve.wait_ge(turned, PRIMED + m + 1)
                    dve.wait_ge(rows, PRIMED + 16 * m + 16)
                    dve.wait_ge(stored, PRIMED + 16 * len(PIECES) * m)
                    nc.vector.tensor_tensor(out[:, :, :].rearrange("p t n -> p (t n)"),
                                            tp[:, :, :].rearrange("p b n -> p (b n)")[:, 0:TT * P],
                                            x1[:, :, :].rearrange("p t n -> p (t n)"), ALU.add).then_inc(added, 1)


class Tensors:

    def __init__(self, dram, out):
        self.out = out
        self.x = dram["x"]
        self.par = dram["par"]
        self.w_in = dram["w_in"]
        self.lora1 = dram["lora1"]
        self.lora2 = dram["lora2"]
        self.gate2 = dram["gate2"]
        self.lambdas = dram["lambdas"]
        self.w_out = dram["w_out"]
        self.w_gate = dram["w_gate"]
        self.w_up = dram["w_up"]
        self.w_down = dram["w_down"]
        self.small = dram["small"]
        self.cos = dram["cos"]
        self.sin = dram["sin"]
        self.first = dram["first"]
        self.keep = dram["keep"]

    def small_of(self, name):
        lo, wd = SCOLS[name]
        return self.small[:, lo:lo + wd]


def encoder(nc, g):
    scratch = lambda name, shape: nc.dram_tensor(f"dram_{name}", list(shape), F32, kind=SCRATCH_KIND).ap()
    g.proj = scratch("proj", (3072, TOK))
    g.sx = scratch("sx", (2, FT, P, CHUNKS * 5 * CH))
    g.bonus = scratch("bonus", (RW, PTOK))
    g.ydir = scratch("ydir", (2, FT, P, PTOK))
    g.hidg_dram = scratch("hidg", (P, 2, PTOK))
    g.mix = scratch("mix", (D, TT * P))
    g.x1 = scratch("x1", (TT * P, D))

    with Ctx(nc, "all") as whole:
        g.par_sb = whole.sb("par", (P, NPAR))
        with Ctx(nc, "mixer") as mixer:
            g.etot = mixer.sb("etot", (P, 2, FT, CHUNKS))
            with Ctx(nc, "lora") as lora:
                g.hid = lora.sb("hid", (HD, 4, PTOK))
                with Ctx(nc, "n") as norm:
                    g.nT = norm.sb("nT", (P, KT, TT * P))
                    norm_in(nc, g)
                    project(nc, g)
                    lora_in(nc, g)
                prep(nc, g)
            chunks(nc, g)
            mix_out(nc, g)
        with Ctx(nc, "heads") as kept:
            g.qx, g.kr = kept.sb("qx", (P, HEADS, 2, TOK)), kept.sb("kr", (P, HEADS, TOK))
            g.vt, g.oT = kept.sb("vt", (P, HEADS, len(VTILES), P)), kept.sb("oT", (P, HEADS, TOK))
            attention_in(nc, g)
            attention(nc, g)
            attention_out(nc, g)
        g.nT = whole.sb("n2T", (P, KT, TT * P))
        out_project(nc, g)
        g.hT = whole.sb("hT", (P, FFT, TOK))
        ffn_up(nc, g)
        ffn_down(nc, g)


def laid_out(inputs):
    a = {n: np.asarray(v) for n, v in inputs.items()}
    cat = np.concatenate
    meta = a["meta_tokens"]
    x = cat([meta, a["x_prompt"][0], meta, a["x_sample"][0], np.zeros((TT * P - TOK, D), np.float32)])
    column = lambda v: v.reshape(-1, P).T
    rows = [column(a["ln1_g"][0]), column(a["ln2_g"][0])]
    rows += [column(a["conv_rkv"][0, n]) for n in range(3)]
    for name in ("mix_w", "mix_a"):
        rows += [column(a[name][0, d]) for d in range(2)]
    rows.append(column(a["mix_g"][0]))
    for name in ("decay_w0", "aaa_a0"):
        rows += [column(a[name][0, d]) for d in range(2)]
    rows += [column(a[name][0].reshape(-1)) for name in ("k_k", "k_a", "r_k", "lnx_g", "lnx_b")]
    rows += [cat([a[name][0]] * 2)[:, None] for name in ("q_norm_g", "k_norm_g")]
    rows.append(a["subln_g"][0][:, None])
    tiles = lambda w: np.ascontiguousarray(w.reshape(w.shape[0] // P, P, w.shape[1] // P, P).transpose(2, 1, 0, 3))
    by_row = lambda w: w.reshape(KT, P, w.shape[1]).transpose(1, 0, 2)
    lora1 = cat([by_row(a["decay_w1"][0, 0]), by_row(a["aaa_a1"][0, 0]), by_row(a["decay_w1"][0, 1]),
                 by_row(a["aaa_a1"][0, 1]), by_row(a["gate_g1"][0])], axis=2)
    second = np.stack([a["decay_w2"][0, 0], a["aaa_a2"][0, 0], a["decay_w2"][0, 1], a["aaa_a2"][0, 1]])
    lora2 = second.reshape(4, HD, FT, P).transpose(2, 1, 0, 3)
    arrays = {
        "x": x, "par": cat(rows, axis=1), "w_in": tiles(a["w_in"][0]), "lora1": lora1, "lora2": lora2,
        "gate2": a["gate_g2"][0], "lambdas": a["diff_lambdas"][0].reshape(-1), "w_out": a["w_out"][0],
        "w_gate": tiles(a["w_gate"][0]), "w_up": tiles(a["w_up"][0]), "w_down": tiles(a["w_down"][0]),
        "small": SMALL_ARRAY, **WIDE,
    }
    return {n: np.ascontiguousarray(v) for n, v in arrays.items()}


def kernel(**inputs):
    import concourse.bacc as _bacc
    from concourse.bass_utils import run_bass_kernel_spmd as _run

    nc = _bacc.Bacc("TRN2", target_bir_lowering=False, num_devices=1)
    arrays = laid_out(inputs)
    dram = {n: nc.dram_tensor(f"in_{n}", a.shape, F32, kind="ExternalInput").ap() for n, a in arrays.items()}
    out = [nc.dram_tensor(f"out_{n}", (1, rows, D), F32, kind="ExternalOutput").ap()
           for n, rows in enumerate((LEN_A - META, LEN_B - META))]
    encoder(nc, Tensors(dram, out))
    r = _run(nc, [{f"in_{n}": a for n, a in arrays.items()}], core_ids=[0])
    return tuple(r.results[0][f"out_{n}"] for n in range(2))
```

```python
import math
from contextlib import ExitStack

import numpy as np

import concourse.bass as bass
from concourse import mybir
from concourse.alu_op_type import AluOpType as ALU

F32 = mybir.dt.float32
F32R = mybir.dt.float32r
ACT = mybir.ActivationFunctionType
AX_X = mybir.AxisListType.X
ds = bass.ds

P = 128
D = 1024
META = 16
LEN_A, LEN_B = META + 256, META + 1024
TOK = LEN_A + LEN_B
KT = D // P
CUTS = (0, 512, 1024, TOK)
TN = len(CUTS) - 1
SPLIT = 5
HALF_COLS = (SPLIT * P, TOK - SPLIT * P)
CH = 64
CH_A, CH_B = -(-LEN_A // CH), -(-LEN_B // CH)
CHUNKS = CH_A + CH_B
PAD_B = CH_A * CH
PTOK = CHUNKS * CH
TT = -(-TOK // P)
RW = 512
FT = RW // P
HEADS = 4
HD = 64
FF = 2816
FFT = FF // P
GL = 160
DECAY = math.exp(-0.5)
LAMBDA_INIT = 0.8 - 0.6 * math.exp(-0.3 * 0)
LEVELS = 5
SEQS = ((0, LEN_A, 0), (LEN_A, LEN_B, PAD_B))

VTILES = [(a + t, min(P, ln - t)) for a, ln, _p in SEQS for t in range(0, ln, P)]
assert [n for _t, n in VTILES] == [P] * 2 + [LEN_A % P] + [P] * 8 + [LEN_B % P]
VRUNS = [(0, 2, P), (2, 3, LEN_A % P), (3, 11, P), (11, 12, LEN_B % P)]

PCOLS = {}
_at = 0
for _name, _n in (("ln1_g", 8), ("ln2_g", 8), ("conv", 36), ("mix_w", 16), ("mix_a", 16), ("mix_g", 8),
                  ("decay_w0", 8), ("aaa_a0", 8), ("k_k", 4), ("k_a", 4), ("r_k", 4), ("lnx_g", 4),
                  ("lnx_b", 4), ("q_norm_g", 1), ("k_norm_g", 1), ("subln_g", 1)):
    PCOLS[_name] = _at
    _at += _n
NPAR = _at


def shape_constants():
    row = np.arange(P)
    h, s = row // CH, row % CH
    t = np.arange(CH)
    eye = np.eye(P, dtype=np.float32)
    block = (row[:, None] // HD == row[None, :] // HD).astype(np.float32)
    out = {"ident": eye, "heads": block}
    own = (h[:, None, None] == np.arange(2)[None, :, None])
    bd = lambda m: (own & m[:, None, :]).reshape(P, P).astype(np.float32)
    out["head_sum"] = block[:, ::HD].copy()
    out["head_mean"] = out["head_sum"] / HD
    out["mean"] = np.full((P, 2), 1 / P, np.float32)
    for d in range(2):
        before = s[:, None] < t[None, :] if d == 0 else s[:, None] > t[None, :]
        after = s[:, None] > t[None, :] if d == 0 else s[:, None] < t[None, :]
        same = s[:, None] == t[None, :]
        out[f"incl{d}"] = (before | same).astype(np.float32)
        out[f"strict_bd{d}"] = bd(before)
        out[f"after_bd{d}"] = bd(after)
        lev = lambda z: (s[:, None] // (2 * z) == t[None, :] // (2 * z)) & (s[:, None] // z != t[None, :] // z)
        out[f"pair_bd{d}"] = bd(lev(1) & before)
        out[f"pairT_bd{d}"] = bd((lev(1) & after) | same)
        for n in range(LEVELS):
            out[f"lev{n}_bd{d}"] = bd((lev(2 << n) & before) | same)
    swap = np.zeros((P, P), np.float32)
    for c in range(2):
        for i in range(8):
            swap[c * HD + 8 + i, c * HD + i] = -1.0
            swap[c * HD + i, c * HD + 8 + i] = 1.0
    out["swap"] = swap
    freqs = (np.float32(500000.0) ** (-np.arange(0, 16, 2, dtype=np.float32) / np.float32(16))).astype(np.float32)
    pos = np.concatenate([np.arange(LEN_A), np.arange(LEN_B)]).astype(np.float32)
    ang = (pos[None, :] * freqs[:, None]).astype(np.float32)
    cos, sin = np.ones((P, TOK), np.float32), np.zeros((P, TOK), np.float32)
    for c in range(2):
        for k in range(2):
            r = c * HD + 8 * k
            cos[r:r + 8], sin[r:r + 8] = np.cos(ang), np.sin(ang)
    first = np.ones((P, CHUNKS, CH), np.float32)
    first[:, :, 0] = 0
    keep = np.ones((P, 2, CHUNKS), np.float32)
    keep[:, 0, [CH_A - 1, CHUNKS - 1]] = 0
    keep[:, 1, [0, CH_A]] = 0
    wide = {"cos": cos, "sin": sin, "first": first.reshape(P, PTOK), "keep": keep.reshape(P, 2 * CHUNKS)}
    return out, wide


SMALL, WIDE = shape_constants()
SCOLS, _at = {}, 0
for _name, _a in SMALL.items():
    SCOLS[_name] = (_at, _a.shape[1])
    _at += _a.shape[1]
NSMALL = _at
SMALL_ARRAY = np.concatenate(list(SMALL.values()), axis=1)
SCRATCH_KIND = "Internal"
PRIMED = 2


class Ctx(ExitStack):

    def __init__(self, nc, stage):
        super().__init__()
        self.nc, self.stage, self.sems = nc, stage, []

    def sb(self, name, shape, dtype=F32):
        return self.enter_context(self.nc.sbuf_tensor(f"{self.stage}_{name}", list(shape), dtype))

    def ps(self, name, shape=(P, 512)):
        return self.enter_context(self.nc.psum_tensor(f"{self.stage}_{name}", list(shape), F32))

    def sem(self, name):
        self.sems.append(self.nc.alloc_semaphore(name=f"{self.stage}_{name}"))
        return self.sems[-1]

    def reset(self):
        self.nc.clear_and_free_semaphores(self.sems)
        self.nc.all_engine_barrier()
        self.sems = []

    def prime(self, eng):
        for sem in self.sems:
            eng.sem_inc(sem, PRIMED)


class Chain:

    def __init__(self, eng, sem, base=0):
        self.eng, self.sem, self.base, self.n = eng, sem, base, 0

    def __call__(self, ins):
        self.n += 1
        ins.then_inc(self.sem, 1)
        self.eng.wait_ge(self.sem, PRIMED + self.base + self.n)


def wide(ap, axis, shape):
    return ap.unsqueeze(axis).to_broadcast(list(shape))


def cut(t, lo, n):
    return t[:, lo:lo + n]


def token_sums(nc, out, squares, head):
    for w in range(TT):
        last = nc.tensor.matmul(out[:, w * head.shape[1]:(w + 1) * head.shape[1]], squares[:, w * P:(w + 1) * P], head,
                                start=True, stop=True)
    return last


def spread(nc, out, values, ident, tokens):
    for w in range(-(-tokens // P)):
        tn = min(P, tokens - w * P)
        last = nc.tensor.matmul(out[:, w * P:w * P + tn], values[:, w * P:(w + 1) * P], ident[:, 0:tn],
                                start=True, stop=True)
    return last


def by_rows(t, heads):
    return t.unsqueeze(2).to_broadcast([P, TT * heads, P // heads])


def three_pass(nc, out, lhsT, rhs, start, stop):
    (lh, ll), (rh, rl) = lhsT, rhs
    nc.tensor.matmul(out, ll, rh, start=start, stop=False)
    nc.tensor.matmul(out, lh, rl, start=False, stop=False)
    return nc.tensor.matmul(out, lh, rh, start=False, stop=stop)


def norm_in(nc, g):
    with Ctx(nc, "n1") as c:
        x = c.sb("x", (P, TT, D))
        xn = c.sb("xn", (P, D))
        ss = c.sb("ss", (P, TT))
        rms = c.sb("rms", (P, TT))
        rstd = c.sb("rstd", (P, TT))
        small = c.sb("ident", (P, P))
        tp = [c.ps("tpa"), c.ps("tpb")]
        loaded, squared, rooted, chain = c.sem("loaded"), c.sem("squared"), c.sem("rooted"), c.sem("chain")
        scaled, turned, taken = c.sem("scaled"), c.sem("turned"), c.sem("taken")
        GROUPS = [(lo, min(lo + 3, TT), c.sem(f"x_loaded{lo}")) for lo in range(0, TT, 3)]
        high, rest = c.sem("high"), c.sem("rest")
        c.callback(c.reset)
        with nc.Block() as block:
            @block.sync
            def _(sp):
                c.prime(sp)
                for lo, hi, sem in GROUPS:
                    sp.dma_start(x[:, lo:hi, :], g.x[lo * P:hi * P, :].rearrange("(t p) d -> p t d", p=P)
                                 ).then_inc(sem, 16)
                sp.dma_start(small[:, :], g.small[:, 0:P]).then_inc(loaded, 16)
                sp.dma_start(g.par_sb[:, :], g.par).then_inc(loaded, 16)

            @block.scalar
            def _(act):
                chained = Chain(act, chain)
                for t in range(TT):
                    for lo, _hi, sem in GROUPS:
                        if t == lo:
                            act.wait_ge(sem, PRIMED + 16)
                    chained(nc.scalar.activation(xn[:, :], x[:, t, :], ACT.Square, accum_out=ss[:, t:t + 1]))
                nc.scalar.copy(xn[:, 0:1], ss[:, 0:1]).then_inc(squared, 1)
                act.wait_ge(squared, PRIMED + 2)
                nc.scalar.activation(rms[:, :], rstd[:, :], ACT.Sqrt).then_inc(rooted, 1)
                with act.Fori(0, TT) as i:
                    act.wait_ge(taken, PRIMED + i + 1)
                    nc.scalar.copy(g.nh[:, :, ds(i * P, P)], g.nT[:, :, ds(i * P, P)]).then_inc(high, 1)

            @block.vector
            def _(dve):
                dve.wait_ge(loaded, PRIMED + 32)
                dve.wait_ge(squared, PRIMED + 1)
                nc.vector.tensor_scalar(rstd[:, :], ss[:, :], 1.0 / D, 1e-6, ALU.mult, ALU.add).then_inc(squared, 1)
                dve.wait_ge(rooted, PRIMED + 1)
                nc.vector.reciprocal(rstd[:, :], rms[:, :]).then_inc(rooted, 1)
                dve.wait_ge(rooted, PRIMED + 2)
                gain = cut(g.par_sb, PCOLS["ln1_g"], KT)

                def remainder(i):
                    dve.wait_ge(high, PRIMED + i + 1)
                    at = ds(i * P, P)
                    nc.vector.tensor_tensor(g.nl[:, :, at], g.nT[:, :, at], g.nh[:, :, at].bitcast(F32), ALU.subtract
                                            ).then_inc(rest, 1)

                def tile(i, first=False):
                    dve.wait_ge(turned, PRIMED + i)
                    nc.vector.tensor_scalar(xn[:, :], x[:, ds(i, 1), :].rearrange("p a d -> p (a d)"),
                                            rstd[:, ds(i, 1)], None, ALU.mult).then_inc(scaled, 1)
                    if not first:
                        remainder(i - 1)
                    dve.wait_ge(turned, PRIMED + i + 1)
                    for b in range(2):
                        last = nc.vector.tensor_tensor(
                            g.nT[:, 4 * b:4 * b + 4, ds(i * P, P)],
                            tp[b][:, :].rearrange("p (k t) -> p k t", k=4),
                            wide(gain[:, 4 * b:4 * b + 4], 2, (P, 4, P)), ALU.mult)
                    last.then_inc(taken, 1)
                tile(0, first=True)
                with dve.Fori(1, TT) as i:
                    tile(i)
                remainder(TT - 1)

            @block.tensor
            def _(pe):
                pe.wait_ge(loaded, PRIMED + 32)
                with pe.Fori(0, TT) as i:
                    pe.wait_ge(scaled, PRIMED + i + 1)
                    pe.wait_ge(taken, PRIMED + i)
                    for k in range(KT):
                        last = nc.tensor.transpose(tp[k // 4][:, (k % 4) * P:(k % 4 + 1) * P],
                                                   xn[:, k * P:(k + 1) * P], small[:, :])
                    last.then_inc(turned, 1)


def project(nc, g):
    MT = 3072 // P
    CONV = 3 * FT
    with Ctx(nc, "pj") as c:
        packed = [c.sb(f"packed{s}", (P, KT, P)) for s in range(2)]
        w = [[c.sb(f"w{s}{part}", (P, KT, P), F32R) for part in ("high", "rest")] for s in range(2)]
        raw = [c.sb(f"raw{s}", (P, TOK)) for s in range(2)]
        mixed = [c.sb(f"mixed{s}", (P, TOK)) for s in range(2)]
        acc = [[c.ps(f"acc{s}{n}") for n in range(TN)] for s in range(2)]
        w_in = [c.sem(f"w_in{s}") for s in range(2)]
        done = [c.sem(f"done{s}") for s in range(2)]
        copied = [c.sem(f"copied{s}") for s in range(2)]
        conved = [c.sem(f"conved{s}") for s in range(2)]
        stored = [c.sem(f"stored{s}") for s in range(2)]
        chain = c.sem("chain")
        cut_high, cut_rest = [[c.sem(f"{n}{s}") for s in range(2)] for n in ("cut_high", "cut_rest")]
        line = lambda t: t[:, :, :].rearrange("p k n -> p (k n)")
        STEPS = MT // 2
        c.callback(c.reset)
        with nc.Block() as block:
            @block.sync
            def _(sp):
                c.prime(sp)
                def load(i, s):
                    sp.wait_ge(cut_rest[s], PRIMED + i)
                    sp.dma_start(packed[s][:, :, :], g.w_in[ds(2 * i + s, 1)].rearrange("a p k n -> (a p) k n")
                                 ).then_inc(w_in[s], 16)

                def store(i, s, conv):
                    if conv:
                        sp.wait_ge(conved[s], PRIMED + i + 1)
                    else:
                        sp.wait_ge(copied[s], PRIMED + TN * i + TN)
                    sp.dma_start(g.proj[ds((2 * i + s) * P, P), :], (mixed if conv else raw)[s][:, :]
                                 ).then_inc(stored[s], 16)
                for s in range(2):
                    load(0, s)
                for conv, lo, hi in ((True, 0, CONV // 2), (False, CONV // 2, STEPS - 1)):
                    with sp.Fori(lo, hi) as i:
                        for s in range(2):
                            load(i + 1, s)
                            store(i, s, conv)
                for s in range(2):
                    store(STEPS - 1, s, False)
                for s in range(2):
                    sp.wait_ge(stored[s], PRIMED + 16 * STEPS)

            @block.tensor
            def _(pe):
                with pe.Fori(0, STEPS) as i:
                    for s in range(2):
                        pe.wait_ge(cut_rest[s], PRIMED + i + 1)
                        for n in range(TN):
                            pe.wait_ge(copied[s], PRIMED + TN * i)
                            for k in range(KT):
                                cols = slice(CUTS[n], CUTS[n + 1])
                                last = three_pass(nc, acc[s][n][:, 0:CUTS[n + 1] - CUTS[n]],
                                                  (w[s][0][:, k, :], w[s][1][:, k, :]),
                                                  (g.nh[:, k, cols], g.nl[:, k, cols]), k == 0, k == KT - 1)
                            last.then_inc(done[s], 1)

            @block.scalar
            def _(act):
                def cut_weights(i, s):
                    act.wait_ge(w_in[s], PRIMED + 16 * i + 16)
                    act.wait_ge(done[s], PRIMED + TN * i)
                    nc.scalar.copy(line(w[s][0]), line(packed[s])).then_inc(cut_high[s], 1)

                def copy_out(i, s):
                    act.wait_ge(stored[s], PRIMED + 16 * i)
                    for n in range(TN):
                        act.wait_ge(done[s], PRIMED + TN * i + n + 1)
                        nc.scalar.copy(raw[s][:, CUTS[n]:CUTS[n + 1]], acc[s][n][:, 0:CUTS[n + 1] - CUTS[n]]
                                       ).then_inc(copied[s], 1)
                for s in range(2):
                    cut_weights(0, s)
                with act.Fori(0, STEPS - 1) as i:
                    for s in range(2):
                        copy_out(i, s)
                        cut_weights(i + 1, s)
                for s in range(2):
                    copy_out(STEPS - 1, s)

            @block.vector
            def _(dve):
                def rest_of_weights(i, s):
                    dve.wait_ge(cut_high[s], PRIMED + i + 1)
                    nc.vector.tensor_tensor(line(w[s][1]), line(packed[s]), line(w[s][0]).bitcast(F32), ALU.subtract
                                            ).then_inc(cut_rest[s], 1)
                for s in range(2):
                    rest_of_weights(0, s)
                with dve.Fori(0, CONV // 2) as i:
                    chained = Chain(dve, chain, i * 6)
                    for s in range(2):
                        dve.wait_ge(copied[s], PRIMED + TN * i + TN)
                        dve.wait_ge(stored[s], PRIMED + 16 * i)
                        tap = lambda n: g.par_sb[:, ds(PCOLS["conv"] + n * CONV + 2 * i + s, 1)]
                        chained(nc.vector.tensor_scalar(mixed[s][:, :], raw[s][:, :], tap(1), None, ALU.mult))
                        for lo, ln, _p in SEQS:
                            last = nc.vector.scalar_tensor_tensor(
                                out=mixed[s][:, lo + 1:lo + ln], in0=raw[s][:, lo:lo + ln - 1], scalar=tap(0),
                                in1=mixed[s][:, lo + 1:lo + ln], op0=ALU.mult, op1=ALU.add)
                            if lo == 0:
                                chained(last)
                        chained(last)
                        for lo, ln, _p in SEQS:
                            last = nc.vector.scalar_tensor_tensor(
                                out=mixed[s][:, lo:lo + ln - 1], in0=raw[s][:, lo + 1:lo + ln], scalar=tap(2),
                                in1=mixed[s][:, lo:lo + ln - 1], op0=ALU.mult, op1=ALU.add)
                        last.then_inc(conved[s], 1)
                        rest_of_weights(i + 1, s)
                with dve.Fori(CONV // 2, STEPS - 1) as i:
                    for s in range(2):
                        rest_of_weights(i + 1, s)


def lora_in(nc, g):
    CASES = [("mix_w", 0), ("mix_a", 0), ("mix_w", 1), ("mix_a", 1), ("mix_g", 0)]
    ORDER = [4, 0, 1, 2, 3]
    with Ctx(nc, "lo") as c:
        delta = c.sb("delta", (P, KT, TOK))
        mixed = [c.sb(f"mixed{s}", (P, TOK)) for s in range(2)]
        w = c.sb("w", (P, KT, 4 * HD + GL))
        acc = [c.ps(f"acc{n}") for n in range(TN)]
        acc2 = [c.ps(f"acc2{n}") for n in range(TN)]
        loaded, mixed_s, copied, chain = c.sem("loaded"), c.sem("mixed_s"), c.sem("copied"), c.sem("chain")
        zeroed, stored = c.sem("zeroed"), c.sem("stored")
        hidg = c.sb("hidg", (P, 2, PTOK))
        used = [c.sem(f"used{s}") for s in range(2)]
        cols = [(0, HD), (HD, HD), (2 * HD, HD), (3 * HD, HD), (4 * HD, GL)]
        c.callback(c.reset)
        with nc.Block() as block:
            @block.sync
            def _(sp):
                c.prime(sp)
                sp.dma_start(w[:, :, :], g.lora1).then_inc(loaded, 16)
                sp.wait_ge(copied, PRIMED + 5)
                sp.wait_ge(zeroed, PRIMED + 2)
                sp.dma_start(g.hidg_dram[:, 0, :], hidg[:, 0, :]).then_inc(stored, 16)
                sp.dma_start(g.hidg_dram[0:GL - P, 1, :], hidg[0:GL - P, 1, :]).then_inc(stored, 16)
                sp.wait_ge(stored, PRIMED + 32)

            @block.gpsimd
            def _(pool):
                for t in (g.hid, hidg):
                    nc.gpsimd.memset(t[:, :, LEN_A:PAD_B], 0.0)
                    nc.gpsimd.memset(t[:, :, PAD_B + LEN_B:PTOK], 0.0).then_inc(zeroed, 1)

            @block.vector
            def _(dve):
                nT = g.nT
                tile = lambda t, k: t[:, ds(k, 1), 0:TOK].rearrange("p a t -> p (a t)")

                def difference(k):
                    chained = Chain(dve, chain, 2 * k)
                    d, x = tile(delta, k), tile(nT, k)
                    for lo, ln, _p in SEQS:
                        hi = lo + ln
                        nc.vector.tensor_tensor(d[:, lo + 1:hi - 1], x[:, lo:hi - 2], x[:, lo + 2:hi], ALU.add)
                        nc.vector.tensor_copy(d[:, lo:lo + 1], x[:, lo + 1:lo + 2])
                        last = nc.vector.tensor_copy(d[:, hi - 1:hi], x[:, hi - 2:hi - 1])
                    chained(last)
                    chained(nc.vector.scalar_tensor_tensor(out=d, in0=d, scalar=0.5, in1=x, op0=ALU.mult,
                                                           op1=ALU.subtract))
                for turn, m in enumerate(ORDER):
                    mix, d = CASES[m]
                    with dve.Fori(0, KT // 2) as i:
                        for s in range(2):
                            if turn == 0:
                                difference(2 * i + s)
                            dve.wait_ge(used[s], PRIMED + turn * (KT // 2) + i)
                            nc.vector.scalar_tensor_tensor(
                                out=mixed[s][:, :], in0=tile(delta, 2 * i + s),
                                scalar=g.par_sb[:, ds(PCOLS[mix] + d * KT + 2 * i + s, 1)],
                                in1=tile(nT, 2 * i + s), op0=ALU.mult, op1=ALU.add).then_inc(mixed_s, 1)

            @block.tensor
            def _(pe):
                pe.wait_ge(loaded, PRIMED + 16)
                for turn, m in enumerate(ORDER):
                    lo, wd = cols[m]
                    if turn:
                        pe.wait_ge(copied, PRIMED + turn)
                    for k in range(KT):
                        pe.wait_ge(mixed_s, PRIMED + turn * KT + k + 1)
                        for n in range(TN):
                            for a, (off, rows) in enumerate(((0, min(wd, P)), (P, wd - P))):
                                if rows <= 0:
                                    continue
                                last = nc.tensor.matmul((acc, acc2)[a][n][0:rows, 0:CUTS[n + 1] - CUTS[n]],
                                                        w[:, k, lo + off:lo + off + rows],
                                                        mixed[k % 2][:, CUTS[n]:CUTS[n + 1]],
                                                        start=(k == 0), stop=(k == KT - 1))
                        last.then_inc(used[k % 2], 1)

            @block.scalar
            def _(act):
                for turn, m in enumerate(ORDER):
                    act.wait_ge(used[1], PRIMED + (turn + 1) * (KT // 2))
                    wd = cols[m][1]
                    func = (ACT.Tanh, ACT.Copy, ACT.Tanh, ACT.Copy, ACT.Sigmoid)[m]
                    parts = [(g.hid[:, m, :], acc, HD)] if m < 4 else [(hidg[:, 0, :], acc, P),
                                                                       (hidg[0:GL - P, 1, :], acc2, GL - P)]
                    for dst, ps, rows in parts:
                        for n in range(TN):
                            lo = CUTS[n]
                            for a, ln, p in SEQS:
                                x0, x1 = max(lo, a), min(CUTS[n + 1], a + ln)
                                if x0 < x1:
                                    last = nc.scalar.activation(dst[:, p + x0 - a:p + x1 - a],
                                                                ps[n][0:rows, x0 - lo:x1 - lo], func)
                    last.then_inc(copied, 1)


def prep(nc, g):
    with Ctx(nc, "pr") as c:
        slots = lambda name: [c.sb(f"{name}{s}", (P, PTOK)) for s in range(2)]
        r, k, v = slots("r"), slots("k"), slots("v")
        w2 = [c.sb(f"w2{s}", (HD, 4, P)) for s in range(2)]
        heads, head_sum, ident = c.sb("heads", (P, P)), c.sb("head_sum", (P, 2)), c.sb("ident", (P, P))
        first = c.sb("first", (P, PTOK))
        keep = c.sb("keep", (P, 2, CHUNKS))
        q, kk, kds = c.sb("q", (P, PTOK)), c.sb("kk", (P, PTOK)), c.sb("kds", (P, PTOK))
        sg, av, cs, ex, kd = (slots(n) for n in ("sg", "av", "cs", "ex", "kd"))
        e1 = c.sb("e1", (P, PTOK))
        tot = c.sb("tot", (P, 2, CHUNKS))
        st = c.sb("st", (P, 2, 2 * TT))
        sx = [c.sb(f"sx{d}", (P, CHUNKS, 5, CH)) for d in range(2)]
        psa, psb, psq = c.ps("psa", (P, 3 * 512)), c.ps("psb", (P, 3 * 512)), c.ps("psq")
        consts, zeroed = c.sem("consts"), c.sem("zeroed")
        loaded = [c.sem(f"loaded{s}") for s in range(2)]
        squared, sums, floored, rooted, inverted, rows, spreads, normed = (
            c.sem(n) for n in ("squared", "sums", "floored", "rooted", "inverted", "rows", "spreads", "normed"))
        scaled_r, bonus, stored = c.sem("scaled_r"), c.sem("bonus"), c.sem("stored")
        products = c.sem("products")
        sig_w, sig_a, summed, exped = c.sem("sig_w"), c.sem("sig_a"), c.sem("summed"), c.sem("exped")
        vcopied, ready, chain = c.sem("vcopied"), c.sem("ready"), c.sem("chain")
        par = lambda name, off: cut(g.par_sb, PCOLS[name] + off, 1)
        chunked = lambda t: t[:, :].rearrange("p (c t) -> p c t", t=CH)
        c.callback(c.reset)
        with nc.Block() as block:
            @block.sync
            def _(sp):
                c.prime(sp)
                sp.dma_start(heads[:, :], g.small_of("heads")).then_inc(consts, 16)
                sp.dma_start(head_sum[:, :], g.small_of("head_sum")).then_inc(consts, 16)
                sp.dma_start(ident[:, :], g.small_of("ident")).then_inc(consts, 16)
                sp.dma_start(first[:, :], g.first).then_inc(consts, 16)
                sp.dma_start(keep[:, :, :], g.keep.rearrange("p (d c) -> p d c", d=2)).then_inc(consts, 16)
                sp.wait_ge(zeroed, PRIMED + 6)

                def load(f):
                    s = f % 2
                    if f >= 2:
                        sp.wait_ge(bonus, PRIMED + f - 1)
                    for n, t in enumerate((k, r, v)):
                        for a, ln, p in SEQS:
                            row = ((1, 0, 2)[n] * FT + f) * P
                            sp.dma_start(t[s][:, p:p + ln], g.proj[row:row + P, a:a + ln]).then_inc(loaded[s], 16)
                    sp.dma_start(w2[s][:, :, :], g.lora2[f]).then_inc(loaded[s], 16)
                load(0)
                for f in range(FT):
                    if f + 1 < FT:
                        load(f + 1)
                    for d in range(2):
                        sp.wait_ge(ready, PRIMED + 2 * f + d + 1)
                        sp.wait_ge(vcopied, PRIMED + 2 * f + d + 1)
                        sp.dma_start(g.sx[d, f], sx[d][:, :, :, :].rearrange("p c x t -> p (c x t)")).then_inc(stored, 16)
                    sp.wait_ge(bonus, PRIMED + f + 1)
                    sp.dma_start(g.bonus[f * P:(f + 1) * P, :], kds[:, :]).then_inc(stored, 16)
                sp.wait_ge(stored, PRIMED + 48 * FT)

            @block.gpsimd
            def _(pool):
                for t in (*r, *k, *v):
                    for a, ln, p in SEQS:
                        last = nc.gpsimd.memset(t[:, p + ln:PAD_B if p == 0 else PTOK], 0.0)
                    last.then_inc(zeroed, 1)

            @block.tensor
            def _(pe):
                def product(ps, lhsT, rhs, sem):
                    for lo in range(0, PTOK, 512):
                        hi = min(lo + 512, PTOK)
                        last = nc.tensor.matmul(ps[:, lo:hi], lhsT, rhs[:, lo:hi], start=True, stop=True)
                    last.then_inc(sem, 1)

                def square_sums(f):
                    pe.wait_ge(squared, PRIMED + f + 1)
                    pe.wait_ge(floored, PRIMED + f)
                    token_sums(nc, psq, q, head_sum[:, :]).then_inc(sums, 1)

                def spread_norms(f):
                    pe.wait_ge(rows, PRIMED + f + 1)
                    pe.wait_ge(sig_a, PRIMED + 2 * f)
                    spread(nc, psa, q, ident, PTOK).then_inc(spreads, 1)
                pe.wait_ge(consts, PRIMED + 80)
                square_sums(0)
                spread_norms(0)
                for f in range(FT):
                    s = f % 2
                    pe.wait_ge(loaded[s], PRIMED + 112 * (f // 2) + 112)
                    pe.wait_ge(bonus, PRIMED + f)
                    product(psb, w2[s][:, 0, :], g.hid[:, 0, :], products)
                    pe.wait_ge(normed, PRIMED + f + 1)
                    product(psa, w2[s][:, 1, :], g.hid[:, 1, :], products)
                    pe.wait_ge(sig_w, PRIMED + 2 * f + 1)
                    product(psb, w2[s][:, 2, :], g.hid[:, 2, :], products)
                    pe.wait_ge(sig_a, PRIMED + 2 * f + 1)
                    product(psa, w2[s][:, 3, :], g.hid[:, 3, :], products)
                    if f + 1 < FT:
                        square_sums(f + 1)
                    pe.wait_ge(sig_w, PRIMED + 2 * f + 2)
                    pe.wait_ge(scaled_r, PRIMED + f + 1)
                    product(psb, heads[:, :], kds, products)
                    if f + 1 < FT:
                        spread_norms(f + 1)

            @block.scalar
            def _(act):
                def square(f):
                    act.wait_ge(loaded[f % 2], PRIMED + 112 * (f // 2) + 112)
                    act.wait_ge(spreads, PRIMED + f)
                    nc.scalar.activation(q[:, :], k[f % 2][:, :], ACT.Square, scale=par("k_k", f)).then_inc(squared, 1)

                def root(f):
                    act.wait_ge(floored, PRIMED + f + 1)
                    nc.scalar.activation(st[:, 0, :], st[:, 0, :], ACT.Sqrt).then_inc(rooted, 1)

                def to_rows(f):
                    act.wait_ge(inverted, PRIMED + f + 1)
                    nc.scalar.copy(q[:, :].rearrange("p (a b) -> p a b", b=HD), by_rows(st[:, 1, :], 2)).then_inc(rows, 1)
                square(0)
                root(0)
                to_rows(0)
                for f in range(FT):
                    ahead = f + 1 < FT
                    for d in range(2):
                        act.wait_ge(products, PRIMED + 5 * f + 2 * d + 1)
                        nc.scalar.activation(sg[d][:, :], psb[:, 0:PTOK], ACT.Sigmoid, bias=par("decay_w0", d * FT + f)
                                             ).then_inc(sig_w, 1)
                        act.wait_ge(products, PRIMED + 5 * f + 2 * d + 2)
                        nc.scalar.activation(av[d][:, :], psa[:, 0:PTOK], ACT.Sigmoid, bias=par("aaa_a0", d * FT + f)
                                             ).then_inc(sig_a, 1)
                    act.wait_ge(stored, PRIMED + 48 * f)
                    for d in range(2):
                        nc.scalar.copy(sx[d][:, :, 4, :], chunked(v[f % 2])).then_inc(vcopied, 1)
                    if ahead:
                        square(f + 1)
                    for d in range(2):
                        act.wait_ge(summed, PRIMED + 2 * f + d + 1)
                        if d:
                            act.wait_ge(ready, PRIMED + 2 * f + 1)
                        nc.scalar.activation(tot[:, d, :], tot[:, d, :], ACT.Exp, scale=-DECAY)
                        nc.scalar.activation(e1[:, :], cs[d][:, :], ACT.Exp, scale=-DECAY).then_inc(exped, 1)
                        nc.scalar.activation(ex[d][:, :], ex[d][:, :], ACT.Exp, scale=-DECAY).then_inc(exped, 1)
                        nc.scalar.activation(cs[d][:, :], cs[d][:, :], ACT.Exp, scale=DECAY).then_inc(exped, 1)
                    if ahead:
                        root(f + 1)
                        to_rows(f + 1)

            @block.vector
            def _(dve):
                def floor(f):
                    dve.wait_ge(sums, PRIMED + f + 1)
                    nc.vector.tensor_scalar(st[:, 0, :], psq[:, 0:2 * TT], 1e-24, None, ALU.max).then_inc(floored, 1)

                def invert(f):
                    dve.wait_ge(rooted, PRIMED + f + 1)
                    nc.vector.reciprocal(st[:, 1, :], st[:, 0, :]).then_inc(inverted, 1)
                dve.wait_ge(consts, PRIMED + 80)
                LINKS = 5
                floor(0)
                invert(0)
                for f in range(FT):
                    s = f % 2
                    chained = Chain(dve, chain, f * LINKS)
                    dve.wait_ge(ready, PRIMED + 2 * f)
                    dve.wait_ge(spreads, PRIMED + f + 1)
                    last = nc.vector.scalar_tensor_tensor(out=kk[:, :], in0=k[s][:, :], scalar=par("k_k", f),
                                                          in1=psa[:, 0:PTOK], op0=ALU.mult, op1=ALU.mult)
                    last.then_inc(normed, 1)
                    dve.wait_ge(normed, PRIMED + f + 1)
                    for d in range(2):
                        dve.wait_ge(sig_w, PRIMED + 2 * f + d + 1)
                        dve.wait_ge(sig_a, PRIMED + 2 * f + d + 1)
                        c3 = chunked(cs[d])
                        nc.vector.tensor_scalar(kd[d][:, :], av[d][:, :], -1.0, par("k_a", f), ALU.add, ALU.mult)
                        chained(nc.vector.tensor_tensor_scan(cs[d][:, :], first[:, :], sg[d][:, :], 0.0,
                                                             ALU.mult, ALU.add))
                        nc.vector.tensor_copy(tot[:, d, :].unsqueeze(2), c3[:, :, CH - 1:CH])
                        if d == 0:
                            nc.vector.tensor_tensor(ex[d][:, :], cs[d][:, :], sg[d][:, :], ALU.subtract
                                                    ).then_inc(summed, 1)
                        else:
                            chained(nc.vector.tensor_tensor(chunked(ex[d]), c3[:, :, CH - 1:CH].to_broadcast([P, CHUNKS, CH]),
                                                            c3, ALU.subtract))
                            nc.vector.tensor_tensor(cs[d][:, :], ex[d][:, :], sg[d][:, :], ALU.add
                                                    ).then_inc(summed, 1)
                        last = nc.vector.scalar_tensor_tensor(out=kd[d][:, :], in0=kd[d][:, :], scalar=1.0,
                                                              in1=k[s][:, :], op0=ALU.add, op1=ALU.mult)
                        nc.vector.tensor_tensor(av[d][:, :], kk[:, :], av[d][:, :], ALU.mult)
                    chained(last)
                    dve.wait_ge(stored, PRIMED + 48 * f)
                    chained(nc.vector.tensor_tensor(kds[:, :], kd[0][:, :], kd[1][:, :], ALU.add))
                    nc.vector.scalar_tensor_tensor(out=kds[:, :], in0=r[s][:, :], scalar=par("r_k", f), in1=kds[:, :],
                                                   op0=ALU.mult, op1=ALU.mult).then_inc(scaled_r, 1)
                    for d in range(2):
                        dve.wait_ge(exped, PRIMED + 6 * f + 3 * d + 3)
                        o = lambda x: sx[d][:, :, x, :]
                        nc.vector.tensor_tensor(g.etot[:, d, f, :], tot[:, d, :], keep[:, d, :], ALU.mult)
                        nc.vector.tensor_tensor(o(0), chunked(r[s]), chunked(e1), ALU.mult)
                        nc.vector.scalar_tensor_tensor(out=o(1), in0=chunked(kk), scalar=-1.0, in1=chunked(ex[d]),
                                                       op0=ALU.mult, op1=ALU.mult)
                        nc.vector.tensor_tensor(o(2), chunked(av[d]), chunked(cs[d]), ALU.mult)
                        nc.vector.tensor_tensor(o(3), chunked(kd[d]), chunked(cs[d]), ALU.mult).then_inc(ready, 1)
                        if f + 1 < FT:
                            (floor, invert)[d](f + 1)
                    dve.wait_ge(products, PRIMED + 5 * f + 5)
                    nc.vector.tensor_tensor(kds[:, :], psb[:, 0:PTOK], v[s][:, :], ALU.mult).then_inc(bonus, 1)
                    assert chained.n == LINKS


def chunks(nc, g):
    J = 2
    PASSES = FT // J
    LOADS = (0, 3, CHUNKS // 2 + 2, CHUNKS)
    PAIRS = (CHUNKS - 2) // 2
    with Ctx(nc, "ch") as c:
        masks = c.sb("masks", (P, NSMALL))
        mask = {n: masks[:, lo:lo + wd] for n, (lo, wd) in SCOLS.items()}
        per_d = lambda name, shape: [c.sb(f"{name}{d}", shape) for d in range(2)]
        slots = lambda name, shape: [[c.sb(f"{name}{d}{s}", shape) for s in range(2)] for d in range(2)]
        sx = per_d("sx", (P, J, CHUNKS, 5, CH))
        ys = per_d("ys", (P, J, PTOK))
        bka = per_d("bka", (P, J, P))
        e_d = per_d("ed", (P, 2, J, P))
        xbd = per_d("xbd", (P, J, P))
        bbd, ubd = per_d("bbd", (P, J, P)), per_d("ubd", (P, J, P))
        sst, snw = per_d("sst", (P, J, P)), per_d("snw", (P, J, P))
        ops = slots("ops", (P, J, 4, 2, CH))
        ebd, akT = slots("ebd", (P, J, P)), slots("akT", (P, J, P))
        arT = slots("arT", (P, J, 2, CH))
        bkt = slots("bkt", (P, J, 2, P))
        vbd = slots("vbd", (P, J, P))
        bank = lambda name: [c.ps(f"{name}{d}") for d in range(2)]
        psa = bank("psa")
        psm = bank("psm")
        pse = bank("pse")
        pss = bank("pss")
        consts, zeroed, stored = c.sem("consts"), c.sem("zeroed"), c.sem("stored")
        loaded = [c.sem(f"loaded{h}") for h in range(3)]
        two = lambda name: [c.sem(f"{name}{d}") for d in range(2)]
        staged, first_products, a_read, v_copied = two("staged"), two("first"), two("a_read"), two("v_copied")
        turned, prepared = two("turned"), two("prepared")
        b_ready, b_copied, u_ready, u_copied = two("b_ready"), two("b_copied"), two("u_ready"), two("u_copied")
        y_ready, s_read, y_copied, s_new = two("y_ready"), two("s_read"), two("y_copied"), two("s_new")
        chain = two("chain")
        z_ready, x_ready, e_ready, e_copied = two("z_ready"), two("x_ready"), two("e_ready"), two("e_copied")
        pair = lambda ap: ap.rearrange("p (j t) -> p j t", j=J)
        halves = lambda ap: ap.rearrange("p j (h t) -> p j h t", h=2)
        flat = lambda ap: ap.rearrange("p a b -> p (a b)")

        def at(d, n):
            return n if d == 0 else n * -1 + (CHUNKS - 1)

        nothing = lambda d, k, n, slot: None

        def weave(eng, p, stages, between=None, ahead=nothing):
            pre, level, b_step, u_step, y_step = stages

            def one(place, d, n, slot, second, first=False, last=False):
                k = p * CHUNKS + n
                if not second:
                    if place == 0:
                        pre(d, k, n, slot)
                    levels = {3: 0, 4: 1, 5: 2, 6: 3, 8: 4}
                else:
                    levels = {1: 5, 4: 6, 5: 7, 6: 8, 7: 9}
                if place in levels:
                    level(d, k, n, slot, levels[place])
                if not second and place == 3 and not first:
                    b_step(d, k - 1, n - 1, 1 - slot)
                if not second and place == 7 and not first:
                    u_step(d, k - 1, n - 1, 1 - slot)
                if second and place == 2:
                    if not last:
                        ahead(d, k + 1, n + 1, 1 - slot)
                    if not first:
                        y_step(d, k - 1, n - 1, 1 - slot)

            def together(*halves):
                for place in range(9):
                    for d, n, slot, second, edge in halves:
                        one(place, d, n, slot, second, **edge)

            FIRST, LAST, INNER = {"first": True}, {"last": True}, {}

            def step(n, slot, last=False):
                together((0, n, slot, False, INNER), (1, n - 1, 1 - slot, True, INNER))
                together((0, n, slot, True, LAST if last else INNER), (1, n, slot, False, INNER))
            together((0, 0, 0, False, FIRST))
            together((0, 0, 0, True, FIRST), (1, 0, 0, False, FIRST))
            if between:
                between(p, 0)
            together((0, 1, 1, False, INNER), (1, 0, 0, True, FIRST))
            together((0, 1, 1, True, INNER), (1, 1, 1, False, INNER))
            for h, (lo, hi) in enumerate(((1, 1 + PAIRS // 2), (1 + PAIRS // 2, PAIRS))):
                if between:
                    between(p, h + 1)
                with eng.Fori(lo, hi) as m:
                    step(2 * m, 0)
                    step(2 * m + 1, 1)
            step(CHUNKS - 2, 0)
            step(CHUNKS - 1, 1, last=True)
            together((1, CHUNKS - 1, 1, True, LAST))
            for q in (b_step, u_step, y_step):
                for d in range(2):
                    q(d, p * CHUNKS + CHUNKS - 1, CHUNKS - 1, 1)

        with nc.Block() as block:
            @block.sync
            def _(sp):
                c.prime(sp)
                sp.dma_start(masks[:, :], g.small).then_inc(consts, 16)
                for p in range(PASSES):
                    for h, (lo, hi) in enumerate(zip(LOADS, LOADS[1:])):
                        for d in range(2):
                            if p:
                                sp.wait_ge(y_ready[d], PRIMED + (p - 1) * CHUNKS + LOADS[h + 1])
                            lo, hi = LOADS[h:h + 2]
                            if d:
                                lo, hi = CHUNKS - hi, CHUNKS - lo
                            for j in range(J):
                                sp.dma_start(sx[d][:, j, lo:hi].rearrange("p c x t -> p (c x t)"),
                                             g.sx[d, p * J + j][:, lo * 5 * CH:hi * 5 * CH]).then_inc(loaded[h], 16)
                    for d in range(2):
                        sp.wait_ge(y_copied[d], PRIMED + (p + 1) * CHUNKS)
                        for j in range(J):
                            sp.dma_start(g.ydir[d, p * J + j], ys[d][:, j, :]).then_inc(stored, 16)
                sp.wait_ge(stored, PRIMED + 32 * J * PASSES)

            @block.gpsimd
            def _(pool):
                for d in range(2):
                    for t in (ops[d][0], ops[d][1], sst[d]):
                        nc.gpsimd.memset(t[:], 0.0).then_inc(zeroed, 1)

            @block.scalar
            def _(act):
                copy = nc.scalar.copy

                def stage(d, k, n, slot):
                    act.wait_ge(b_ready[d], PRIMED + k - 1)
                    for h in range(2):
                        rows = slice(h * CH, h * CH + CH)
                        for j in range(J):
                            src = sx[d][rows, j, ds(at(d, n), 1), :, :].rearrange("p a x t -> p (a x) t")
                            last = copy(ops[d][slot][rows, j, :, h, :], src[:, 1:5, :])
                    last.then_inc(staged[d], 1)

                def pre(d, k, n, slot):
                    act.wait_ge(first_products[d], PRIMED + k + 1)
                    act.wait_ge(y_ready[d], PRIMED + k - 1)
                    copy(bkt[d][slot][:, :, :, :].rearrange("p j x t -> p (j x t)"), pse[d][:, :]
                         ).then_inc(turned[d], 1)
                    act.wait_ge(a_read[d], PRIMED + k + 1)
                    copy(flat(vbd[d][slot][:, :, :]), psm[d][:, J * P:2 * J * P]).then_inc(v_copied[d], 1)

                def level(d, k, n, slot, w):
                    if w % 2:
                        act.wait_ge(e_ready[d], PRIMED + LEVELS * k + w // 2 + 1)
                        if w // 2 < LEVELS - 1:
                            copy(e_d[d][:, :, :, :].rearrange("p e j t -> p (e j t)"), pse[d][:, :]
                                 ).then_inc(e_copied[d], 1)
                        else:
                            copy(flat(ebd[d][slot][:, :, :]), pse[d][:, 0:J * P]).then_inc(e_copied[d], 1)

                def b_copy(d, k, n, slot):
                    act.wait_ge(b_ready[d], PRIMED + k + 1)
                    copy(flat(bbd[d][:, :, :]), pss[d][:, 0:J * P]).then_inc(b_copied[d], 1)

                def y_copy(d, k, n, slot):
                    act.wait_ge(s_read[d], PRIMED + k + 1)
                    copy(ys[d][:, :, ds(at(d, n) * CH, CH)], pair(pss[d][:, J * P:J * P + J * CH])
                         ).then_inc(y_copied[d], 1)

                def between(p, h):
                    if h == 0:
                        act.wait_ge(stored, PRIMED + 32 * J * p)
                    else:
                        act.wait_ge(loaded[h], PRIMED + 32 * J * (p + 1))
                act.wait_ge(zeroed, PRIMED + 6)
                with act.Fori(0, PASSES) as p:
                    act.wait_ge(loaded[0], PRIMED + 32 * J * (p + 1))
                    for d in range(2):
                        stage(d, p * CHUNKS, 0, 0)
                    weave(act, p, (pre, level, b_copy, nothing, y_copy), between, ahead=stage)

            @block.tensor
            def _(pe):
                pe.wait_ge(consts, PRIMED + 16)
                mm = nc.tensor.matmul

                def of(d, n, j, lo, hi):
                    return sx[d][:, j, ds(at(d, n), 1), lo:hi, :].rearrange("p a x t -> p (a x t)")

                def pre(d, k, n, slot):
                    pe.wait_ge(prepared[d], PRIMED + k)
                    pe.wait_ge(x_ready[d], PRIMED + LEVELS * k)
                    pe.wait_ge(e_copied[d], PRIMED + LEVELS * k)
                    pe.wait_ge(staged[d], PRIMED + k + 1)
                    for j in range(J):
                        a, b, kx, v = (flat(ops[d][slot][:, j, x]) for x in range(4))
                        mm(psm[d][:, j * P:(j + 1) * P], a, b, start=True, stop=True)
                        nc.tensor.transpose(psm[d][:, (J + j) * P:(J + j + 1) * P], v, mask["ident"])
                        for x, lhsT in enumerate((b, kx)):
                            mm(psa[d][:, (2 * j + x) * P:(2 * j + x + 1) * P], lhsT, of(d, n, j, 0, 2),
                               start=True, stop=True)
                            last = nc.tensor.transpose(pse[d][:, (2 * j + x) * P:(2 * j + x + 1) * P], lhsT,
                                                       mask["ident"])
                    last.then_inc(first_products[d], 1)

                def level(d, k, n, slot, w):
                    lev = w // 2
                    if w % 2 == 0:
                        if lev == 0:
                            pe.wait_ge(v_copied[d], PRIMED + k + 1)
                            pe.wait_ge(turned[d], PRIMED + k + 1)
                            pe.wait_ge(prepared[d], PRIMED + k + 1)
                        else:
                            pe.wait_ge(e_copied[d], PRIMED + LEVELS * k + lev)
                        for j in range(J):
                            last = mm(psm[d][:, j * P:(j + 1) * P], bka[d][:, j, :], e_d[d][:, 0, j, :],
                                      start=True, stop=True)
                        last.then_inc(z_ready[d], 1)
                    else:
                        pe.wait_ge(x_ready[d], PRIMED + LEVELS * k + lev + 1)
                        for j in range(J):
                            eT = e_d[d][:, 1, j, :]
                            last = mm(pse[d][:, j * P:(j + 1) * P], eT, xbd[d][:, j, :], start=True, stop=True)
                            if lev < LEVELS - 1:
                                last = mm(pse[d][:, (J + j) * P:(J + j + 1) * P], xbd[d][:, j, :], eT,
                                          start=True, stop=True)
                        last.then_inc(e_ready[d], 1)

                def b_step(d, k, n, slot):
                    pe.wait_ge(s_new[d], PRIMED + k)
                    pe.wait_ge(y_copied[d], PRIMED + k)
                    for j in range(J):
                        o = pss[d][:, j * P:(j + 1) * P]
                        mm(o, akT[d][slot][:, j, :], vbd[d][slot][:, j, :], start=True, stop=False)
                        last = mm(o, flat(ops[d][slot][:, j, 0]), sst[d][:, j, :], start=False, stop=True)
                    last.then_inc(b_ready[d], 1)

                def u_step(d, k, n, slot):
                    pe.wait_ge(b_copied[d], PRIMED + k + 1)
                    for j in range(J):
                        last = mm(pss[d][:, j * P:(j + 1) * P], ebd[d][slot][:, j, :], bbd[d][:, j, :],
                                  start=True, stop=True)
                    last.then_inc(u_ready[d], 1)

                def y_step(d, k, n, slot):
                    pe.wait_ge(u_copied[d], PRIMED + k + 1)
                    for j in range(J):
                        o = pss[d][:, J * P + j * CH:J * P + (j + 1) * CH]
                        v, u = vbd[d][slot][:, j, :], ubd[d][:, j, :]
                        mm(o, v, arT[d][slot][:, j, 1, :], start=True, stop=False)
                        mm(o, u, arT[d][slot][:, j, 0, :], start=False, stop=False)
                        mm(o, sst[d][:, j, :], of(d, n, j, 0, 1), start=False, stop=True)
                        o = pss[d][:, j * P:(j + 1) * P]
                        mm(o, bkt[d][slot][:, j, 0, :], u, start=True, stop=False)
                        last = mm(o, bkt[d][slot][:, j, 1, :], v, start=False, stop=True)
                    last.then_inc(y_ready[d], 1)
                with pe.Fori(0, PASSES) as p:
                    weave(pe, p, (pre, level, b_step, u_step, y_step))

            @block.vector
            def _(dve):
                tt = nc.vector.tensor_tensor
                both = lambda name: wide(mask[name], 1, (P, J, P))

                def blocks(out, src, name):
                    return tt(halves(out), wide(src, 2, (P, J, 2, CH)),
                              wide(mask[name].rearrange("p (h t) -> p h t", h=2), 1, (P, J, 2, CH)), ALU.mult)

                def pre(d, k, n, slot):
                    chained = Chain(dve, chain[d], k * 2)
                    dve.wait_ge(first_products[d], PRIMED + k + 1)
                    dve.wait_ge(y_ready[d], PRIMED + k - 1)
                    ps_a = psa[d][:, :].rearrange("p (j x y t) -> p j x y t", j=J, x=2, y=2)
                    e, eT = e_d[d][:, 0, :, :], e_d[d][:, 1, :, :]
                    tt(bka[d][:, :, :], pair(psm[d][:, 0:J * P]), both(f"after_bd{d}"), ALU.mult
                       ).then_inc(a_read[d], 1)
                    chained(blocks(e, ps_a[:, :, 0, 1, :], f"pair_bd{d}"))
                    chained(tt(bka[d][:, :, :], bka[d][:, :, :], both("ident"), ALU.add))
                    tt(e, e, both("ident"), ALU.add)
                    tt(eT, bka[d][:, :, :], both(f"pairT_bd{d}"), ALU.mult)
                    blocks(akT[d][slot][:, :, :], ps_a[:, :, 1, 1, :], f"strict_bd{d}")
                    tt(arT[d][slot][:, :, :, :], ps_a[:, :, :, 0, :],
                       mask[f"incl{d}"].unsqueeze(1).unsqueeze(1).to_broadcast([P, J, 2, CH]), ALU.mult
                       ).then_inc(prepared[d], 1)

                def level(d, k, n, slot, w):
                    if w % 2 == 0:
                        dve.wait_ge(z_ready[d], PRIMED + LEVELS * k + w // 2 + 1)
                        tt(xbd[d][:, :, :], pair(psm[d][:, 0:J * P]), both(f"lev{w // 2}_bd{d}"), ALU.mult
                           ).then_inc(x_ready[d], 1)

                def u_copy(d, k, n, slot):
                    dve.wait_ge(u_ready[d], PRIMED + k + 1)
                    nc.vector.tensor_copy(ubd[d][:, :, :], pair(pss[d][:, 0:J * P])).then_inc(u_copied[d], 1)

                def state(d, k, n, slot):
                    dve.wait_ge(y_ready[d], PRIMED + k + 1)
                    tt(snw[d][:, :, :], pair(pss[d][:, 0:J * P]), sst[d][:, :, :], ALU.add
                       ).then_inc(s_read[d], 1)
                    dve.wait_ge(s_read[d], PRIMED + k + 1)
                    tt(sst[d][:, :, :], snw[d][:, :, :],
                       g.etot[:, d, ds(p * J, J), ds(at(d, n), 1)].to_broadcast([P, J, P]), ALU.mult
                       ).then_inc(s_new[d], 1)
                dve.wait_ge(consts, PRIMED + 16)
                dve.wait_ge(zeroed, PRIMED + 6)
                with dve.Fori(0, PASSES) as p:
                    weave(dve, p, (pre, level, nothing, u_copy, state))


def mix_out(nc, g):
    with Ctx(nc, "mo") as c:
        of_tiles = lambda name: [c.sb(f"{name}{f}", (P, PTOK)) for f in range(FT)]
        y0, y1, bon = of_tiles("y0"), of_tiles("y1"), of_tiles("bon")
        sq, rows = c.sb("sq", (P, PTOK)), c.sb("rows", (P, PTOK))
        st = c.sb("st", (P, 2, 2 * TT))
        heads, head_mean, ident = c.sb("heads", (P, P)), c.sb("head_mean", (P, 2)), c.sb("ident", (P, P))
        zero = c.sb("zero", (P, KT, TT * P - TOK))
        hidg, w2 = c.sb("hidg", (P, 2, PTOK)), c.sb("w2", (P, 2, RW))
        psa, psb, psq = c.ps("psa", (P, 3 * 512)), c.ps("psb", (P, 3 * 512)), c.ps("psq")
        consts, gate_in, pads, zeroed, stored = (c.sem(n) for n in ("consts", "gate_in", "pads", "zeroed", "stored"))
        loaded = [c.sem(f"loaded{f}") for f in range(FT)]
        added, means, centred, squared, sums, spreads_var, inverted, rooted, spreads, gates, scaled, shifted, done = (
            c.sem(n) for n in ("added", "means", "centred", "squared", "sums", "spreads_var", "inverted", "rooted",
                               "spreads", "gates", "scaled", "shifted", "done"))
        par = lambda name, f: cut(g.par_sb, PCOLS[name] + f, 1)
        pieces = [(lo, min(lo + 512, PTOK)) for lo in range(0, PTOK, 512)]
        c.callback(c.reset)
        with nc.Block() as block:
            @block.sync
            def _(sp):
                c.prime(sp)
                for t, name in ((heads, "heads"), (head_mean, "head_mean"), (ident, "ident")):
                    sp.dma_start(t[:, :], g.small_of(name)).then_inc(consts, 16)
                for f in range(FT):
                    for n, t in enumerate((y0, y1)):
                        sp.dma_start(t[f][:, :], g.ydir[n, f]).then_inc(loaded[f], 16)
                    sp.dma_start(bon[f][:, :], g.bonus[f * P:(f + 1) * P, :]).then_inc(loaded[f], 16)
                    if f == 0:
                        sp.dma_start(hidg[:, 0, :], g.hidg_dram[:, 0, :]).then_inc(gate_in, 16)
                        sp.dma_start(hidg[0:GL - P, 1, :], g.hidg_dram[0:GL - P, 1, :]).then_inc(gate_in, 16)
                        sp.dma_start(w2[:, 0, :], g.gate2[0:P, :]).then_inc(gate_in, 16)
                        sp.dma_start(w2[0:GL - P, 1, :], g.gate2[P:GL, :]).then_inc(gate_in, 16)
                sp.wait_ge(zeroed, PRIMED + 1)
                sp.dma_start(g.mix[:, TOK:TT * P].rearrange("(k p) t -> p k t", p=P), zero[:, :, :]).then_inc(pads, 16)
                for f in range(FT):
                    sp.wait_ge(done, PRIMED + f + 1)
                    for a, ln, p in SEQS:
                        sp.dma_start(g.mix[f * P:(f + 1) * P, a:a + ln], y1[f][:, p:p + ln]).then_inc(stored, 16)
                sp.wait_ge(stored, PRIMED + 32 * FT)
                sp.wait_ge(pads, PRIMED + 16)

            @block.gpsimd
            def _(pool):
                nc.gpsimd.memset(zero[:], 0.0).then_inc(zeroed, 1)

            @block.tensor
            def _(pe):
                def mean(f):
                    pe.wait_ge(added, PRIMED + f + 1)
                    pe.wait_ge(scaled, PRIMED + f - 1)
                    for lo, hi in pieces:
                        last = nc.tensor.matmul(psa[:, lo:hi], heads[:, :], y0[f][:, lo:hi], start=True, stop=True)
                    last.then_inc(means, 1)

                def variance(f):
                    pe.wait_ge(squared, PRIMED + f + 1)
                    pe.wait_ge(spreads_var, PRIMED + f)
                    token_sums(nc, psq, sq, head_mean[:, :]).then_inc(sums, 1)
                pe.wait_ge(consts, PRIMED + 48)
                mean(0)
                variance(0)
                pe.wait_ge(gate_in, PRIMED + 64)
                for f in range(FT):
                    pe.wait_ge(done, PRIMED + f)
                    for lo, hi in pieces:
                        nc.tensor.matmul(psb[:, lo:hi], w2[:, 0, f * P:(f + 1) * P], hidg[:, 0, lo:hi],
                                         start=True, stop=False)
                        last = nc.tensor.matmul(psb[:, lo:hi], w2[0:GL - P, 1, f * P:(f + 1) * P],
                                                hidg[0:GL - P, 1, lo:hi], start=False, stop=True)
                    last.then_inc(gates, 1)
                    if f + 1 < FT:
                        mean(f + 1)
                    pe.wait_ge(rooted, PRIMED + f + 1)
                    pe.wait_ge(centred, PRIMED + min(f + 2, FT))
                    spread(nc, psa, rows, ident, PTOK).then_inc(spreads, 1)
                    if f + 1 < FT:
                        variance(f + 1)

            @block.scalar
            def _(act):
                for f in range(FT):
                    act.wait_ge(centred, PRIMED + f + 1)
                    act.wait_ge(sums, PRIMED + f)
                    nc.scalar.activation(sq[:, :], y1[f][:, :], ACT.Square).then_inc(squared, 1)
                    act.wait_ge(inverted, PRIMED + f + 1)
                    act.wait_ge(spreads, PRIMED + f)
                    nc.scalar.activation(rows[:, :].rearrange("p (a b) -> p a b", b=HD), by_rows(st[:, 1, :], 2),
                                         ACT.Sqrt).then_inc(rooted, 1)

            @block.vector
            def _(dve):
                def centre(f):
                    dve.wait_ge(loaded[f], PRIMED + 48)
                    nc.vector.tensor_tensor(y0[f][:, :], y0[f][:, :], y1[f][:, :], ALU.add).then_inc(added, 1)
                    dve.wait_ge(means, PRIMED + f + 1)
                    nc.vector.scalar_tensor_tensor(out=y1[f][:, :], in0=psa[:, 0:PTOK], scalar=-1.0 / HD,
                                                   in1=y0[f][:, :], op0=ALU.mult, op1=ALU.add).then_inc(centred, 1)

                def inverse(f):
                    dve.wait_ge(sums, PRIMED + f + 1)
                    nc.vector.tensor_scalar(st[:, 0, :], psq[:, 0:2 * TT], 64e-5, None, ALU.add).then_inc(spreads_var, 1)
                    dve.wait_ge(spreads_var, PRIMED + f + 1)
                    dve.wait_ge(rooted, PRIMED + f)
                    nc.vector.reciprocal(st[:, 1, :], st[:, 0, :]).then_inc(inverted, 1)
                centre(0)
                inverse(0)
                for f in range(FT):
                    if f + 1 < FT:
                        centre(f + 1)
                    y = y1[f][:, :]
                    dve.wait_ge(spreads, PRIMED + f + 1)
                    dve.wait_ge(centred, PRIMED + f + 1)
                    nc.vector.scalar_tensor_tensor(out=y, in0=y, scalar=par("lnx_g", f), in1=psa[:, 0:PTOK],
                                                   op0=ALU.mult, op1=ALU.mult).then_inc(scaled, 1)
                    dve.wait_ge(scaled, PRIMED + f + 1)
                    nc.vector.scalar_tensor_tensor(out=y, in0=y, scalar=par("lnx_b", f), in1=bon[f][:, :],
                                                   op0=ALU.add, op1=ALU.add).then_inc(shifted, 1)
                    dve.wait_ge(shifted, PRIMED + f + 1)
                    dve.wait_ge(gates, PRIMED + f + 1)
                    nc.vector.tensor_tensor(y, psb[:, 0:PTOK], y, ALU.mult).then_inc(done, 1)
                    if f + 1 < FT:
                        inverse(f + 1)


def attention_in(nc, g):
    with Ctx(nc, "ai") as c:
        two = lambda name: [c.sb(f"{name}{s}", (P, TOK)) for s in range(2)]
        raw, nrm, rot = two("raw"), two("nrm"), two("rot")
        sq = [c.sb(f"sq{s}", (P, TT * P)) for s in range(2)]
        st = [c.sb(f"st{s}", (P, 2, 2 * TT)) for s in range(2)]
        rows = [c.sb(f"rows{s}", (P, TT * P)) for s in range(2)]
        cos, sin = c.sb("cos", (P, TOK)), c.sb("sin", (P, TOK))
        heads, swap, ident = c.sb("heads", (P, 2)), c.sb("swap", (P, P)), c.sb("ident", (P, P))
        psn, psr, psq = c.ps("psn", (P, 3 * 512)), c.ps("psr", (P, 3 * 512)), c.ps("psq")
        squared, sums, meaned, rooted, inverted, spreads, normed, rotated, roped, placed = (
            c.sem(n) for n in ("squared", "sums", "meaned", "rooted", "inverted", "spreads", "normed",
                               "rotated", "roped", "placed"))
        consts, zeroed, padded, cosed, sined = (c.sem(n) for n in ("consts", "zeroed", "padded", "cosed", "sined"))
        v_turned, v_copied = c.sem("v_turned"), c.sem("v_copied")
        loaded, v_loaded = [[c.sem(f"{n}{s}") for s in range(2)] for n in ("loaded", "v_loaded")]
        TILES = 2 * HEADS
        with nc.Block() as block:
            @block.sync
            def _(sp):
                c.prime(sp)
                for t, name in ((heads, "head_mean"), (swap, "swap"), (ident, "ident")):
                    sp.dma_start(t[:, :], g.small_of(name)).then_inc(consts, 16)
                sp.dma_start(cos[:, :], g.cos).then_inc(consts, 16)
                sp.dma_start(sin[:, :], g.sin).then_inc(consts, 16)
                with sp.Fori(0, TILES // 2) as i:
                    for s in range(2):
                        sp.wait_ge(normed, PRIMED + 2 * i + s - 1 if s else PRIMED + 2 * i - 1)
                        sp.dma_start(raw[s][:, :], g.proj[ds((3 * FT + 2 * i + s) * P, P), :]).then_inc(loaded[s], 16)
                with sp.Fori(0, HEADS // 2) as i:
                    for s in range(2):
                        if s == 0:
                            sp.wait_ge(normed, PRIMED + TILES)
                        sp.wait_ge(v_turned, PRIMED + 2 * i)
                        sp.dma_start(raw[s][:, :], g.proj[ds((5 * FT + 2 * i + s) * P, P), :]).then_inc(v_loaded[s], 16)

            @block.gpsimd
            def _(pool):
                for x in range(2):
                    nc.gpsimd.memset(g.qx[(1 - x) * HD:(2 - x) * HD, :, x, :], 0.0).then_inc(zeroed, 1)

            @block.scalar
            def _(act):
                def square(i, s):
                    t = 2 * i + s
                    act.wait_ge(loaded[s], PRIMED + 16 * i + 16)
                    act.wait_ge(sums, PRIMED + t - 1)
                    nc.scalar.activation(sq[s][:, 0:TOK], raw[s][:, :], ACT.Square).then_inc(squared, 1)

                def root(t, s):
                    act.wait_ge(inverted, PRIMED + t + 1)
                    act.wait_ge(spreads, PRIMED + t - 1)
                    nc.scalar.activation(rows[s][:, :].rearrange("p (a b) -> p a b", b=HD), by_rows(st[s][:, 1, :], 2),
                                         ACT.Sqrt).then_inc(rooted, 1)

                def place(i, s, which):
                    t = 2 * i + s
                    act.wait_ge(roped, PRIMED + t + 1)
                    if which == 0:
                        for x in range(2):
                            rows = slice(x * HD, (x + 1) * HD)
                            last = nc.scalar.copy(g.qx[rows, ds(t, 1), x, :].rearrange("p a t -> p (a t)"),
                                                  rot[s][rows, :])
                        last.then_inc(placed, 1)
                def tile(i, s, which, ahead=2):
                    if ahead:
                        root(2 * i + s + 1, 1 - s)
                    if ahead == 2:
                        square(i + 1, s)
                    place(i, s, which)
                square(0, 0)
                square(0, 1)
                root(0, 0)
                act.wait_ge(zeroed, PRIMED + 2)
                for which, lo, hi in ((0, 0, 2), (1, 2, 3)):
                    with act.Fori(lo, hi) as i:
                        for s in range(2):
                            tile(i, s, which)
                tile(3, 0, 1, ahead=1)
                tile(3, 1, 1, ahead=0)

            @block.tensor
            def _(pe):
                pe.wait_ge(consts, PRIMED + 80)

                def sum_up(t, s):
                    pe.wait_ge(squared, PRIMED + t + 1)
                    pe.wait_ge(meaned, PRIMED + t)
                    token_sums(nc, psq, sq[s], heads[:, :]).then_inc(sums, 1)

                def tile(i, s, ahead=True):
                    t = 2 * i + s
                    pe.wait_ge(rooted, PRIMED + t + 1)
                    pe.wait_ge(normed, PRIMED + t)
                    spread(nc, psn, rows[s], ident, TOK).then_inc(spreads, 1)
                    if ahead:
                        sum_up(t + 1, 1 - s)
                    pe.wait_ge(normed, PRIMED + t + 1)
                    pe.wait_ge(sined, PRIMED + t)
                    for lo in range(0, TOK, 512):
                        hi = min(lo + 512, TOK)
                        last = nc.tensor.matmul(psr[:, lo:hi], swap[:, :], nrm[s][:, lo:hi], start=True, stop=True)
                    last.then_inc(rotated, 1)
                pe.wait_ge(padded, PRIMED + 2)
                sum_up(0, 0)
                with pe.Fori(0, TILES // 2 - 1) as i:
                    for s in range(2):
                        tile(i, s)
                tile(TILES // 2 - 1, 0)
                tile(TILES // 2 - 1, 1, ahead=False)
                pe.wait_ge(sined, PRIMED + TILES)
                pe.wait_ge(normed, PRIMED + TILES)
                with pe.Fori(0, HEADS // 2) as i:
                    for s, ps in enumerate((psn, psr)):
                        pe.wait_ge(v_loaded[s], PRIMED + 16 * i + 16)
                        pe.wait_ge(v_copied, PRIMED + 2 * i + s - 1 if s else PRIMED + 2 * i)
                        for w, (t0, tn) in enumerate(VTILES):
                            last = nc.tensor.transpose(ps[0:tn, w * P:(w + 1) * P],
                                                       raw[s][:, t0:t0 + tn], ident[:, :])
                        last.then_inc(v_turned, 1)

            @block.vector
            def _(dve):
                for s in range(2):
                    nc.vector.memset(sq[s][:, TOK:TT * P], 0.0).then_inc(padded, 1)
                dve.wait_ge(consts, PRIMED + 80)

                def inverse(t, s):
                    dve.wait_ge(sums, PRIMED + t + 1)
                    dve.wait_ge(rooted, PRIMED + t - 1)
                    nc.vector.tensor_scalar(st[s][:, 0, :], psq[:, 0:2 * TT], 1e-6, None, ALU.add).then_inc(meaned, 1)
                    dve.wait_ge(meaned, PRIMED + t + 1)
                    nc.vector.reciprocal(st[s][:, 1, :], st[s][:, 0, :]).then_inc(inverted, 1)

                def tile(i, s, which, ahead=True):
                    t = 2 * i + s
                    dve.wait_ge(spreads, PRIMED + t + 1)
                    nc.vector.scalar_tensor_tensor(out=nrm[s][:, :], in0=raw[s][:, :],
                                                   scalar=cut(g.par_sb, PCOLS[("q_norm_g", "k_norm_g")[which]], 1),
                                                   in1=psn[:, 0:TOK], op0=ALU.mult, op1=ALU.mult).then_inc(normed, 1)
                    if ahead:
                        inverse(t + 1, 1 - s)
                    if which == 0:
                        dve.wait_ge(placed, PRIMED + t - 1)
                    dve.wait_ge(rotated, PRIMED + t + 1)
                    nc.vector.tensor_tensor(rot[s][:, :], psr[:, 0:TOK], sin[:, :], ALU.mult).then_inc(sined, 1)
                    nc.vector.tensor_tensor(nrm[s][:, :], nrm[s][:, :], cos[:, :], ALU.mult).then_inc(cosed, 1)
                    dve.wait_ge(sined, PRIMED + t + 1)
                    dve.wait_ge(cosed, PRIMED + t + 1)
                    out = (rot[s][:, :] if which == 0 else
                           g.kr[:, ds(t - HEADS, 1), :].rearrange("p a t -> p (a t)"))
                    nc.vector.tensor_tensor(out, nrm[s][:, :], rot[s][:, :], ALU.add).then_inc(roped, 1)
                inverse(0, 0)
                for which, lo, hi in ((0, 0, 2), (1, 2, 3)):
                    with dve.Fori(lo, hi) as i:
                        for s in range(2):
                            tile(i, s, which)
                tile(3, 0, 1)
                tile(3, 1, 1, ahead=False)
                with dve.Fori(0, HEADS // 2) as i:
                    for s, ps in enumerate((psn, psr)):
                        h = 2 * i + s
                        dve.wait_ge(v_turned, PRIMED + h + 1)
                        for w0, w1, rows in VRUNS:
                            last = nc.vector.tensor_copy(g.vt[0:rows, ds(h, 1), w0:w1, :].rearrange("p a w t -> p (a w t)"),
                                                         ps[0:rows, w0 * P:w1 * P])
                        last.then_inc(v_copied, 1)


def attention(nc, g):
    units = []
    v0 = 0
    for a, ln, _p in SEQS:
        pieces = -(-ln // P)
        even = -(-ln // pieces)
        units += [(a + t, min(even, ln - t), a, ln, v0) for t in range(0, ln, even)]
        v0 += pieces
    NU = len(units)
    with Ctx(nc, "at") as c:
        ident = c.sb("ident", (P, P))
        pr = [[c.sb(f"pr{s}{x}", (P, LEN_B)) for x in range(2)] for s in range(2)]
        amT = [c.sb(f"amT{s}", (P, 9, P)) for s in range(2)]
        st = [c.sb(f"st{s}", (P, 2, 8)) for s in range(2)]
        lam = c.sb("lam", (P, 4 * HD))
        lams = c.sb("lams", (P, 4))
        pS = [c.ps("pS0", (P, 3, 512)), c.ps("pS1", (P, 3, 512))]
        pT, pO = c.ps("pT"), c.ps("pO")
        consts, chain, lamb = c.sem("consts"), c.sem("chain"), c.sem("lamb")
        two = lambda name: [c.sem(f"{name}0"), c.sem(f"{name}1")]
        scores, row_max, maxed, exped = two("scores"), two("row_max"), two("maxed"), two("exped")
        diffed, outs, ocopied = c.sem("diffed"), c.sem("outs"), c.sem("ocopied")
        turned, tcopied = c.sem("turned"), c.sem("tcopied")
        batches = [-(-(-(-u[3] // P)) // 4) for u in units]
        NB = sum(batches)
        bat0 = [sum(batches[:u]) for u in range(NU)]
        scale = HD ** -0.5
        line = lambda t: t[:, :, :].rearrange("p a b -> p (a b)")

        def weave(eng, h, ahead, batch, finish):
            for u in range(NU + 1):
                if u < NU:
                    ahead(h, u, 0)
                if u:
                    batch(h, u - 1, 0)
                if u < NU:
                    ahead(h, u, 1)
                if u:
                    for b in range(1, batches[u - 1]):
                        batch(h, u - 1, b)
                    finish(h, u - 1)

        with nc.Block() as block:
            @block.sync
            def _(sp):
                c.prime(sp)
                sp.dma_start(ident[:, :], g.small_of("ident")).then_inc(consts, 16)
                sp.dma_start(lam[:, :], g.lambdas.partition_broadcast(P)).then_inc(consts, 16)

            @block.tensor
            def _(pe):
                pe.wait_ge(consts, PRIMED + 32)
                mm = nc.tensor.matmul

                def score(h, u, x):
                    q0, qn, a, ln, v0 = units[u]
                    pe.wait_ge(exped[x], PRIMED + NU * h + u)
                    for lo in range(0, ln, 512):
                        wd = min(512, ln - lo)
                        last = mm(pS[x][0:qn, lo // 512, 0:wd], q_now[:, x, q0:q0 + qn], k_of(h)[:, a + lo:a + lo + wd],
                                  start=True, stop=True)
                    last.then_inc(scores[x], 1)

                def turn(h, u, b):
                    q0, qn, a, ln, v0 = units[u]
                    if b == 0:
                        pe.wait_ge(diffed, PRIMED + NU * h + u + 1)
                    pe.wait_ge(tcopied, PRIMED + NB * h + bat0[u] + b)
                    for w in range(4 * b, min(4 * b + 4, -(-ln // P))):
                        kn = min(P, ln - w * P)
                        last = nc.tensor.transpose(pT[0:kn, (w % 4) * P:(w % 4) * P + qn],
                                                   pr[u % 2][0][0:qn, w * P:w * P + kn], ident[0:qn, 0:qn])
                    last.then_inc(turned, 1)
                    if b:
                        times_v(h, u, b - 1)

                def times_v(h, u, b):
                    q0, qn, a, ln, v0 = units[u]
                    nk = -(-ln // P)
                    if b == 0:
                        pe.wait_ge(ocopied, PRIMED + NU * h + u)
                    pe.wait_ge(tcopied, PRIMED + NB * h + bat0[u] + b + 1)
                    for w in range(4 * b, min(4 * b + 4, nk)):
                        kn = min(P, ln - w * P)
                        last = mm(pO[:, 0:qn], v_now[0:kn, v0 + w, :], amT[u % 2][0:kn, w, 0:qn],
                                  start=(w == 0), stop=(w == nk - 1))
                    if b == batches[u] - 1:
                        last.then_inc(outs, 1)
                k_of = lambda h: g.kr[:, ds(h, 1), :].rearrange("p a t -> p (a t)")
                for h in range(HEADS):
                    q_now, v_now = g.qx[:, h], g.vt[:, h]
                    k_of = lambda h: g.kr[:, h]
                    weave(pe, h, score, turn, lambda h, u: times_v(h, u, batches[u] - 1))

            @block.scalar
            def _(act):
                act.wait_ge(lamb, PRIMED + 1)
                nc.scalar.activation(lams[:, 0:2], lams[:, 0:2], ACT.Exp).then_inc(lamb, 1)

                def exp(h, u, x):
                    q0, qn, a, ln, v0 = units[u]
                    act.wait_ge(maxed[x], PRIMED + NU * h + u + 1)
                    nc.scalar.activation(pr[u % 2][x][0:qn, 0:ln], line(pS[x])[0:qn, 0:ln], ACT.Exp,
                                         bias=st[u % 2][0:qn, x, 1:2], scale=scale,
                                         accum_out=st[u % 2][0:qn, x, 2:3]).then_inc(exped[x], 1)

                def out_of(h, u):
                    q0, qn, a, ln, v0 = units[u]
                    act.wait_ge(outs, PRIMED + NU * h + u + 1)
                    nc.scalar.copy(g.oT[:, ds(h, 1), q0:q0 + qn].rearrange("p a t -> p (a t)"), pO[:, 0:qn]
                                   ).then_inc(ocopied, 1)
                with act.Fori(0, HEADS) as h:
                    weave(act, h, exp, lambda h, u, b: None, out_of)

            @block.vector
            def _(dve):
                LINKS = 3 * NU
                dve.wait_ge(consts, PRIMED + 32)
                pre = Chain(dve, chain)
                for x in range(2):
                    pre(nc.vector.tensor_tensor(lam[:, 2 * x * HD:(2 * x + 1) * HD], lam[:, 2 * x * HD:(2 * x + 1) * HD],
                                                lam[:, (2 * x + 1) * HD:(2 * x + 2) * HD], ALU.mult))
                    pre(nc.vector.reduce_sum(lams[:, x:x + 1], lam[:, 2 * x * HD:(2 * x + 1) * HD], AX_X))
                pre(nc.vector.tensor_copy(lams[:, 3:4], lams[:, 0:1]))
                nc.vector.tensor_copy(lams[:, 2:3], lams[:, 1:2]).then_inc(lamb, 1)
                dve.wait_ge(lamb, PRIMED + 2)
                pre(nc.vector.tensor_tensor(lams[:, 2:3], lams[:, 1:2], lams[:, 0:1], ALU.subtract))
                pre(nc.vector.tensor_scalar(lams[:, 3:4], lams[:, 2:3], -LAMBDA_INIT, None, ALU.add))
                PRE = pre.n

                def largest(h, u, x):
                    q0, qn, a, ln, v0 = units[u]
                    s = st[u % 2]
                    dve.wait_ge(scores[x], PRIMED + NU * h + u + 1)
                    nc.vector.reduce_max(s[0:qn, x, 0:1], line(pS[x])[0:qn, 0:ln], AX_X).then_inc(row_max[x], 1)
                    dve.wait_ge(row_max[x], PRIMED + NU * h + u + 1)
                    nc.vector.tensor_scalar(s[0:qn, x, 1:2], s[0:qn, x, 0:1], -scale, None, ALU.mult
                                            ).then_inc(maxed[x], 1)

                def turn_copy(h, u, b):
                    q0, qn, a, ln, v0 = units[u]
                    dve.wait_ge(turned, PRIMED + NB * h + bat0[u] + b + 1)
                    dve.wait_ge(outs, PRIMED + NU * h + u - 1)
                    w0, w1 = 4 * b, min(4 * b + 4, -(-ln // P))
                    full = min(w1, ln // P)
                    if full > w0:
                        last = nc.vector.tensor_copy(amT[u % 2][:, w0:full, 0:qn],
                                                     pT[:, :].rearrange("p (w t) -> p w t", w=4)[:, 0:full - w0, 0:qn])
                    if full < w1:
                        kn = ln - full * P
                        last = nc.vector.tensor_copy(amT[u % 2][0:kn, full, 0:qn],
                                                     pT[0:kn, (full % 4) * P:(full % 4) * P + qn])
                    last.then_inc(tcopied, 1)

                with dve.Fori(0, HEADS) as h:
                    chained = Chain(dve, chain, h * LINKS + PRE)

                    def difference(u):
                        q0, qn, a, ln, v0 = units[u]
                        s = st[u % 2]
                        for x in range(2):
                            dve.wait_ge(exped[x], PRIMED + NU * h + u + 1)
                        chained(nc.vector.reciprocal(s[0:qn, :, 3:4], s[0:qn, :, 2:3]))
                        chained(nc.vector.tensor_tensor(s[0:qn, 1, 4:5], s[0:qn, 1, 3:4], lams[0:qn, 3:4], ALU.mult))
                        p0, p1 = pr[u % 2][0][0:qn, 0:ln], pr[u % 2][1][0:qn, 0:ln]
                        chained(nc.vector.tensor_scalar(p1, p1, s[0:qn, 1, 4:5], None, ALU.mult))
                        nc.vector.scalar_tensor_tensor(out=p0, in0=p0, scalar=s[0:qn, 0, 3:4], in1=p1,
                                                       op0=ALU.mult, op1=ALU.add).then_inc(diffed, 1)

                    def one(h, u, x):
                        if x == 0 and u:
                            difference(u - 1)
                        largest(h, u, x)

                    def batch(h, u, b):
                        if b == 0 and u == NU - 1:
                            difference(u)
                        turn_copy(h, u, b)
                    weave(dve, h, one, batch, lambda h, u: None)


def attention_out(nc, g):
    with Ctx(nc, "ao") as c:
        sq, rows = [[c.sb(f"{n}{s}", (P, TT * P)) for s in range(2)] for n in ("sq", "rows")]
        st = [c.sb(f"st{s}", (P, 2, TT)) for s in range(2)]
        mean, ident, sg = c.sb("mean", (P, 2)), c.sb("ident", (P, P)), c.sb("sg", (P, 1))
        psn = [c.ps(f"psn{s}", (P, 3 * 512)) for s in range(2)]
        psq = c.ps("psq")
        consts, stored, gained, padded = c.sem("consts"), c.sem("stored"), c.sem("gained"), c.sem("padded")
        squared, sums, meaned, inverted, rooted, spreads, done = (
            c.sem(n) for n in ("squared", "sums", "meaned", "inverted", "rooted", "spreads", "done"))
        c.callback(c.reset)
        with nc.Block() as block:
            @block.sync
            def _(sp):
                c.prime(sp)
                sp.dma_start(mean[:, :], g.small_of("mean")).then_inc(consts, 16)
                sp.dma_start(ident[:, :], g.small_of("ident")).then_inc(consts, 16)
                for h in range(HEADS):
                    sp.wait_ge(done, PRIMED + h + 1)
                    sp.dma_start(g.mix[RW + h * P:RW + (h + 1) * P, 0:TOK], g.oT[:, h]).then_inc(stored, 16)
                sp.wait_ge(stored, PRIMED + 16 * HEADS)

            @block.scalar
            def _(act):
                def square(h):
                    if h >= 2:
                        act.wait_ge(sums, PRIMED + h - 1)
                    nc.scalar.activation(sq[h % 2][:, 0:TOK], g.oT[:, h], ACT.Square).then_inc(squared, 1)
                square(0)
                for h in range(HEADS):
                    if h + 1 < HEADS:
                        square(h + 1)
                    act.wait_ge(inverted, PRIMED + h + 1)
                    if h >= 2:
                        act.wait_ge(spreads, PRIMED + h - 1)
                    nc.scalar.activation(rows[h % 2][:, :].rearrange("p (a b) -> p a b", b=P),
                                         by_rows(st[h % 2][:, 1, :], 1), ACT.Sqrt).then_inc(rooted, 1)

            @block.tensor
            def _(pe):
                def sum_up(h):
                    pe.wait_ge(squared, PRIMED + h + 1)
                    if h:
                        pe.wait_ge(meaned, PRIMED + h)
                    token_sums(nc, psq, sq[h % 2], mean[:, 0:1]).then_inc(sums, 1)
                pe.wait_ge(consts, PRIMED + 32)
                pe.wait_ge(padded, PRIMED + 2)
                sum_up(0)
                for h in range(HEADS):
                    if h + 1 < HEADS:
                        sum_up(h + 1)
                    pe.wait_ge(rooted, PRIMED + h + 1)
                    if h >= 2:
                        pe.wait_ge(done, PRIMED + h - 1)
                    spread(nc, psn[h % 2], rows[h % 2], ident, TOK).then_inc(spreads, 1)

            @block.vector
            def _(dve):
                for s in range(2):
                    nc.vector.memset(sq[s][:, TOK:TT * P], 0.0).then_inc(padded, 1)
                nc.vector.tensor_scalar(sg[:, :], cut(g.par_sb, PCOLS["subln_g"], 1), 1.0 - LAMBDA_INIT, None, ALU.mult
                                        ).then_inc(gained, 1)
                dve.wait_ge(gained, PRIMED + 1)

                def inverse(h):
                    dve.wait_ge(sums, PRIMED + h + 1)
                    if h >= 2:
                        dve.wait_ge(rooted, PRIMED + h - 1)
                    nc.vector.tensor_scalar(st[h % 2][:, 0, :], psq[:, 0:TT], 1e-6, None, ALU.add).then_inc(meaned, 1)
                    dve.wait_ge(meaned, PRIMED + h + 1)
                    nc.vector.reciprocal(st[h % 2][:, 1, :], st[h % 2][:, 0, :]).then_inc(inverted, 1)
                inverse(0)
                for h in range(HEADS):
                    if h + 1 < HEADS:
                        inverse(h + 1)
                    dve.wait_ge(spreads, PRIMED + h + 1)
                    nc.vector.scalar_tensor_tensor(out=g.oT[:, h], in0=g.oT[:, h], scalar=sg[:, 0:1],
                                                   in1=psn[h % 2][:, 0:TOK], op0=ALU.mult, op1=ALU.mult
                                                   ).then_inc(done, 1)


def out_project(nc, g):
    with Ctx(nc, "op") as c:
        w = c.sb("w", (P, KT, D))
        ident = c.sb("ident", (P, P))
        m = [c.sb(f"m{s}", (P, KT, P)) for s in range(2)]
        x = [c.sb(f"x{s}", (P, D)) for s in range(2)]
        xn = c.sb("xn", (P, D))
        st = c.sb("st", (P, 4))
        acc = [c.ps(f"acc{s}", (P, 2, 512)) for s in range(2)]
        tp = c.ps("tp", (P, 2, 512))
        weights, stored, half_loaded = c.sem("weights"), c.sem("stored"), [c.sem(f"half_loaded{b}") for b in range(2)]
        loaded = [c.sem(f"loaded{s}") for s in range(2)]
        products = [c.sem(f"products{s}") for s in range(2)]
        added, squared, rooted, scaled = c.sem("added"), c.sem("squared"), c.sem("rooted"), c.sem("scaled")
        chain = [c.sem(f"chain{s}") for s in range(2)]
        turned, taken = c.sem("turned"), c.sem("taken")
        gain = cut(g.par_sb, PCOLS["ln2_g"], KT)
        PAIRS = TT // 2

        c.callback(c.reset)
        with nc.Block() as block:
            @block.sync
            def _(sp):
                c.prime(sp)
                def weights_half(b):
                    cols = slice(b * 512, (b + 1) * 512)
                    sp.dma_start(w[:, :, cols], g.w_out[:, cols].rearrange("(k p) n -> p k n", p=P)
                                 ).then_inc(half_loaded[b], 16)
                sp.dma_start(ident[:, :], g.small_of("ident")).then_inc(weights, 16)
                weights_half(0)

                def load(i, s, t, stores=None):
                    sp.wait_ge(products[s], PRIMED + i)
                    sp.wait_ge(chain[s], PRIMED + 2 * i)
                    if stores is not None:
                        sp.wait_ge(scaled, PRIMED + stores)
                        sp.wait_ge(stored, PRIMED + 16 * stores)
                    sp.dma_start(m[s][:, :, :], g.mix[:, ds(t * P, P)].rearrange("(k p) t -> p k t", p=P)
                                 ).then_inc(loaded[s], 16)
                    sp.dma_start(x[s][:, :], g.x[ds(t * P, P), :]).then_inc(loaded[s], 16)

                def store(s, t):
                    sp.wait_ge(added, PRIMED + t + 1)
                    sp.dma_start(g.x1[ds(t * P, P), :], x[s][:, :]).then_inc(stored, 16)
                load(0, 0, 0)
                weights_half(1)
                load(0, 1, 1)
                with sp.Fori(0, PAIRS - 1) as i:
                    for s in range(2):
                        store(s, 2 * i + s)
                        load(i + 1, s, 2 * i + 2 + s, stores=2 * i + s + 1)
                store(0, 2 * PAIRS - 2)
                load(PAIRS, 0, 2 * PAIRS, stores=2 * PAIRS - 1)
                store(1, 2 * PAIRS - 1)
                store(0, 2 * PAIRS)
                sp.wait_ge(taken, PRIMED + TT)
                sp.dma_start(g.n2_dram, g.n2T[1][:, :, :]).then_inc(weights, 16)
                sp.wait_ge(weights, PRIMED + 32)

            @block.tensor
            def _(pe):
                pe.wait_ge(weights, PRIMED + 16)
                pe.wait_ge(half_loaded[0], PRIMED + 16)

                def product(i, s, t, first=False):
                    pe.wait_ge(loaded[s], PRIMED + 32 * i + 32)
                    pe.wait_ge(chain[s], PRIMED + 2 * i)
                    for b in range(2):
                        if b and first:
                            pe.wait_ge(half_loaded[1], PRIMED + 16)
                        for k in range(KT):
                            last = nc.tensor.matmul(acc[s][:, b, :], m[s][:, k, :], w[:, k, b * 512:(b + 1) * 512],
                                                    start=(k == 0), stop=(k == KT - 1))
                    last.then_inc(products[s], 1)

                def turn(t):
                    pe.wait_ge(scaled, PRIMED + t + 1)
                    pe.wait_ge(taken, PRIMED + t)
                    for k in range(KT):
                        last = nc.tensor.transpose(tp[:, k // 4, (k % 4) * P:(k % 4 + 1) * P],
                                                   xn[:, k * P:(k + 1) * P], ident[:, :])
                    last.then_inc(turned, 1)
                product(0, 0, 0, first=True)
                with pe.Fori(0, PAIRS) as i:
                    product(i, 1, 2 * i + 1)
                    turn(2 * i)
                    product(i + 1, 0, 2 * i + 2)
                    turn(2 * i + 1)
                turn(2 * PAIRS)

            @block.scalar
            def _(act):
                def tile(i, s, t):
                    act.wait_ge(added, PRIMED + t + 1)
                    act.wait_ge(turned, PRIMED + t)
                    nc.scalar.activation(xn[:, :], x[s][:, :], ACT.Square, accum_out=st[:, 0:1]).then_inc(squared, 1)
                    act.wait_ge(chain[s], PRIMED + 2 * i + 1)
                    nc.scalar.activation(st[:, 2:3], st[:, 1:2], ACT.Sqrt).then_inc(rooted, 1)
                with act.Fori(0, PAIRS) as i:
                    tile(i, 0, 2 * i)
                    tile(i, 1, 2 * i + 1)
                tile(PAIRS, 0, 2 * PAIRS)

            @block.vector
            def _(dve):
                def tile(i, s, t, half):
                    chained = Chain(dve, chain[s], 2 * i)
                    dve.wait_ge(products[s], PRIMED + i + 1)
                    nc.vector.tensor_tensor(x[s][:, :].rearrange("p (b n) -> p b n", b=2), acc[s][:, :, :],
                                            x[s][:, :].rearrange("p (b n) -> p b n", b=2), ALU.add
                                            ).then_inc(added, 1)
                    dve.wait_ge(squared, PRIMED + t + 1)
                    nc.vector.tensor_scalar(st[:, 1:2], st[:, 0:1], 1.0 / D, 1e-6, ALU.mult, ALU.add
                                            ).then_inc(chain[s], 1)
                    chained.n += 1
                    dve.wait_ge(rooted, PRIMED + t + 1)
                    chained(nc.vector.reciprocal(st[:, 3:4], st[:, 2:3]))
                    nc.vector.tensor_scalar(xn[:, :], x[s][:, :], st[:, 3:4], None, ALU.mult).then_inc(scaled, 1)
                    dve.wait_ge(turned, PRIMED + t + 1)
                    nc.vector.tensor_tensor(g.n2T[half][:, :, ds((t - half * SPLIT) * P, P)].rearrange("p (b k) t -> p b k t", b=2),
                                            tp[:, :, :].rearrange("p b (k t) -> p b k t", k=4),
                                            gain.rearrange("p (b k) -> p b k", b=2).unsqueeze(3).to_broadcast([P, 2, 4, P]),
                                            ALU.mult).then_inc(taken, 1)
                with dve.Fori(0, SPLIT // 2) as i:
                    tile(i, 0, 2 * i, 0)
                    tile(i, 1, 2 * i + 1, 0)
                tile(SPLIT // 2, 0, SPLIT - 1, 0)
                tile(SPLIT // 2, 1, SPLIT, 1)
                with dve.Fori(SPLIT // 2 + 1, PAIRS) as i:
                    tile(i, 0, 2 * i, 1)
                    tile(i, 1, 2 * i + 1, 1)
                tile(PAIRS, 0, 2 * PAIRS, 1)


def ffn_up(nc, g, half):
    wd = HALF_COLS[half]
    cw = wd // 2
    with Ctx(nc, f"fu{half}") as c:
        raw = [c.sb(f"raw{y}", (P, KT, P)) for y in range(2)]
        w = [[c.sb(f"w{y}{part}", (P, KT, P), F32R) for part in ("high", "rest")] for y in range(2)]
        gate = c.sb("gate", (P, wd))
        acc = [[[c.ps(f"acc{s}{y}{n}") for n in range(2)] for y in range(2)] for s in range(2)]
        both = lambda name: [c.sem(f"{name}{y}") for y in range(2)]
        loaded, cut_high, cut_rest = both("loaded"), both("cut_high"), both("cut_rest")
        products = both("products")
        n_loaded = [c.sem(f"n_loaded{b}") for b in range(KT // 2)]
        n_high, n_rest = c.sem("n_high"), c.sem("n_rest")
        silued, multiplied, h_high, h_rest = c.sem("silued"), c.sem("multiplied"), c.sem("h_high"), c.sem("h_rest")
        line = lambda t: t[:, :, :].rearrange("p k n -> p (k n)")
        row = lambda t, m: t[:, ds(m, 1), 0:wd].rearrange("p a t -> p (a t)")
        c.callback(c.reset)
        with nc.Block() as block:
            @block.sync
            def _(sp):
                c.prime(sp)

                def weights(m):
                    for y, src in enumerate((g.w_gate, g.w_up)):
                        sp.wait_ge(cut_rest[y], PRIMED + m)
                        sp.dma_start(raw[y][:, :, :], src[ds(m, 1)].rearrange("a p k n -> (a p) k n")
                                     ).then_inc(loaded[y], 16)
                weights(0)
                if half:
                    for b in range(KT // 2):
                        sp.dma_start(g.n2T[half][:, 2 * b:2 * b + 2, :], g.n2_dram[:, 2 * b:2 * b + 2, 0:wd]
                                     ).then_inc(n_loaded[b], 16)
                with sp.Fori(1, FFT) as m:
                    weights(m)

            @block.tensor
            def _(pe):
                pe.wait_ge(n_rest, PRIMED + KT)
                with pe.Fori(0, FFT // 2) as i:
                    for s in range(2):
                        m = 2 * i + s
                        for y in range(2):
                            pe.wait_ge(cut_rest[y], PRIMED + m + 1)
                            pe.wait_ge(multiplied, PRIMED + m - 1)
                            for n in range(2):
                                cols = slice(n * cw, (n + 1) * cw)
                                for k in range(KT):
                                    last = three_pass(nc, acc[s][y][n][:, 0:cw], (w[y][0][:, k, :], w[y][1][:, k, :]),
                                                      (g.nh[:, k, cols], g.nl[:, k, cols]), k == 0, k == KT - 1)
                                last.then_inc(products[y], 1)

            @block.scalar
            def _(act):
                def cut_weights(m, y):
                    act.wait_ge(loaded[y], PRIMED + 16 * m + 16)
                    act.wait_ge(products[y], PRIMED + 2 * m)
                    nc.scalar.copy(line(w[y][0]), line(raw[y])).then_inc(cut_high[y], 1)

                def tile(m, s, ahead=True):
                    act.wait_ge(h_rest, PRIMED + m)
                    for n in range(2):
                        act.wait_ge(products[0], PRIMED + 2 * m + n + 1)
                        last = nc.scalar.activation(gate[:, n * cw:(n + 1) * cw], acc[s][0][n][:, 0:cw], ACT.Silu)
                    last.then_inc(silued, 1)
                    if ahead:
                        cut_weights(m + 1, 0)
                    act.wait_ge(multiplied, PRIMED + m + 1)
                    nc.scalar.copy(row(g.hh, m), gate[:, :]).then_inc(h_high, 1)
                    if ahead:
                        cut_weights(m + 1, 1)
                cut_weights(0, 0)
                cut_weights(0, 1)
                for k in range(KT):
                    if half and k % 2 == 0:
                        act.wait_ge(n_loaded[k // 2], PRIMED + 16)
                    nc.scalar.copy(g.nh[:, k, 0:wd], g.n2T[half][:, k, 0:wd]).then_inc(n_high, 1)
                with act.Fori(0, FFT // 2 - 1) as i:
                    for s in range(2):
                        tile(2 * i + s, s)
                tile(FFT - 2, 0)
                tile(FFT - 1, 1, ahead=False)

            @block.vector
            def _(dve):
                def rest_of_weights(m, y):
                    dve.wait_ge(cut_high[y], PRIMED + m + 1)
                    nc.vector.tensor_tensor(line(w[y][1]), line(raw[y]), line(w[y][0]).bitcast(F32), ALU.subtract
                                            ).then_inc(cut_rest[y], 1)

                def tile(m, s, ahead=True):
                    if ahead:
                        rest_of_weights(m + 1, 0)
                    dve.wait_ge(silued, PRIMED + m + 1)
                    for n in range(2):
                        dve.wait_ge(products[1], PRIMED + 2 * m + n + 1)
                        last = nc.vector.tensor_tensor(gate[:, n * cw:(n + 1) * cw], acc[s][1][n][:, 0:cw],
                                                       gate[:, n * cw:(n + 1) * cw], ALU.mult)
                    last.then_inc(multiplied, 1)
                    dve.wait_ge(h_high, PRIMED + m + 1)
                    nc.vector.tensor_tensor(row(g.hl, m), gate[:, :], row(g.hh, m).bitcast(F32), ALU.subtract
                                            ).then_inc(h_rest, 1)
                    if ahead:
                        rest_of_weights(m + 1, 1)
                rest_of_weights(0, 0)
                rest_of_weights(0, 1)
                for k in range(KT):
                    dve.wait_ge(n_high, PRIMED + k + 1)
                    nc.vector.tensor_tensor(g.nl[:, k, 0:wd], g.n2T[half][:, k, 0:wd], g.nh[:, k, 0:wd].bitcast(F32),
                                            ALU.subtract).then_inc(n_rest, 1)
                with dve.Fori(0, FFT // 2 - 1) as i:
                    for s in range(2):
                        tile(2 * i + s, s)
                tile(FFT - 2, 0)
                tile(FFT - 1, 1, ahead=False)


def ffn_down(nc, g, half):
    wd = HALF_COLS[half]
    cw = wd // 2
    tiles = -(-wd // P)
    PIECES = ([(META, P - META, 0, 1, 0, 0), (0, P, 1, 1, 0, P - META), (0, META, 2, 1, 0, 2 * P - META),
               (32, P - 32, 2, 1, 1, 0), (0, P, 3, 2, 1, 96)],
              [(0, P, 0, 5, 1, 96 + 2 * P), (0, 32, 5, 1, 1, 992)])[half]
    with Ctx(nc, f"fd{half}") as c:
        raw = [c.sb(f"raw{s}", (P, FFT, P)) for s in range(2)]
        w = [[c.sb(f"w{s}{part}", (P, FFT, P), F32R) for part in ("high", "rest")] for s in range(2)]
        x1, out = c.sb("x1", (P, tiles, P)), c.sb("out", (P, tiles, P))
        yT = c.sb("yT", (P, tiles * P))
        ident = c.sb("ident", (P, P))
        acc = [[c.ps(f"acc{s}{n}") for n in range(2)] for s in range(2)]
        tp = c.ps("tp", (P, 2 * 512))
        by_slot = lambda name: [c.sem(f"{name}{s}") for s in range(2)]
        loaded, cut_high, cut_rest, products = (by_slot(n) for n in ("loaded", "cut_high", "cut_rest", "products"))
        consts, rows, copied = c.sem("consts"), c.sem("rows"), c.sem("copied")
        turned, added, stored, zeroed = c.sem("turned"), c.sem("added"), c.sem("stored"), c.sem("zeroed")
        STEPS = KT // 2
        line = lambda t: t[:, :, :].rearrange("p k n -> p (k n)")
        c.callback(c.reset)
        with nc.Block() as block:
            @block.sync
            def _(sp):
                c.prime(sp)
                sp.dma_start(ident[:, :], g.small_of("ident")).then_inc(consts, 16)

                def weights(i, s):
                    sp.wait_ge(cut_rest[s], PRIMED + i)
                    sp.dma_start(raw[s][:, :, :], g.w_down[ds(2 * i + s, 1)].rearrange("a p k n -> (a p) k n")
                                 ).then_inc(loaded[s], 16)

                def residual(m):
                    sp.wait_ge(added, PRIMED + m)
                    rows0 = half * SPLIT * P
                    sp.dma_start(x1[:, :, :], g.x1[rows0:rows0 + tiles * P, ds(m * P, P)
                                                   ].rearrange("(t p) n -> p t n", p=P)).then_inc(rows, 16)

                def store(m):
                    sp.wait_ge(added, PRIMED + m + 1)
                    for p0, pn, t0, tn, o, r0 in PIECES:
                        dst = g.out[o][0, r0:r0 + pn * tn, ds(m * P, P)]
                        sp.dma_start(dst.rearrange("(t p) n -> p t n", t=tn), out[p0:p0 + pn, t0:t0 + tn, :]
                                     ).then_inc(stored, 16)
                weights(0, 0)
                weights(0, 1)
                residual(0)
                with sp.Fori(0, STEPS - 1) as i:
                    for s in range(2):
                        weights(i + 1, s)
                        residual(2 * i + s + 1)
                        store(2 * i + s)
                residual(KT - 1)
                store(KT - 2)
                store(KT - 1)
                sp.wait_ge(stored, PRIMED + 16 * len(PIECES) * KT)

            @block.tensor
            def _(pe):
                pe.wait_ge(consts, PRIMED + 16)
                pe.wait_ge(zeroed, PRIMED + 1)

                def product(i, s):
                    pe.wait_ge(cut_rest[s], PRIMED + i + 1)
                    pe.wait_ge(copied, PRIMED + 4 * i + 2 * s - 2)
                    for n in range(2):
                        cols = slice(n * cw, (n + 1) * cw)
                        for k in range(FFT):
                            last = three_pass(nc, acc[s][n][:, 0:cw], (w[s][0][:, k, :], w[s][1][:, k, :]),
                                              (g.hh[:, k, cols], g.hl[:, k, cols]), k == 0, k == FFT - 1)
                        last.then_inc(products[s], 1)

                def turn(m):
                    pe.wait_ge(copied, PRIMED + 2 * m + 2)
                    pe.wait_ge(added, PRIMED + m)
                    for t in range(tiles):
                        last = nc.tensor.transpose(tp[:, t * P:(t + 1) * P], yT[:, t * P:(t + 1) * P], ident[:, :])
                    last.then_inc(turned, 1)
                product(0, 0)
                with pe.Fori(0, STEPS - 1) as i:
                    product(i, 1)
                    turn(2 * i)
                    product(i + 1, 0)
                    turn(2 * i + 1)
                product(STEPS - 1, 1)
                turn(KT - 2)
                turn(KT - 1)

            @block.scalar
            def _(act):
                def cut_weights(i, s):
                    act.wait_ge(loaded[s], PRIMED + 16 * i + 16)
                    act.wait_ge(products[s], PRIMED + 2 * i)
                    nc.scalar.copy(line(w[s][0]), line(raw[s])).then_inc(cut_high[s], 1)

                def copy_out(i, s):
                    act.wait_ge(turned, PRIMED + 2 * i + s)
                    for n in range(2):
                        act.wait_ge(products[s], PRIMED + 2 * i + n + 1)
                        nc.scalar.copy(yT[:, n * cw:(n + 1) * cw], acc[s][n][:, 0:cw]).then_inc(copied, 1)
                cut_weights(0, 0)
                cut_weights(0, 1)
                with act.Fori(0, STEPS - 1) as i:
                    for s in range(2):
                        copy_out(i, s)
                        cut_weights(i + 1, s)
                copy_out(STEPS - 1, 0)
                copy_out(STEPS - 1, 1)

            @block.vector
            def _(dve):
                def rest_of_weights(i, s):
                    dve.wait_ge(cut_high[s], PRIMED + i + 1)
                    nc.vector.tensor_tensor(line(w[s][1]), line(raw[s]), line(w[s][0]).bitcast(F32), ALU.subtract
                                            ).then_inc(cut_rest[s], 1)

                def add(m):
                    dve.wait_ge(turned, PRIMED + m + 1)
                    dve.wait_ge(rows, PRIMED + 16 * m + 16)
                    dve.wait_ge(stored, PRIMED + 16 * len(PIECES) * m)
                    nc.vector.tensor_tensor(out[:, :, :].rearrange("p t n -> p (t n)"), tp[:, 0:tiles * P],
                                            x1[:, :, :].rearrange("p t n -> p (t n)"), ALU.add).then_inc(added, 1)
                nc.vector.memset(yT[:, :], 0.0).then_inc(zeroed, 1)
                rest_of_weights(0, 0)
                rest_of_weights(0, 1)
                with dve.Fori(0, STEPS - 1) as i:
                    for s in range(2):
                        rest_of_weights(i + 1, s)
                        add(2 * i + s)
                add(KT - 2)
                add(KT - 1)


class Tensors:

    def __init__(self, dram, out):
        self.out = out
        self.x = dram["x"]
        self.par = dram["par"]
        self.w_in = dram["w_in"]
        self.lora1 = dram["lora1"]
        self.lora2 = dram["lora2"]
        self.gate2 = dram["gate2"]
        self.lambdas = dram["lambdas"]
        self.w_out = dram["w_out"]
        self.w_gate = dram["w_gate"]
        self.w_up = dram["w_up"]
        self.w_down = dram["w_down"]
        self.small = dram["small"]
        self.cos = dram["cos"]
        self.sin = dram["sin"]
        self.first = dram["first"]
        self.keep = dram["keep"]

    def small_of(self, name):
        lo, wd = SCOLS[name]
        return self.small[:, lo:lo + wd]


def encoder(nc, g):
    scratch = lambda name, shape: nc.dram_tensor(f"dram_{name}", list(shape), F32, kind=SCRATCH_KIND).ap()
    g.proj = scratch("proj", (3072, TOK))
    g.sx = scratch("sx", (2, FT, P, CHUNKS * 5 * CH))
    g.bonus = scratch("bonus", (RW, PTOK))
    g.ydir = scratch("ydir", (2, FT, P, PTOK))
    g.hidg_dram = scratch("hidg", (P, 2, PTOK))
    g.mix = scratch("mix", (D, TT * P))
    g.x1 = scratch("x1", (TT * P, D))
    g.n2_dram = scratch("n2", (P, KT, (TT - SPLIT) * P))

    with Ctx(nc, "all") as whole:
        g.par_sb = whole.sb("par", (P, NPAR))
        with Ctx(nc, "mixer") as mixer:
            g.etot = mixer.sb("etot", (P, 2, FT, CHUNKS))
            with Ctx(nc, "lora") as lora:
                g.hid = lora.sb("hid", (HD, 4, PTOK))
                with Ctx(nc, "n") as norm:
                    g.nT = norm.sb("nT", (P, KT, TT * P))
                    with Ctx(nc, "parts") as parts:
                        g.nh, g.nl = (parts.sb(n, (P, KT, TT * P), F32R) for n in ("nh", "nl"))
                        norm_in(nc, g)
                        project(nc, g)
                    lora_in(nc, g)
                prep(nc, g)
            chunks(nc, g)
            mix_out(nc, g)
        with Ctx(nc, "heads") as kept:
            g.qx, g.kr = kept.sb("qx", (P, HEADS, 2, TOK)), kept.sb("kr", (P, HEADS, TOK))
            g.vt, g.oT = kept.sb("vt", (P, HEADS, len(VTILES), P)), kept.sb("oT", (P, HEADS, TOK))
            attention_in(nc, g)
            attention(nc, g)
            attention_out(nc, g)
        for half in range(2):
            with Ctx(nc, f"h{half}") as hidden:
                g.hh, g.hl = (hidden.sb(n, (P, FFT, HALF_COLS[half]), F32R) for n in ("hh", "hl"))
                with Ctx(nc, f"n{half}") as normed:
                    n2 = normed.sb("n2T", (P, KT, HALF_COLS[half]))
                    if half == 0:
                        with Ctx(nc, "later") as later:
                            g.n2T = [n2, later.sb("n2T", (P, KT, (TT - SPLIT) * P))]
                            out_project(nc, g)
                    g.n2T = [n2, n2]
                    g.nh, g.nl = (normed.sb(n, (P, KT, HALF_COLS[half]), F32R) for n in ("nh", "nl"))
                    ffn_up(nc, g, half)
                ffn_down(nc, g, half)


def laid_out(inputs):
    a = {n: np.asarray(v) for n, v in inputs.items()}
    cat = np.concatenate
    meta = a["meta_tokens"]
    x = cat([meta, a["x_prompt"][0], meta, a["x_sample"][0], np.zeros((TT * P - TOK, D), np.float32)])
    column = lambda v: v.reshape(-1, P).T
    rows = [column(a["ln1_g"][0]), column(a["ln2_g"][0])]
    rows += [column(a["conv_rkv"][0, n]) for n in range(3)]
    for name in ("mix_w", "mix_a"):
        rows += [column(a[name][0, d]) for d in range(2)]
    rows.append(column(a["mix_g"][0]))
    for name in ("decay_w0", "aaa_a0"):
        rows += [column(a[name][0, d]) for d in range(2)]
    rows += [column(a[name][0].reshape(-1)) for name in ("k_k", "k_a", "r_k", "lnx_g", "lnx_b")]
    rows += [cat([a[name][0]] * 2)[:, None] for name in ("q_norm_g", "k_norm_g")]
    rows.append(a["subln_g"][0][:, None])
    tiles = lambda w: np.ascontiguousarray(w.reshape(w.shape[0] // P, P, w.shape[1] // P, P).transpose(2, 1, 0, 3))
    by_row = lambda w: w.reshape(KT, P, w.shape[1]).transpose(1, 0, 2)
    lora1 = cat([by_row(a["decay_w1"][0, 0]), by_row(a["aaa_a1"][0, 0]), by_row(a["decay_w1"][0, 1]),
                 by_row(a["aaa_a1"][0, 1]), by_row(a["gate_g1"][0])], axis=2)
    second = np.stack([a["decay_w2"][0, 0], a["aaa_a2"][0, 0], a["decay_w2"][0, 1], a["aaa_a2"][0, 1]])
    lora2 = second.reshape(4, HD, FT, P).transpose(2, 1, 0, 3)
    arrays = {
        "x": x, "par": cat(rows, axis=1), "w_in": tiles(a["w_in"][0]), "lora1": lora1, "lora2": lora2,
        "gate2": a["gate_g2"][0], "lambdas": a["diff_lambdas"][0].reshape(-1), "w_out": a["w_out"][0],
        "w_gate": tiles(a["w_gate"][0]), "w_up": tiles(a["w_up"][0]), "w_down": tiles(a["w_down"][0]),
        "small": SMALL_ARRAY, **WIDE,
    }
    return {n: np.ascontiguousarray(v) for n, v in arrays.items()}


def kernel(**inputs):
    import concourse.bacc as _bacc
    from concourse.bass_utils import run_bass_kernel_spmd as _run

    nc = _bacc.Bacc("TRN2", target_bir_lowering=False, num_devices=1)
    arrays = laid_out(inputs)
    dram = {n: nc.dram_tensor(f"in_{n}", a.shape, F32, kind="ExternalInput").ap() for n, a in arrays.items()}
    out = [nc.dram_tensor(f"out_{n}", (1, rows, D), F32, kind="ExternalOutput").ap()
           for n, rows in enumerate((LEN_A - META, LEN_B - META))]
    encoder(nc, Tensors(dram, out))
    r = _run(nc, [{f"in_{n}": a for n, a in arrays.items()}], core_ids=[0])
    return tuple(r.results[0][f"out_{n}"] for n in range(2))
```
